# Optimizing a Trainium2 kernel written in Bass

```python
import math
import jax, jax.numpy as jnp
from jax import lax
import numpy as np

D_MODEL = 1024
BATCH = 1
SEQ = 256
DEPTH = 2

N_A_LAYERS = DEPTH // 2
N_B_LAYERS = DEPTH - N_A_LAYERS
A_HEADS = 8
A_DK = 128
A_DV = 128
A_QK = A_HEADS * A_DK
A_V = A_HEADS * A_DV
A_CONV = 4
A_CONV_CH = 2 * A_QK + A_V
A_IN = 2 * A_QK + 2 * A_V + 2 * A_HEADS
A_CHUNK = 64
B_HEADS = 8
B_DH = 64
B_QK = B_HEADS * 2 * B_DH
B_V = B_HEADS * 2 * B_DH
B_QBLOCK = 128
REL_BUCKETS = 32
REL_MAX_DIST = 128
N_EXPERTS = 16
N_GROUPS = 4
EXPERTS_PER_GROUP = N_EXPERTS // N_GROUPS
TOP_K = 2
D_EXPERT = 512
DN_ALPHA = (2 * DEPTH) ** 0.25
DN_BETA = (8 * DEPTH) ** -0.25
LN_EPS = 1e-5
RMS_EPS = 1e-6

kernel_name = 'hybrid_gdn_diffattn_yoco_moe'

F32 = jnp.float32

def layer_norm(x, w, b):
    xf = x.astype(F32)
    mu = xf.mean(-1, keepdims=True)
    var = jnp.square(xf - mu).mean(-1, keepdims=True)
    return ((xf - mu) * lax.rsqrt(var + LN_EPS) * w.astype(F32) + b.astype(F32)).astype(x.dtype)

def rms_norm_f32(x, w):
    xf = x.astype(F32)
    return xf * lax.rsqrt(jnp.mean(xf * xf, -1, keepdims=True) + RMS_EPS) * w.astype(F32)

def l2norm(x):
    return x * lax.rsqrt(jnp.sum(x * x, -1, keepdims=True) + RMS_EPS)

def causal_depthwise_conv(x, w):
    c = x.shape[-1]
    return lax.conv_general_dilated(x, w[:, None, :], window_strides=(1,),
                                    padding=[(w.shape[0] - 1, 0)],
                                    dimension_numbers=('NWC', 'WIO', 'NWC'),
                                    feature_group_count=c)

def chunked_gated_delta_rule(q, k, v, g, beta):
    bsz, t_len, h, dk = q.shape
    dv = v.shape[-1]
    nc = t_len // A_CHUNK

    def chunks(t):
        t = t.reshape((bsz, nc, A_CHUNK, h) + t.shape[3:])
        return jnp.moveaxis(t, 3, 1)

    q, k, v, g, beta = map(chunks, (q, k, v, g, beta))
    g = jnp.cumsum(g, axis=-1)
    idx = jnp.arange(A_CHUNK)
    incl = idx[:, None] >= idx[None, :]
    strict = idx[:, None] > idx[None, :]
    decay = jnp.exp(jnp.where(incl, g[..., :, None] - g[..., None, :], -jnp.inf))
    kk = jnp.einsum('bhncd,bhnsd->bhncs', k, k)
    m = jnp.where(strict, beta[..., :, None] * kk * decay, 0.0)
    a_mat = m + jnp.eye(A_CHUNK, dtype=F32)
    u = lax.linalg.triangular_solve(a_mat, beta[..., None] * v, left_side=True,
                                    lower=True, unit_diagonal=True)
    w = lax.linalg.triangular_solve(a_mat, (beta * jnp.exp(g))[..., None] * k, left_side=True,
                                    lower=True, unit_diagonal=True)
    qk = jnp.einsum('bhncd,bhnsd->bhncs', q, k) * decay
    g_last = g[..., -1:]
    q_dec = q * jnp.exp(g)[..., None]
    k_dec = k * jnp.exp(g_last - g)[..., None]
    chunk_decay = jnp.exp(g_last)[..., None]
    xs = tuple(jnp.moveaxis(t, 2, 0) for t in (q_dec, k_dec, u, w, qk, chunk_decay))

    def step(s, inp):
        q_c, k_c, u_c, w_c, qk_c, dec_c = inp
        v_new = u_c - jnp.einsum('bhcd,bhde->bhce', w_c, s)
        o_c = jnp.einsum('bhcd,bhde->bhce', q_c, s) + jnp.einsum('bhcs,bhse->bhce', qk_c, v_new)
        s = s * dec_c + jnp.einsum('bhcd,bhce->bhde', k_c, v_new)
        return s, o_c

    s0 = jnp.zeros((bsz, h, dk, dv), F32)
    _, o = lax.scan(step, s0, xs)
    return o.transpose(1, 0, 3, 2, 4).reshape(bsz, t_len, h, dv)

def gated_deltanet_mixer(x, w_in, conv_w, a_log, dt_bias, norm_w, w_out):
    bsz, t_len, _ = x.shape
    proj = x @ w_in
    qkv, z, a, b = jnp.split(proj, [A_CONV_CH, A_CONV_CH + A_V, A_CONV_CH + A_V + A_HEADS], axis=-1)
    qkv = jax.nn.silu(causal_depthwise_conv(qkv, conv_w))
    q, k, v = jnp.split(qkv, [A_QK, 2 * A_QK], axis=-1)
    q = l2norm(q.reshape(bsz, t_len, A_HEADS, A_DK).astype(F32)) * (A_DK ** -0.5)
    k = l2norm(k.reshape(bsz, t_len, A_HEADS, A_DK).astype(F32))
    v = v.reshape(bsz, t_len, A_HEADS, A_DV).astype(F32)
    beta = jax.nn.sigmoid(b.astype(F32))
    g = -jnp.exp(a_log.astype(F32)) * jax.nn.softplus(a.astype(F32) + dt_bias.astype(F32))
    o = chunked_gated_delta_rule(q, k, v, g, beta)
    o = rms_norm_f32(o, norm_w) * jax.nn.silu(z.reshape(bsz, t_len, A_HEADS, A_DV).astype(F32))
    return o.reshape(bsz, t_len, A_V).astype(x.dtype) @ w_out

def t5_bucket(n):
    max_exact = REL_BUCKETS // 2
    nf = jnp.maximum(n, 1).astype(F32)
    large = max_exact + (jnp.log(nf / max_exact) / math.log(REL_MAX_DIST / max_exact)
                         * (REL_BUCKETS - max_exact)).astype(jnp.int32)
    large = jnp.minimum(large, REL_BUCKETS - 1)
    return jnp.where(n < max_exact, n, large)

def shared_kv(x, w_kv):
    bsz, t_len, _ = x.shape
    kv = x @ w_kv
    k = kv[..., :B_QK].reshape(bsz, t_len, B_HEADS, 2, B_DH).transpose(0, 2, 3, 1, 4)
    v = kv[..., B_QK:].reshape(bsz, t_len, B_HEADS, 2 * B_DH).transpose(0, 2, 1, 3)
    return k, v

def diff_attention_mixer(x, k_sh, v_sh, dist_bias, w_q, lam, subln_w, w_out, lambda_init):
    bsz, t_len, _ = x.shape
    nb = t_len // B_QBLOCK
    q = (x @ w_q).reshape(bsz, nb, B_QBLOCK, B_HEADS, 2, B_DH).transpose(1, 0, 3, 4, 2, 5)
    lam_f = lam.astype(F32)
    lam_val = (jnp.exp(jnp.sum(lam_f[0] * lam_f[1])) - jnp.exp(jnp.sum(lam_f[2] * lam_f[3]))
               + lambda_init)
    k_pos = jnp.arange(t_len)
    scale = B_DH ** -0.5

    def one_block(args):
        q_blk, blk = args
        q_pos = blk * B_QBLOCK + jnp.arange(B_QBLOCK)
        rel = q_pos[:, None] - k_pos[None, :]
        bias = dist_bias[:, jnp.clip(rel, 0, t_len - 1)]
        s = jnp.einsum('bhiqd,bhikd->bhiqk', q_blk, k_sh).astype(F32) * scale + bias[None, :, None]
        s = jnp.where(rel >= 0, s, -jnp.inf)
        p = jax.nn.softmax(s, axis=-1)
        attn = p[:, :, 0] - lam_val * p[:, :, 1]
        return jnp.einsum('bhqk,bhkd->bhqd', attn.astype(v_sh.dtype), v_sh)

    o = lax.map(one_block, (q, jnp.arange(nb)))
    o = o.transpose(1, 0, 3, 2, 4).reshape(bsz, t_len, B_HEADS, 2 * B_DH)
    o = rms_norm_f32(o, subln_w) * (1.0 - lambda_init)
    return o.reshape(bsz, t_len, B_V).astype(x.dtype) @ w_out

def grouped_moe(x, router_w, router_b, w_gate, w_up, w_down):
    bsz, t_len, _ = x.shape
    probs = jax.nn.softmax((x @ router_w).astype(F32) + router_b.astype(F32), axis=-1)
    pg = probs.reshape(bsz, t_len, N_GROUPS, EXPERTS_PER_GROUP)
    top_in_group, _ = lax.top_k(pg, TOP_K)
    best_group = jnp.argmax(top_in_group.sum(-1), axis=-1)
    group_probs = jnp.einsum('btge,btg->bte', pg, jax.nn.one_hot(best_group, N_GROUPS, dtype=F32))
    top_w, top_i = lax.top_k(group_probs, TOP_K)
    top_w = top_w / top_w.sum(-1, keepdims=True)
    expert_idx = best_group[..., None] * EXPERTS_PER_GROUP + top_i
    gate = jnp.sum(jax.nn.one_hot(expert_idx, N_EXPERTS, dtype=F32) * top_w[..., None], axis=-2)
    gate = gate.astype(x.dtype)
    y = jnp.zeros_like(x)
    for e in range(N_EXPERTS):
        h = jax.nn.silu(x @ w_gate[e]) * (x @ w_up[e])
        y = y + gate[..., e:e + 1] * (h @ w_down[e])
    return y

def lambda_init_for(layer):
    return 0.8 - 0.6 * math.exp(-0.3 * layer)

def setup_inputs(seed: int = 0) -> dict:
    key = jax.random.key(seed)
    ks = jax.random.split(key, 20)

    def nrm(k, shape, scale):
        return jax.random.normal(k, shape, F32) * scale

    x = nrm(ks[0], (BATCH, SEQ, D_MODEL), 1.0)
    a_w_in = nrm(ks[1], (N_A_LAYERS, D_MODEL, A_IN), D_MODEL ** -0.5)
    a_conv = nrm(ks[2], (N_A_LAYERS, A_CONV, A_CONV_CH), A_CONV ** -0.5)
    a_A_log = jnp.log(jax.random.uniform(ks[3], (N_A_LAYERS, A_HEADS), F32, 1.0, 16.0))
    dt = jnp.exp(jax.random.uniform(ks[4], (N_A_LAYERS, A_HEADS), F32, math.log(1e-3), math.log(1e-1)))
    a_dt_bias = dt + jnp.log(-jnp.expm1(-dt))
    a_norm_w = 1.0 + nrm(ks[5], (N_A_LAYERS, A_DV), 0.05)
    a_w_out = nrm(ks[6], (N_A_LAYERS, A_V, D_MODEL), DN_BETA * A_V ** -0.5)
    b_w_q = nrm(ks[7], (N_B_LAYERS, D_MODEL, B_QK), D_MODEL ** -0.5)
    b_w_kv = nrm(ks[8], (D_MODEL, B_QK + B_V), D_MODEL ** -0.5)
    b_lambda = nrm(ks[9], (N_B_LAYERS, 4, B_DH), 0.1)
    b_subln_w = 1.0 + nrm(ks[10], (N_B_LAYERS, 2 * B_DH), 0.05)
    b_w_out = nrm(ks[11], (N_B_LAYERS, B_V, D_MODEL), DN_BETA * B_V ** -0.5)
    rel_bias = nrm(ks[12], (REL_BUCKETS, B_HEADS), 0.5)
    router_w = nrm(ks[13], (D_MODEL, N_EXPERTS), D_MODEL ** -0.5)
    router_b = nrm(ks[14], (N_EXPERTS,), 0.01)
    moe_w_gate = nrm(ks[15], (DEPTH, N_EXPERTS, D_MODEL, D_EXPERT), D_MODEL ** -0.5)
    moe_w_up = nrm(ks[16], (DEPTH, N_EXPERTS, D_MODEL, D_EXPERT), D_MODEL ** -0.5)
    moe_w_down = nrm(ks[17], (DEPTH, N_EXPERTS, D_EXPERT, D_MODEL), DN_BETA * D_EXPERT ** -0.5)
    ln_w = 1.0 + nrm(ks[18], (DEPTH, 2, D_MODEL), 0.05)
    ln_b = nrm(ks[19], (DEPTH, 2, D_MODEL), 0.02)
    return {'x': x, 'a_w_in': a_w_in, 'a_conv': a_conv, 'a_A_log': a_A_log,
            'a_dt_bias': a_dt_bias, 'a_norm_w': a_norm_w, 'a_w_out': a_w_out,
            'b_w_q': b_w_q, 'b_w_kv': b_w_kv, 'b_lambda': b_lambda, 'b_subln_w': b_subln_w,
            'b_w_out': b_w_out, 'rel_bias': rel_bias, 'router_w': router_w, 'router_b': router_b,
            'moe_w_gate': moe_w_gate, 'moe_w_up': moe_w_up, 'moe_w_down': moe_w_down,
            'ln_w': ln_w, 'ln_b': ln_b}

def reference(x, a_w_in, a_conv, a_A_log, a_dt_bias, a_norm_w, a_w_out, b_w_q, b_w_kv,
              b_lambda, b_subln_w, b_w_out, rel_bias, router_w, router_b,
              moe_w_gate, moe_w_up, moe_w_down, ln_w, ln_b):
    t_len = x.shape[1]
    dist_bias = rel_bias[t5_bucket(jnp.arange(t_len))].T.astype(F32)
    k_sh = None
    v_sh = None
    for l in range(DEPTH):
        if l < N_A_LAYERS:
            h = gated_deltanet_mixer(x, a_w_in[l], a_conv[l], a_A_log[l], a_dt_bias[l],
                                     a_norm_w[l], a_w_out[l])
        else:
            if l == N_A_LAYERS:
                k_sh, v_sh = shared_kv(x, b_w_kv)
            j = l - N_A_LAYERS
            h = diff_attention_mixer(x, k_sh, v_sh, dist_bias, b_w_q[j], b_lambda[j],
                                     b_subln_w[j], b_w_out[j], lambda_init_for(l))
        x = layer_norm(DN_ALPHA * x + h, ln_w[l, 0], ln_b[l, 0])
        y = grouped_moe(x, router_w, router_b, moe_w_gate[l], moe_w_up[l], moe_w_down[l])
        x = layer_norm(DN_ALPHA * x + y, ln_w[l, 1], ln_b[l, 1])
    return x


_drawn_inputs = setup_inputs


def setup_inputs(seed=0):
    import zlib

    import numpy as np

    out = dict(_drawn_inputs(seed))
    spreads = {}
    factors = {'b_lambda': 4.335}
    for name, (base, spread) in spreads.items():
        noise = np.random.default_rng([zlib.crc32(name.encode()), seed]).standard_normal(out[name].shape)
        drawn = base * np.exp(spread * noise) if base else spread * noise
        out[name] = __import__('jax').numpy.asarray(drawn.astype(out[name].dtype))
    for name, factor in factors.items():
        out[name] = (out[name] * factor).astype(out[name].dtype)
    return out
```

```python
from contextlib import ExitStack
import math

import numpy as np

import concourse.bass as bass
from concourse import mybir

F32 = mybir.dt.float32
I32 = mybir.dt.int32
ACT = mybir.ActivationFunctionType
ALU = mybir.AluOpType
AX_X = mybir.AxisListType.X

P = 128
T = 256
TT = T // P
D = 1024
KC = D // P
HA = 8
HB = 8
DH = 64
TAPS = 4
NE = 16
GRP = 4
FE = 512
CAP = 64
PASSES = T // CAP
DEPTH = 2
ALPHA = (2 * DEPTH) ** 0.25
LN_EPS = 1e-5
RMS_EPS = 1e-6
LAMBDA_INIT = 0.8 - 0.6 * math.exp(-0.3)
BUCKETS = 32
MAX_DIST = 128
REV = 384
MASKED = -1e30

SLOT = 4096
RING = 6
BASE_A = 0
BASE_M0 = BASE_A + 10
BASE_B = BASE_M0 + 3 * NE
BASE_M1 = BASE_B + 8

C_ID, C_ONE, C_TRI, C_TRIS, C_LOW, C_LOWS, C_LEV, C_ALPHA = 0, 1, 2, 3, 4, 5, 6, 13
C_REV = 14
C_IOTA = 15 * P
C_W4 = C_IOTA + CAP
C_COLS = C_W4 + GRP


def constants():
    i = np.arange(P)
    r, c = i[:, None], i[None, :]
    out = np.zeros((P, C_COLS), np.float32)

    def put(k, m):
        out[:, k * P:(k + 1) * P] = m

    put(C_ID, r == c)
    put(C_ONE, 1.0)
    put(C_TRI, r <= c)
    put(C_TRIS, r < c)
    put(C_LOW, r >= c)
    put(C_LOWS, r > c)
    for n in range(7):
        s = 1 << n
        put(C_LEV + n, (r // (2 * s) == c // (2 * s)) & (r // s % 2 == 1) & (c // s % 2 == 0))
    put(C_ALPHA, ALPHA * (r == c))
    put(C_REV, r + c == P - 1)
    out[:, C_IOTA:C_IOTA + CAP] = np.arange(CAP)
    out[:, C_W4:C_W4 + GRP] = GRP - np.arange(GRP)
    return out


def bucket_rows():
    out = np.zeros((BUCKETS, REV), np.float32)
    half = BUCKETS // 2
    for m in range(T):
        n = T - 1 - m
        b = n if n < half else min(BUCKETS - 1, half + int(
            np.float32(np.log(np.float32(n) / np.float32(half)) / math.log(MAX_DIST / half) * (BUCKETS - half))))
        out[b, m] = 1.0
    return out


def build(nc, x, a_w_in, a_conv, a_A_log, a_dt_bias, a_norm_w, a_w_out, b_w_q, b_w_kv, b_lambda, b_subln_w,
          b_w_out, rel_bias, router_w, router_b, moe_w_gate, moe_w_up, moe_w_down, ln_w, ln_b, consts, buckets,
          bias_rows, out):
    with ExitStack() as ctx:
        def sb(name, shape, dt=F32):
            return ctx.enter_context(nc.sbuf_tensor(name, shape, dt))

        def sem(name):
            return ctx.enter_context(nc.semaphore(name))

        ring = sb("ring", [P, RING, SLOT])
        xN = sb("xN", [P, TT, D])
        xT = sb("xT", [P, KC, T])
        oN = sb("oN", [P, TT, D])
        cst = sb("cst", [P, C_COLS])
        arena = sb("arena", [P, 19456])
        small = sb("small", [P, 768])
        flag = sb("flag", [P, 1], I32)

        def mask(k):
            return cst[:, k * P:(k + 1) * P]

        ident, ones, tri, tris, low, lows, alphaI = (mask(k) for k in (C_ID, C_ONE, C_TRI, C_TRIS, C_LOW, C_LOWS, C_ALPHA))
        reverse = mask(C_REV)
        iota = cst[:, C_IOTA:C_IOTA + CAP]
        w4 = cst[:, C_W4:C_W4 + GRP]

        taken = [0]

        def tiny(*shape):
            n = int(np.prod(shape))
            v = small[:, taken[0]:taken[0] + n]
            taken[0] += n
            assert taken[0] <= 768
            if len(shape) == 2:
                v = v.rearrange("p (a b) -> p a b", a=shape[0])
            if len(shape) == 3:
                v = v.rearrange("p (a b c) -> p a b c", a=shape[0], b=shape[1])
            return v

        def view(at, *shape):
            n = int(np.prod(shape))
            v = arena[:, at:at + n]
            if len(shape) == 2:
                v = v.rearrange("p (a b) -> p a b", a=shape[0])
            if len(shape) == 3:
                v = v.rearrange("p (a b c) -> p a b c", a=shape[0], b=shape[1])
            return v

        qkT = view(0, 16, T)
        vN = view(4096, TT, D)
        kN = view(6144, HA, P)
        z = view(7168, TT, D)
        Dm = view(9216, 16, P)
        Nm = view(11264, 16, P)
        QK = view(13312, 16, P)
        Ti = view(15360, 16, P)
        TiT = view(17408, 16, P)
        conv = view(11264, 4, T)
        vT = view(15360, 8, T)
        sq = view(17408, 4, 512)
        PT = xT[:, :, :].rearrange("p a (b c) -> p (a b) c", b=2)
        S = view(15360, HA, P)
        qS = view(16384, HA, P)
        oT = view(9216, KC, T)
        lnpA = view(11264, 2, D)

        kT = view(0, HB, T)
        vB = view(2048, TT, D)
        qz = view(4096, HB, 2, T)
        bias = view(8192, HB, T)
        braw = view(13312, HB, T)
        sc = view(13312, 2, 2 * T)
        pa = view(14336, 2, 2 * T)
        at = view(15360, 2, T)
        atT = view(15872, 2, TT, P)
        brow = view(16384, REV)
        oh = view(16768, REV)
        rbT = view(17152, HB)
        lam = view(17160, 4, DH)
        lp = view(17416, 2, DH)
        nwB = view(17544, P)

        xeT = view(0, 2, KC * CAP)
        sg = view(1024, 2, 256)
        hN = view(1536, 2, 256)
        hTG = view(2048, 2, 512)
        ys = view(3072, D)
        Pb = view(4096, 2, TT, CAP)
        G2 = view(4352, TT, P)
        RK = view(4608, TT, NE * PASSES + 2)
        gate = view(4740, TT, NE + 2)
        rt = view(4800, 1024)
        ovw = view(7168, 3, SLOT)

        cw = tiny(TAPS * 24)
        wab = view(13312, KC, 16)
        cwr = view(13440, P)
        ab = tiny(TT, 16)
        alog = tiny(8)
        dtb = tiny(8)
        g = tiny(TT, HA)
        beta = tiny(TT, HA)
        gt1 = tiny(TT, HA)
        gt2 = tiny(TT, HA)
        gc = tiny(TT, HA)
        eg = tiny(TT, HA)
        kd = tiny(TT, HA)
        nb = tiny(TT, HA)
        nbe = tiny(TT, HA)
        ms = tiny(TT, HA)
        nw = tiny(P)
        st6 = tiny(TT, 2, 6)
        mv = tiny(TT, 2)
        rstd = tiny(TT)
        nmr = tiny(TT)
        rw = sb("rw", [P, KC, NE])
        rb = tiny(NE)
        lam2 = tiny(2)
        lamv = tiny(1)
        smx = tiny(2, 2)
        ssum = tiny(2, 2)
        srec = tiny(2, 2)

        bank = [ctx.enter_context(nc.psum_tensor(f"bank{b}", [P, 512], F32)) for b in range(8)]
        Y = bank[0:4]
        GU, XG, YD = bank[4:6], bank[6], bank[7]

        order = []

        def fill(name, n, banks):
            order.extend((name, i, banks[i % len(banks)]) for i in range(n))

        four, low4 = (4, 5, 6, 7), (0, 1, 2, 3)
        fill("xT0", 4, four)
        fill("cw", 1, (4,))
        fill("ab", 1, (5,))
        fill("qk", 8, low4)
        fill("cum", 1, (6,))
        fill("grow", 4, (7, 4, 5, 6))
        fill("qk2", 8, low4)
        fill("vch", 8, low4)
        fill("zz", 4, low4)
        fill("vtr", 4, four)
        fill("ssq", 8, four)
        fill("kk", 4, four)
        fill("kq", 4, four)
        fill("dtr", 4, low4)
        fill("ttr", 4, low4)
        for lev in range(1, 7):
            fill(f"p{lev}", 4, (0, 1, 4, 5))
            if lev < 6:
                fill(f"t{lev}", 4, (2, 6))
            fill(f"tt{lev}", 4, (3, 7))
        fill("ktr", 2, (4, 5))
        fill("vn0", 2, (6, 7))
        fill("o0", 2, (4, 5))
        fill("s1", 2, (6, 7))
        fill("ks", 2, (4, 5))
        fill("qs", 2, (6, 7))
        fill("vn1", 2, (4, 5))
        fill("o1", 2, (6, 7))
        fill("oTa", 4, four)
        fill("ya", 4, low4)
        fill("xT1", 4, four)
        fill("lg0", 1, (4,))
        fill("rk0", 1, (5,))
        fill("y0", 4, low4)
        fill("xT2", 4, four)
        fill("brow", 1, (4,))
        fill("q", 8, (5, 6, 7, 4))
        fill("k", 8, (5, 6, 7, 4))
        fill("v", 4, (5, 6, 7, 4))
        fill("bias", 4, (5, 6, 7, 4))
        for i in range(16):
            order.append(("sc", i, 4 + i % 2))
            if i >= 1:
                order.append(("atT", i - 1, 6))
                order.append(("av", i - 1, 7))
        order.append(("atT", 15, 6))
        order.append(("av", 15, 7))
        fill("oTb", 4, four)
        fill("yb", 4, low4)
        fill("xT3", 4, four)
        fill("lg1", 1, (4,))
        fill("rk1", 1, (5,))
        fill("y1", 4, low4)
        where, per_bank = {}, [0] * 8
        for name, i, b in order:
            where[name, i] = (b, per_bank[b])
            per_bank[b] += 1
        full = [sem(f"bank{b}_full") for b in range(8)]
        free = [sem(f"bank{b}_free") for b in range(8)]

        def ps(name, i=0):
            return bank[where[name, i][0]]

        def before_fill(eng, name, i=0):
            b, k = where[name, i]
            if k:
                eng.wait_ge(free[b], k)

        def filled(ins, name, i=0):
            ins.then_inc(full[where[name, i][0]], 1)

        def wait_full(eng, name, i=0):
            b, k = where[name, i]
            eng.wait_ge(full[b], k + 1)

        def emptied(ins, name, i=0):
            ins.then_inc(free[where[name, i][0]], 1)

        def wait_emptied(eng, name, i=0):
            b, k = where[name, i]
            eng.wait_ge(free[b], k + 1)

        ld_x, ld_cst, ld_cw, ld_ab, ld_par = (sem(n) for n in ("ld_x", "ld_cst", "ld_cw", "ld_ab", "ld_par"))
        ld_att, ld_lnp, ld_bias, st_bias, st_out = (sem(n) for n in ("ld_att", "ld_lnp", "ld_bias", "st_bias", "st_out"))
        ring_loaded = [sem(f"ring{s}_loaded") for s in range(RING)]
        dve_step, act_step, pool_step = sem("dve_step"), sem("act_step"), sem("pool_step")
        names = """gate_abs softplus_done gates_ready beta_ready decay_in decay_ready dm_exp dm_ready silu_done
            sq_ready norm_root qk_normed z_ready nb_ready T_init L_ready r1_ready o_squared o_mean o_root o_normed
            ln_var ln_root ln_scale ln_normed ln_scaled x_ready logits_ready exp_done sel_ready flag_ready
            brow_ready sc_ready p_ready at_ready lam_sum lam_exp lam_ready qz_zero nwB_ready""".split()
        Sm = {n: sem(n) for n in names}

        moe_sems = [{n: sem(f"moe{layer}_{n}") for n in """P_built G_built gathered xe_ready gu_done sg_ready h_ready ht_done
            ht_ready down_done ys_ready scattered o_P o_gathered o_xe o_loaded o_gu o_sg o_h o_ht o_htr o_down o_ys
            o_done""".split()} for layer in range(DEPTH)]

        def signal(ins, name):
            ins.then_inc(Sm[name], 1)

        counts = {}

        def in_step(eng, ins, s):
            counts[s.name] = counts.get(s.name, 0) + 1
            ins.then_inc(s, 1)
            eng.wait_ge(s, counts[s.name])

        def after_load(eng, n):
            eng.wait_ge(ring_loaded[n % RING], 16 * (n // RING + 1))

        def slot(n):
            return ring[:, n % RING, :].rearrange("p (k n) -> p k n", k=KC)

        def w_cols(w, c):
            return w[:, c:c + 512].rearrange("(k p) n -> p k n", p=P)

        block = ctx.enter_context(nc.Block())

        @block.sync
        def _(sp):
            def wait_released(n):
                if n < BASE_M0:
                    n -= BASE_A
                    last = (("qk", 4 * n + 3) if n < 2 else ("qk2", 4 * n - 5) if n < 4 else ("vch", 4 * n - 13) if n < 6
                            else ("zz", 2 * n - 11) if n < 8 else ("ya", n - 6))
                    wait_full(sp, *last)
                elif n < BASE_B or n >= BASE_M1:
                    layer, base = (0, BASE_M0) if n < BASE_B else (1, BASE_M1)
                    e, part = divmod(n - base, 3)
                    sp.wait_ge(moe_sems[layer]["gu_done" if part < 2 else "down_done"], e + 1)
                else:
                    n -= BASE_B
                    last = (("q", 4 * n + 3) if n < 2 else ("k", 4 * n - 5) if n < 4 else ("v", 2 * n - 7) if n < 6
                            else ("yb", n - 4))
                    wait_full(sp, *last)

            def stream(n, src):
                if n >= RING:
                    wait_released(n - RING)
                sp.dma_start(slot(n), src).then_inc(ring_loaded[n % RING], 16)

            sp.dma_start(xN[:, :, :], x[0].rearrange("(t p) d -> p t d", p=P)).then_inc(ld_x, 16)
            for n in range(8):
                stream(BASE_A + n, w_cols(a_w_in[0], 512 * n))
            for n in range(2):
                stream(BASE_A + 8 + n, w_cols(a_w_out[0], 512 * n))

            def expert_load(layer, n, e, j):
                w = (moe_w_gate, moe_w_up, moe_w_down)[j % 3]
                src = w[layer, bass.ds(e, 1)].rearrange("o (k p) n -> p (o k) n", p=P)
                dst = ring[:, n % RING, :].rearrange("p (k n) -> p k n", k=(KC, KC, FE // P)[j % 3])
                sp.dma_start(dst, src).then_inc(ring_loaded[n % RING], 16)

            def experts(layer, base):
                for j in range(6):
                    wait_released(base + j - RING)
                    expert_load(layer, base + j, j // 3, j)
                with sp.Fori(1, NE // 2) as pair:
                    for j in range(6):
                        before = 2 * pair - 2 + j // 3
                        sp.wait_ge(moe_sems[layer]["gu_done" if j % 3 < 2 else "down_done"], before + 1)
                        expert_load(layer, base + j, 2 * pair + j // 3, j)

            experts(0, BASE_M0)
            for n in range(2):
                stream(BASE_B + n, w_cols(b_w_q[0], 512 * n))
            for n in range(4):
                stream(BASE_B + 2 + n, w_cols(b_w_kv, 512 * n))
            for n in range(2):
                stream(BASE_B + 6 + n, w_cols(b_w_out[0], 512 * n))
            experts(1, BASE_M1)
            sp.wait_ge(Sm["x_ready"], 4 * TT)
            sp.dma_start(out[0].rearrange("(t p) d -> p t d", p=P), xN[:, :, :]).then_inc(st_out, 16)
            sp.wait_ge(st_out, 16)

        @block.tensor
        def _(pe):
            def transposes(name, i, parts):
                before_fill(pe, name, i)
                for j, src in enumerate(parts):
                    last = pe.transpose(ps(name, i)[:, j * P:(j + 1) * P], src, ident)
                filled(last, name, i)

            def transpose_x(r):
                for i in range(4):
                    transposes(f"xT{r}", i, [xN[:, tt, kc * P:(kc + 1) * P] for kc in (2 * i, 2 * i + 1) for tt in range(TT)])

            def xT_made(r):
                for i in range(4):
                    wait_emptied(pe, f"xT{r}", i)

            def columns(name, i, n, ct):
                before_fill(pe, name, i)
                for kc in range(KC):
                    last = pe.matmul(ps(name, i)[:, 0:T], slot(n)[:, kc, ct * P:(ct + 1) * P], xT[:, kc, :],
                                     start=kc == 0, stop=kc == KC - 1)
                filled(last, name, i)
                return last

            def rows(name, i, n, tt):
                before_fill(pe, name, i)
                for kc in range(KC):
                    last = pe.matmul(ps(name, i)[:, :], xT[:, kc, tt * P:(tt + 1) * P], slot(n)[:, kc, :],
                                     start=kc == 0, stop=kc == KC - 1)
                filled(last, name, i)
                return last

            pe.wait_ge(ld_x, 16)
            pe.wait_ge(ld_cst, 16)
            transpose_x(0)
            pe.wait_ge(ld_cw, 16)
            before_fill(pe, "cw")
            filled(pe.transpose(ps("cw")[:, 0:96], cwr[0:96, :], ident[0:96, 0:96]), "cw")
            pe.wait_ge(ld_ab, 16)
            xT_made(0)
            before_fill(pe, "ab")
            for tt in range(TT):
                for kc in range(KC):
                    last = pe.matmul(ps("ab")[:, tt * 16:(tt + 1) * 16], xT[:, kc, tt * P:(tt + 1) * P], wab[:, kc, :],
                                     start=kc == 0, stop=kc == KC - 1)
            filled(last, "ab")
            for n in range(2):
                after_load(pe, n)
                for ct in range(4):
                    last = columns("qk", 4 * n + ct, n, ct)
            pe.wait_ge(Sm["gates_ready"], 1)
            before_fill(pe, "cum")
            gall = g[:, :, :].rearrange("p a b -> p (a b)")
            pe.matmul(ps("cum")[:, 0:16], tri, gall, start=True, stop=True)
            filled(pe.matmul(ps("cum")[:, 16:32], ones, gall, start=True, stop=True), "cum")
            for i in range(4):
                before_fill(pe, "grow", i)
                for j in range(4):
                    ch = 4 * i + j
                    last = pe.matmul(ps("grow", i)[:, j * P:(j + 1) * P], gall[:, ch:ch + 1].to_broadcast([P, P]), tri,
                                     start=True, stop=True)
                filled(last, "grow", i)
            for n in range(2, 6):
                after_load(pe, n)
                for ct in range(4):
                    last = columns("qk2" if n < 4 else "vch", 4 * (n % 2) + ct, n, ct)
            for n in range(6, 8):
                after_load(pe, n)
                for tt in range(TT):
                    last = rows("zz", 2 * (n - 6) + tt, n, tt)
            pe.wait_ge(Sm["silu_done"], 24)
            for i in range(4):
                tt, hg = i // 2, i % 2
                transposes("vtr", i, [vT[:, 4 * hg + j, tt * P:(tt + 1) * P] for j in range(4)])
            for i in range(8):
                before_fill(pe, "ssq", i)
                pe.wait_ge(Sm["sq_ready"], i + 1)
                filled(pe.matmul(ps("ssq", i)[:, :], ones, sq[:, i % 4, :], start=True, stop=True), "ssq", i)
            pe.wait_ge(Sm["qk_normed"], 8)
            for name, q0 in (("kk", 8), ("kq", 0)):
                for b in range(4):
                    before_fill(pe, name, b)
                    for j in range(4):
                        h, t0 = 4 * (b % 2) + j, (b // 2) * P
                        last = pe.matmul(ps(name, b)[:, j * P:(j + 1) * P], qkT[:, 8 + h, t0:t0 + P],
                                         qkT[:, q0 + h, t0:t0 + P], start=True, stop=True)
                    filled(last, name, b)
            pe.wait_ge(Sm["dm_ready"], 4)
            for b in range(4):
                transposes("dtr", b, [Dm[:, 4 * b + j, :] for j in range(4)])
            for b in range(4):
                pe.wait_ge(Sm["T_init"], b + 1)
                transposes("ttr", b, [Ti[:, 4 * b + j, :] for j in range(4)])
            for lev in range(1, 7):
                for b in range(4):
                    pe.wait_ge(Sm["L_ready"], 4 * (lev - 1) + b + 1)
                    wait_emptied(pe, f"tt{lev - 1}" if lev > 1 else "ttr", b)
                    before_fill(pe, f"p{lev}", b)
                    for j in range(4):
                        m = 4 * b + j
                        last = pe.matmul(ps(f"p{lev}", b)[:, j * P:(j + 1) * P], Dm[:, m, :], TiT[:, m, :],
                                         start=True, stop=True)
                    filled(last, f"p{lev}", b)
                for b in range(4):
                    wait_emptied(pe, f"p{lev}", b)
                    if lev > 1:
                        wait_emptied(pe, f"t{lev - 1}", b)
                    if lev < 6:
                        before_fill(pe, f"t{lev}", b)
                        for j in range(4):
                            m = 4 * b + j
                            last = pe.matmul(ps(f"t{lev}", b)[:, j * P:(j + 1) * P], PT[:, m, :], Ti[:, m, :],
                                             start=True, stop=True)
                        filled(last, f"t{lev}", b)
                    before_fill(pe, f"tt{lev}", b)
                    for j in range(4):
                        m = 4 * b + j
                        last = pe.matmul(ps(f"tt{lev}", b)[:, j * P:(j + 1) * P], Ti[:, m, :], PT[:, m, :],
                                         start=True, stop=True)
                    filled(last, f"tt{lev}", b)

            def by_head(name, i, lhsT, rhs):
                before_fill(pe, name, i)
                for j in range(4):
                    h = 4 * i + j
                    last = pe.matmul(ps(name, i)[:, j * P:(j + 1) * P], lhsT(h), rhs(h), start=True, stop=True)
                filled(last, name, i)

            for i in range(2):
                transposes("ktr", i, [qkT[:, 8 + 4 * i + j, 0:P] for j in range(4)])
            for b in range(4):
                wait_emptied(pe, "tt6", b)
                wait_emptied(pe, "kq", b)
                wait_emptied(pe, "vtr", b)
            for i in range(2):
                by_head("vn0", i, lambda h: TiT[:, h, :], lambda h: vN[:, 0, h * P:(h + 1) * P])
            for i in range(2):
                wait_emptied(pe, "vn0", i)
                wait_emptied(pe, "ktr", i)
                by_head("o0", i, lambda h: QK[:, h, :], lambda h: vN[:, 0, h * P:(h + 1) * P])
                by_head("s1", i, lambda h: kN[:, h, :], lambda h: vN[:, 0, h * P:(h + 1) * P])
            for i in range(2):
                wait_emptied(pe, "s1", i)
                by_head("ks", i, lambda h: qkT[:, 8 + h, P:T], lambda h: S[:, h, :])
                by_head("qs", i, lambda h: qkT[:, h, P:T], lambda h: S[:, h, :])
            for i in range(2):
                pe.wait_ge(Sm["r1_ready"], i + 1)
                by_head("vn1", i, lambda h: TiT[:, 8 + h, :], lambda h: vN[:, 1, h * P:(h + 1) * P])
            for i in range(2):
                wait_emptied(pe, "vn1", i)
                by_head("o1", i, lambda h: QK[:, 8 + h, :], lambda h: vN[:, 1, h * P:(h + 1) * P])

            def residual(name, alone=False):
                for i in range(4):
                    tt, n = i // 2, i % 2
                    before_fill(pe, name, i)
                    pe.matmul(ps(name, i)[:, :], alphaI, xN[:, tt, n * 512:(n + 1) * 512], start=True, stop=alone)

            def project_out(r, base, src, oname):
                residual(f"y{oname}")
                for i in range(4):
                    pe.wait_ge(Sm["o_normed"], 2 * (1 if oname == "b" else 0) + 2)
                    transposes(f"oT{oname}", i, [oN[:, tt, kc * P:(kc + 1) * P] for kc in (2 * i, 2 * i + 1) for tt in range(TT)])
                for i in range(4):
                    wait_emptied(pe, f"oT{oname}", i)
                for n in range(2):
                    after_load(pe, base + n)
                    for tt in range(TT):
                        i = 2 * tt + n
                        for kc in range(KC):
                            last = pe.matmul(ps(f"y{oname}", i)[:, :], src[:, kc, tt * P:(tt + 1) * P],
                                             slot(base + n)[:, kc, :], start=False, stop=kc == KC - 1)
                        last.then_inc(full[where[f"y{oname}", i][0]], 1)

            project_out(0, BASE_A + 8, oT, "a")

            def route(layer):
                pe.wait_ge(Sm["x_ready"], (4 * layer + 2))
                transpose_x(1 + 2 * layer)
                xT_made(1 + 2 * layer)
                lg = f"lg{layer}"
                before_fill(pe, lg)
                for tt in range(TT):
                    for kc in range(KC):
                        last = pe.matmul(ps(lg)[:, tt * NE:(tt + 1) * NE], xT[:, kc, tt * P:(tt + 1) * P], rw[:, kc, :],
                                         start=kc == 0, stop=kc == KC - 1)
                filled(last, lg)
                residual(f"y{layer}", alone=True)
                pe.wait_ge(Sm["sel_ready"], layer + 1)
                rk = f"rk{layer}"
                before_fill(pe, rk)
                sel = rt[:, 0:2 * NE]
                pe.matmul(ps(rk)[:, 0:NE], tris, sel[:, 0:NE], start=True, stop=True)
                pe.matmul(ps(rk)[:, NE:2 * NE], ones, sel[:, 0:NE], start=True, stop=False)
                pe.matmul(ps(rk)[:, NE:2 * NE], tris, sel[:, NE:2 * NE], start=False, stop=True)
                pe.matmul(ps(rk)[:, 2 * NE:3 * NE], ones, sel[:, 0:NE], start=True, stop=False)
                filled(pe.matmul(ps(rk)[:, 2 * NE:3 * NE], ones, sel[:, NE:2 * NE], start=False, stop=True), rk)

            def gather(buf):
                for kc in range(KC):
                    for tt in range(TT):
                        last = pe.matmul(XG[:, kc * CAP:(kc + 1) * CAP], xN[:, tt, kc * P:(kc + 1) * P],
                                         Pb[:, buf, tt, :], start=tt == 0, stop=tt == TT - 1)
                return last

            def experts(layer, base):
                s = moe_sems[layer]
                pe.wait_ge(s["P_built"], 1)
                wait_emptied(pe, f"rk{layer}")
                gather(0).then_inc(s["gathered"], 1)
                with pe.Fori(0, NE // 2) as pair:
                    for par in range(2):
                        e = 2 * pair + par
                        sg_, su_, sd_ = base + 3 * par, base + 3 * par + 1, base + 3 * par + 2
                        g0 = ring[:, sg_ % RING:sg_ % RING + 2, :].rearrange("p s (k n) -> p s k n", k=KC)
                        dn = ring[:, sd_ % RING, :].rearrange("p (k n) -> p k n", k=FE // P)
                        pe.wait_ge(s["xe_ready"], e + 1)
                        for n in (sg_, su_):
                            pe.wait_ge(ring_loaded[n % RING], 16 * (n // RING + 1) + 16 * pair)
                        for kc in range(KC):
                            for half in range(2):
                                last = pe.matmul(GU[par][64 * half:64 * half + 64, :], xeT[:, par, kc * CAP:(kc + 1) * CAP],
                                                 g0[:, :, kc, 256 * half:256 * half + 256], start=kc == 0, stop=kc == KC - 1)
                        last.then_inc(s["gu_done"], 1)
                        pe.wait_ge(s["P_built"], e + 2)
                        gather(1 - par).then_inc(s["gathered"], 1)
                        pe.wait_ge(s["h_ready"], e + 1)
                        for c in range(2):
                            last = pe.transpose(GU[par][:, c * P:(c + 1) * P], hN[:, par, c * P:(c + 1) * P], ident)
                        if par == 1:
                            pe.wait_ge(s["G_built"], pair + 1)
                            for tt in range(TT):
                                last = pe.transpose(GU[1][:, 256 + tt * P:256 + (tt + 1) * P], G2[:, tt, :], ident)
                        last.then_inc(s["ht_done"], 1)
                        pe.wait_ge(s["ht_ready"], e + 1)
                        pe.wait_ge(ring_loaded[sd_ % RING], 16 * (sd_ // RING + 1) + 16 * pair)
                        if par == 1:
                            pe.wait_ge(s["ys_ready"], 4 * pair + 2)
                        for fc in range(4):
                            lhs = hTG[:, par, (fc % 2) * P + (fc // 2) * CAP:(fc % 2) * P + (fc // 2) * CAP + CAP]
                            for n in range(2):
                                last = pe.matmul(YD[64 * n:64 * n + 64, :], lhs, dn[:, fc, n * 512:(n + 1) * 512],
                                                 start=fc == 0, stop=fc == 3)
                        last.then_inc(s["down_done"], 1)
                    pe.wait_ge(s["ys_ready"], 4 * pair + 4)
                    for i in range(4):
                        tt, n = i // 2, i % 2
                        last = pe.matmul(Y[i][:, :], hTG[:, 1, 256 + tt * P:256 + (tt + 1) * P], ys[:, n * 512:(n + 1) * 512],
                                         start=False, stop=True, skip_group_check=True)
                    last.then_inc(s["scattered"], 1)
                pe.wait_ge(s["scattered"], NE // 2)

            def overflow(layer):
                s = moe_sems[layer]
                pe.wait_ge(Sm["flag_ready"], layer + 1)
                more = pe.value_load(flag[0:1, 0:1], min_val=0, max_val=T)
                with pe.If(more > CAP):
                    pe.sem_inc(s["o_done"], 1)
                    with pe.Fori(1, PASSES) as ps_:
                        with pe.Fori(0, NE) as ei:
                            it = (ps_ - 1) * NE + ei
                            pe.wait_ge(s["o_P"], it + 1)
                            gather(0).then_inc(s["o_gathered"], 1)
                            pe.wait_ge(s["o_xe"], it + 1)
                            pe.wait_ge(s["o_loaded"], 48 * it + 48)
                            wv = ovw[:, 0:2, :].rearrange("p s (k n) -> p s k n", k=KC)
                            for kc in range(KC):
                                for half in range(2):
                                    last = pe.matmul(GU[0][64 * half:64 * half + 64, :], xeT[:, 0, kc * CAP:(kc + 1) * CAP],
                                                     wv[:, :, kc, 256 * half:256 * half + 256], start=kc == 0, stop=kc == KC - 1)
                            last.then_inc(s["o_gu"], 1)
                            pe.wait_ge(s["o_h"], it + 1)
                            for c in range(2):
                                pe.transpose(GU[0][:, c * P:(c + 1) * P], hN[:, 0, c * P:(c + 1) * P], ident)
                            for tt in range(TT):
                                last = pe.transpose(GU[0][:, 256 + tt * P:256 + (tt + 1) * P], G2[:, tt, :], ident)
                            last.then_inc(s["o_ht"], 1)
                            pe.wait_ge(s["o_htr"], it + 1)
                            dn = ovw[:, 2, :].rearrange("p (k n) -> p k n", k=FE // P)
                            for fc in range(4):
                                lhs = hTG[:, 0, (fc % 2) * P + (fc // 2) * CAP:(fc % 2) * P + (fc // 2) * CAP + CAP]
                                for n in range(2):
                                    last = pe.matmul(YD[64 * n:64 * n + 64, :], lhs, dn[:, fc, n * 512:(n + 1) * 512],
                                                     start=fc == 0, stop=fc == 3)
                            last.then_inc(s["o_down"], 1)
                            pe.wait_ge(s["o_ys"], 2 * it + 2)
                            for i in range(4):
                                tt, n = i // 2, i % 2
                                last = pe.matmul(Y[i][:, :], hTG[0:CAP, 0, 256 + tt * P:256 + (tt + 1) * P],
                                                 ys[0:CAP, n * 512:(n + 1) * 512], start=False, stop=True,
                                                 skip_group_check=True)
                            last.then_inc(s["o_done"], 1)
                    pe.wait_ge(s["o_done"], NE * (PASSES - 1) + 1)
                for i in range(4):
                    pe.sem_inc(full[where[f"y{layer}", i][0]], 1)

            route(0)
            experts(0, BASE_M0)
            overflow(0)

            pe.wait_ge(Sm["x_ready"], 4)
            transpose_x(2)
            pe.wait_ge(ld_att, 16 * 4)
            before_fill(pe, "brow")
            filled(pe.matmul(ps("brow")[0:HB, 0:REV], rbT[0:BUCKETS, :], oh[0:BUCKETS, :], start=True, stop=True), "brow")
            xT_made(2)
            for n in range(4):
                after_load(pe, BASE_B + n)
                for ct in range(4):
                    last = columns("q" if n < 2 else "k", 4 * (n % 2) + ct, BASE_B + n, ct)
            for n in range(4, 6):
                after_load(pe, BASE_B + n)
                for tt in range(TT):
                    last = rows("v", 2 * (n - 4) + tt, BASE_B + n, tt)
            pe.wait_ge(ld_bias, 16)
            for i in range(4):
                before_fill(pe, "bias", i)
                filled(pe.matmul(ps("bias", i)[:, :], reverse, braw[:, 2 * i:2 * i + 2, :], start=True, stop=True), "bias", i)
            for i in range(8):
                wait_emptied(pe, "q", i)
                wait_emptied(pe, "k", i)
            for i in range(4):
                wait_emptied(pe, "v", i)

            def av(i):
                qt, h = i // 8, i % 8
                pe.wait_ge(Sm["at_ready"], i + 1)
                before_fill(pe, "atT", i)
                for kt in range(qt + 1):
                    last = pe.transpose(ps("atT", i)[:, kt * P:(kt + 1) * P], at[:, i % 2, kt * P:(kt + 1) * P], ident)
                filled(last, "atT", i)
                wait_emptied(pe, "atT", i)
                before_fill(pe, "av", i)
                for kt in range(qt + 1):
                    last = pe.matmul(ps("av", i)[:, 0:P], atT[:, i % 2, kt, :], vB[:, kt, h * P:(h + 1) * P],
                                     start=kt == 0, stop=kt == qt)
                filled(last, "av", i)

            for i in range(16):
                qt, h = i // 8, i % 8
                before_fill(pe, "sc", i)
                for half in range(2):
                    last = pe.matmul(ps("sc", i)[:, half * T:half * T + (qt + 1) * P], qz[:, h, half, qt * P:(qt + 1) * P],
                                     kT[:, h, 0:(qt + 1) * P], start=True, stop=True)
                filled(last, "sc", i)
                if i >= 1:
                    av(i - 1)
            av(15)
            project_out(2, BASE_B + 6, kT, "b")
            route(1)
            experts(1, BASE_M1)
            overflow(1)

        @block.scalar
        def _(act):
            def go(out_, in_, f, **kw):
                return act.activation(out_, in_, f, **kw)

            act.dma_start(cst[:, :], consts).then_inc(ld_cst, 16)
            act.dma_start(cwr[0:96, :], a_conv[0].rearrange("i (t c) -> (i t) c", c=P)).then_inc(ld_cw, 16)
            act.dma_start(wab[:, :, :], a_w_in[0, :, 4096:4112].rearrange("(k p) n -> p k n", p=P)).then_inc(ld_ab, 16)
            for dst, src in ((alog, a_A_log), (dtb, a_dt_bias), (nw, a_norm_w)):
                act.dma_start(dst, src.to_broadcast([P, src.shape[1]])).then_inc(ld_par, 16)
            act.dma_start(rb, router_b.rearrange("(a n) -> a n", a=1).to_broadcast([P, NE])).then_inc(ld_par, 16)
            act.dma_start(rw[:, :, :], router_w.rearrange("(k p) n -> p k n", p=P)).then_inc(ld_par, 16)

            def xT_half(r):
                for i in (0, 2):
                    wait_full(act, f"xT{r}", i)
                    emptied(go(xT[:, 2 * i:2 * i + 2, :], ps(f"xT{r}", i).rearrange("p (a b) -> p a b", a=2), ACT.Copy),
                            f"xT{r}", i)

            xT_half(0)
            act.wait_ge(Sm["gate_abs"], 1)
            in_step(act, go(gt2, gt2, ACT.Exp, scale=-1.0), act_step)
            act.wait_ge(ld_par, 16 * 5)
            go(alog, alog, ACT.Exp)
            go(beta, ab[:, :, HA:2 * HA], ACT.Exp, scale=-1.0)
            go(gt2, gt2, ACT.Ln, bias=1.0).then_inc(Sm["softplus_done"], 1)
            for t in range(24):
                if t == 8:
                    act.wait_ge(Sm["decay_in"], 1)
                    go(eg, gc, ACT.Exp)
                    go(kd, kd, ACT.Exp).then_inc(Sm["decay_ready"], 1)
                    for i in range(4):
                        wait_emptied(act, "grow", i)
                        d = Dm[:, 4 * i:4 * i + 4, :]
                        go(d, d, ACT.Exp, scale=-1.0).then_inc(Sm["dm_exp"], 1)
                name = ("qk", "qk2", "vch")[t // 8]
                wait_emptied(act, name, t % 8)
                go(qkT[:, t, :] if t < 16 else vT[:, t - 16, :], conv[:, t % 4, :], ACT.Silu).then_inc(Sm["silu_done"], 1)
            for i in range(4):
                wait_full(act, "zz", i)
                emptied(go(z[:, i % 2, 512 * (i // 2):512 * (i // 2) + 512], ps("zz", i)[:, :], ACT.Silu), "zz", i)

            def square(i):
                go(sq[:, i % 4, :].rearrange("p (a b) -> p a b", a=2), qkT[:, 2 * i:2 * i + 2, :], ACT.Square)\
                    .then_inc(Sm["sq_ready"], 1)

            act.wait_ge(Sm["silu_done"], 16)
            for i in range(4):
                square(i)
            for i in range(8):
                wait_full(act, "ssq", i)
                k = float(P) if i < 4 else 1.0
                emptied(go(sq[:, i % 4, :], ps("ssq", i)[:, :], ACT.Sqrt, scale=k, bias=k * RMS_EPS), "ssq", i)
                if i < 4:
                    act.wait_ge(Sm["qk_normed"], i + 1)
                    square(i + 4)
            for b in range(4):
                wait_full(act, "dtr", b)
                emptied(go(QK[:, 4 * b:4 * b + 4, :], ps("dtr", b).rearrange("p (a b) -> p a b", a=4), ACT.Copy), "dtr", b)
            for b in range(4):
                wait_full(act, "ttr", b)
                emptied(go(TiT[:, 4 * b:4 * b + 4, :], ps("ttr", b).rearrange("p (a b) -> p a b", a=4), ACT.Copy), "ttr", b)
            for lev in range(1, 7):
                for b in range(4):
                    if lev > 1:
                        wait_full(act, f"tt{lev - 1}", b)
                    wait_full(act, f"p{lev}", b)
                    emptied(go(PT[:, 4 * b:4 * b + 4, :], ps(f"p{lev}", b).rearrange("p (a b) -> p a b", a=4), ACT.Copy),
                            f"p{lev}", b)
            for i in range(2):
                wait_full(act, "vn0", i)
                emptied(go(vN[:, 0, 512 * i:512 * i + 512], ps("vn0", i)[:, :], ACT.Copy), "vn0", i)
            for i in range(2):
                wait_full(act, "o0", i)
                emptied(go(oN[:, 0, 512 * i:512 * i + 512], ps("o0", i)[:, :], ACT.Copy), "o0", i)
            for i in range(2):
                wait_full(act, "vn1", i)
                emptied(go(vN[:, 1, 512 * i:512 * i + 512], ps("vn1", i)[:, :], ACT.Copy), "vn1", i)

            def heads_norm(r, oname):
                for tt in range(TT):
                    if tt == 0 and oname == "a":
                        for i in range(2):
                            wait_emptied(act, "o0", i)
                    elif oname == "a":
                        for i in range(2):
                            wait_emptied(act, "o1", i)
                    else:
                        for i in range(8):
                            wait_emptied(act, "av", 8 * tt + i)
                    go(xT[:, 4 * tt:4 * tt + 4, :], oN[:, tt, :].rearrange("p (a b) -> p a b", a=4), ACT.Square)\
                        .then_inc(Sm["o_squared"], 1)
                for tt in range(TT):
                    act.wait_ge(Sm["o_mean"], 2 * r + tt + 1)
                    go(ms[:, tt, :], ms[:, tt, :], ACT.Sqrt, scale=1.0 / P, bias=RMS_EPS).then_inc(Sm["o_root"], 1)
                dst = oT if oname == "a" else kT
                for i in (0, 2):
                    wait_full(act, f"oT{oname}", i)
                    emptied(go(dst[:, 2 * i:2 * i + 2, :], ps(f"oT{oname}", i).rearrange("p (a b) -> p a b", a=2), ACT.Copy),
                            f"oT{oname}", i)

            def layer_norm(r, y):
                for tt in range(TT):
                    act.wait_ge(Sm["ln_var"], 2 * r + tt + 1)
                    go(rstd[:, tt:tt + 1], mv[:, tt, 1:2], ACT.Sqrt, bias=LN_EPS).then_inc(Sm["ln_root"], 1)
                    act.wait_ge(Sm["ln_scale"], 2 * r + tt + 1)
                    for n in range(2):
                        emptied(go(xN[:, tt, n * 512:(n + 1) * 512], ps(y, 2 * tt + n)[:, :], ACT.Identity,
                                   scale=rstd[:, tt:tt + 1], bias=nmr[:, tt:tt + 1]), y, 2 * tt + n)

            def experts(layer):
                s = moe_sems[layer]

                def tokens(par, count):
                    act.wait_ge(s["gathered"], count)
                    go(xeT[:, par, :], XG[:, :], ACT.Copy).then_inc(s["xe_ready"], 1)

                xT_half(1 + 2 * layer)
                act.wait_ge(Sm["logits_ready"], layer + 1)
                go(rt[:, 64:96], rt[:, 32:64], ACT.Exp).then_inc(Sm["exp_done"], 1)
                tokens(0, 1)
                with act.Fori(0, NE // 2) as pair:
                    for par in range(2):
                        e = 2 * pair + par
                        act.wait_ge(s["gu_done"], e + 1)
                        go(sg[:, par, :], GU[par][:, 0:256], ACT.Silu).then_inc(s["sg_ready"], 1)
                        tokens(1 - par, e + 2)
                        act.wait_ge(s["down_done"], e + 1)
                        go(ys[CAP * par:CAP * par + CAP, 0:512], YD[0:CAP, :], ACT.Copy).then_inc(s["ys_ready"], 1)

                act.wait_ge(Sm["flag_ready"], layer + 1)
                more = act.value_load(flag[0:1, 0:1], min_val=0, max_val=T)
                with act.If(more > CAP):
                    with act.Fori(1, PASSES) as ps_:
                        with act.Fori(0, NE) as ei:
                            it = (ps_ - 1) * NE + ei
                            act.wait_ge(s["o_done"], it + 1)
                            for j, w in enumerate((moe_w_gate, moe_w_up, moe_w_down)):
                                act.dma_start(ovw[:, j, :].rearrange("p (k n) -> p k n", k=(KC, KC, FE // P)[j]),
                                              w[layer, bass.ds(ei, 1)].rearrange("o (k p) n -> p (o k) n", p=P))\
                                    .then_inc(s["o_loaded"], 16)
                            act.wait_ge(s["o_gathered"], it + 1)
                            go(xeT[:, 0, :], XG[:, :], ACT.Copy).then_inc(s["o_xe"], 1)
                            act.wait_ge(s["o_gu"], it + 1)
                            go(sg[:, 0, :], GU[0][:, 0:256], ACT.Silu).then_inc(s["o_sg"], 1)
                            act.wait_ge(s["o_down"], it + 1)
                            go(ys[0:CAP, 0:512], YD[0:CAP, :], ACT.Copy).then_inc(s["o_ys"], 1)

            heads_norm(0, "a")
            layer_norm(0, "ya")
            experts(0)
            layer_norm(1, "y0")

            act.dma_start(rbT[0:BUCKETS, :], rel_bias).then_inc(ld_att, 16)
            act.dma_start(oh[0:BUCKETS, :], buckets).then_inc(ld_att, 16)
            act.dma_start(lam, b_lambda.rearrange("a i d -> a (i d)").to_broadcast([P, 4 * DH]).rearrange("p (a b) -> p a b", a=4))\
                .then_inc(ld_att, 16)
            act.dma_start(nwB, b_subln_w.to_broadcast([P, P])).then_inc(ld_att, 16)
            xT_half(2)
            act.wait_ge(Sm["lam_sum"], 1)
            go(lam2, lam2, ACT.Exp).then_inc(Sm["lam_exp"], 1)
            act.wait_ge(Sm["qz_zero"], 1)
            for h in range(HB):
                wait_full(act, "q", h)
                go(qz[0:DH, h, 0, :], ps("q", h)[0:DH, 0:T], ACT.Copy, scale=DH ** -0.5)
                emptied(go(qz[DH:P, h, 1, :], ps("q", h)[DH:P, 0:T], ACT.Copy, scale=DH ** -0.5), "q", h)
            for i in range(4):
                wait_full(act, "v", i)
                emptied(go(vB[:, i % 2, 512 * (i // 2):512 * (i // 2) + 512], ps("v", i)[:, :], ACT.Copy), "v", i)

            def heads_out(i):
                qt, h = i // 8, i % 8
                wait_full(act, "atT", i)
                emptied(go(atT[:, i % 2, 0:qt + 1, :], ps("atT", i)[:, 0:(qt + 1) * P].rearrange("p (a b) -> p a b", b=P),
                           ACT.Copy), "atT", i)
                wait_full(act, "av", i)
                emptied(go(oN[:, qt, h * P:(h + 1) * P], ps("av", i)[:, 0:P], ACT.Copy), "av", i)

            for i in range(16):
                w = (i // 8 + 1) * P
                act.wait_ge(Sm["sc_ready"], i + 1)
                for half in range(2):
                    last = go(pa[:, i % 2, half * T:half * T + w], sc[:, i % 2, half * T:half * T + w], ACT.Exp,
                              bias=smx[:, i % 2, half:half + 1], accum_out=ssum[:, i % 2, half:half + 1])
                last.then_inc(Sm["p_ready"], 1)
                if i >= 1:
                    heads_out(i - 1)
            heads_out(15)
            heads_norm(1, "b")
            layer_norm(2, "yb")
            experts(1)
            layer_norm(3, "y1")

        @block.vector
        def _(dve):
            def step(ins):
                in_step(dve, ins, dve_step)

            def xT_half(r):
                for i in (1, 3):
                    wait_full(dve, f"xT{r}", i)
                    emptied(dve.tensor_copy(xT[:, 2 * i:2 * i + 2, :], ps(f"xT{r}", i).rearrange("p (a b) -> p a b", a=2)),
                            f"xT{r}", i)

            def bc(v, n):
                return v.unsqueeze(2).to_broadcast([P, v.shape[1], n])

            def quad(name, i):
                return ps(name, i).rearrange("p (a b) -> p a b", a=4)

            xT_half(0)
            wait_full(dve, "cw")
            emptied(dve.tensor_copy(cw, ps("cw")[:, 0:96]), "cw")
            wait_full(dve, "ab")
            dve.wait_ge(ld_par, 16 * 5)
            emptied(dve.tensor_copy(ab, ps("ab")[:, 0:32].rearrange("p (a b) -> p a b", a=2)), "ab")
            wait_emptied(dve, "ab")
            dtb2 = dtb.unsqueeze(1).to_broadcast([P, TT, HA])
            step(dve.tensor_tensor(gt1, ab[:, :, 0:HA], dtb2, ALU.add))
            dve.scalar_tensor_tensor(gt2, gt1, -1.0, gt1, ALU.mult, ALU.max).then_inc(Sm["gate_abs"], 1)
            dve.wait_ge(Sm["softplus_done"], 1)
            step(dve.scalar_tensor_tensor(gt1, gt1, 0.0, gt2, ALU.max, ALU.add))
            alog2 = alog.unsqueeze(1).to_broadcast([P, TT, HA])
            dve.scalar_tensor_tensor(g, gt1, -1.0, alog2, ALU.mult, ALU.mult).then_inc(Sm["gates_ready"], 1)
            step(dve.tensor_scalar(beta, beta, 1.0, None, ALU.add))
            step(dve.reciprocal(beta, beta))
            dve.tensor_scalar(nb, beta, -1.0, None, ALU.mult).then_inc(Sm["beta_ready"], 1)

            def convolve(t):
                name = ("qk", "qk2", "vch")[t // 8]
                src, dst = ps(name, t % 8), conv[:, t % 4, :]
                wait_full(dve, name, t % 8)
                if t >= 4:
                    dve.wait_ge(Sm["silu_done"], t - 3)
                step(dve.tensor_scalar(dst, src[:, 0:T], cw[:, 3 * 24 + t:3 * 24 + t + 1], None, ALU.mult))
                for s in (1, 2, 3):
                    tap = (3 - s) * 24 + t
                    ins = dve.scalar_tensor_tensor(dst[:, s:T], src[:, 0:T - s], cw[:, tap:tap + 1], dst[:, s:T],
                                                   ALU.mult, ALU.add)
                    if s < 3:
                        step(ins)
                    else:
                        emptied(ins, name, t % 8)

            wait_emptied(dve, "cw")
            for t in range(8):
                convolve(t)
            wait_full(dve, "cum")
            gcf = gc[:, :, :].rearrange("p a b -> p (a b)")
            step(dve.tensor_copy(gcf, ps("cum")[:, 0:16]))
            step(dve.tensor_tensor(kd[:, :, :].rearrange("p a b -> p (a b)"), ps("cum")[:, 16:32], gcf, ALU.subtract))
            dve.sem_inc(free[where["cum", 0][0]], 1)
            dve.sem_inc(Sm["decay_in"], 1)
            for i in range(4):
                wait_full(dve, "grow", i)
                for j in range(4):
                    m = 4 * i + j
                    last = dve.tensor_scalar(Dm[:, m, :], ps("grow", i)[:, j * P:(j + 1) * P], gcf[:, m:m + 1], 0.0,
                                             ALU.subtract, ALU.max)
                emptied(last, "grow", i)
            for t in range(8, 24):
                convolve(t)
            for i in range(4):
                tt, hg = i // 2, i % 2
                wait_full(dve, "vtr", i)
                emptied(dve.tensor_tensor(vN[:, tt, 512 * hg:512 * hg + 512].rearrange("p (a b) -> p a b", a=4),
                                          quad("vtr", i), bc(beta[:, tt, 4 * hg:4 * hg + 4], P), ALU.mult), "vtr", i)
            for i in range(8):
                wait_emptied(dve, "ssq", i)
                step(dve.reciprocal(sq[:, i % 4, :], sq[:, i % 4, :]))
                t2 = qkT[:, 2 * i:2 * i + 2, :]
                dve.tensor_tensor(t2, t2, sq[:, i % 4, :].rearrange("p (a b) -> p a b", a=2), ALU.mult)\
                    .then_inc(Sm["qk_normed"], 1)
            for b in range(4):
                wait_full(dve, "kk", b)
                dve.wait_ge(Sm["nb_ready"], b + 1)
                m4 = Nm[:, 4 * b:4 * b + 4, :]
                emptied(dve.tensor_tensor(m4, quad("kk", b), m4, ALU.mult), "kk", b)
            for b in range(4):
                wait_full(dve, "kq", b)
                wait_emptied(dve, "dtr", b)
                m4 = QK[:, 4 * b:4 * b + 4, :]
                emptied(dve.tensor_tensor(m4, quad("kq", b), m4, ALU.mult), "kq", b)
            for lev in range(1, 7):
                for b in range(4):
                    wait_full(dve, f"tt{lev}", b)
                    if lev < 6:
                        wait_full(dve, f"t{lev}", b)
                        m4 = Ti[:, 4 * b:4 * b + 4, :]
                        emptied(dve.tensor_tensor(m4, quad(f"t{lev}", b), m4, ALU.add), f"t{lev}", b)
                    m4 = TiT[:, 4 * b:4 * b + 4, :]
                    emptied(dve.tensor_tensor(m4, quad(f"tt{lev}", b), m4, ALU.add), f"tt{lev}", b)
            for i in range(2):
                wait_full(dve, "ktr", i)
                emptied(dve.tensor_tensor(kN[:, 4 * i:4 * i + 4, :], quad("ktr", i), bc(kd[:, 0, 4 * i:4 * i + 4], P),
                                          ALU.mult), "ktr", i)
            step(dve.tensor_tensor(nbe, nb, eg, ALU.mult))
            for i in range(2):
                wait_full(dve, "s1", i)
                emptied(dve.tensor_copy(S[:, 4 * i:4 * i + 4, :], quad("s1", i)), "s1", i)
            for i in range(2):
                wait_full(dve, "ks", i)
                tmp = PT[:, 4 * i:4 * i + 4, :]
                emptied(dve.tensor_tensor(tmp, quad("ks", i), bc(nbe[:, 1, 4 * i:4 * i + 4], P), ALU.mult), "ks", i)
                wait_emptied(dve, "ks", i)
                v1 = vN[:, 1, 512 * i:512 * i + 512].rearrange("p (a b) -> p a b", a=4)
                dve.tensor_tensor(v1, v1, tmp, ALU.add).then_inc(Sm["r1_ready"], 1)
                wait_full(dve, "qs", i)
                emptied(dve.tensor_tensor(qS[:, 4 * i:4 * i + 4, :], quad("qs", i), bc(eg[:, 1, 4 * i:4 * i + 4], P),
                                          ALU.mult), "qs", i)
            for i in range(2):
                wait_full(dve, "o1", i)
                wait_emptied(dve, "qs", i)
                emptied(dve.tensor_tensor(oN[:, 1, 512 * i:512 * i + 512].rearrange("p (a b) -> p a b", a=4),
                                          quad("o1", i), qS[:, 4 * i:4 * i + 4, :], ALU.add), "o1", i)

            def heads_norm(r, oname):
                for tt in range(TT):
                    dve.wait_ge(Sm["o_squared"], 2 * r + tt + 1)
                    dve.tensor_reduce(ms[:, tt, :], xT[:, 4 * tt:4 * tt + 4, :].rearrange("p a (b c) -> p (a b) c", b=2),
                                      AX_X, ALU.add).then_inc(Sm["o_mean"], 1)
                if oname == "a":
                    dve.wait_ge(Sm["z_ready"], 1)
                else:
                    dve.wait_ge(Sm["nwB_ready"], 1)
                for tt in range(TT):
                    dve.wait_ge(Sm["o_root"], 2 * r + tt + 1)
                    step(dve.reciprocal(ms[:, tt, :], ms[:, tt, :]))
                    o3 = oN[:, tt, :].rearrange("p (a b) -> p a b", a=8)
                    step(dve.tensor_tensor(o3, o3, bc(ms[:, tt, :], P), ALU.mult))
                    if oname == "a":
                        w = z[:, tt, :].rearrange("p (a b) -> p a b", a=8)
                    else:
                        w = nwB.unsqueeze(1).to_broadcast([P, HB, P])
                    dve.tensor_tensor(o3, o3, w, ALU.mult).then_inc(Sm["o_normed"], 1)
                dst = oT if oname == "a" else kT
                for i in (1, 3):
                    wait_full(dve, f"oT{oname}", i)
                    emptied(dve.tensor_copy(dst[:, 2 * i:2 * i + 2, :], ps(f"oT{oname}", i).rearrange("p (a b) -> p a b", a=2)),
                            f"oT{oname}", i)

            def layer_norm(r, y, lnp):
                for tt in range(TT):
                    for n in range(2):
                        wait_full(dve, y, 2 * tt + n)
                        last = dve.bn_stats(st6[:, tt, n, :], ps(y, 2 * tt + n)[:, :])
                    step(last)
                    dve.bn_aggr(mv[:, tt, :], st6[:, tt, :, :].rearrange("p a b -> p (a b)")).then_inc(Sm["ln_var"], 1)
                for tt in range(TT):
                    dve.wait_ge(Sm["ln_root"], 2 * r + tt + 1)
                    step(dve.reciprocal(rstd[:, tt:tt + 1], rstd[:, tt:tt + 1]))
                    dve.scalar_tensor_tensor(nmr[:, tt:tt + 1], mv[:, tt, 0:1], -1.0, rstd[:, tt:tt + 1], ALU.mult, ALU.mult)\
                        .then_inc(Sm["ln_scale"], 1)
                dve.wait_ge(ld_lnp, 32 * (r + 1))
                for tt in range(TT):
                    for n in range(2):
                        wait_emptied(dve, y, 2 * tt + n)
                    dve.tensor_tensor(xN[:, tt, :], xN[:, tt, :], lnp[:, 0, :], ALU.mult).then_inc(Sm["ln_scaled"], 1)

            def route(layer):
                lg, p, a, b_, c, d = (rt[:, 32 * k:32 * k + 32] for k in range(1, 7))
                sel = rt[:, 0:32]

                def t2(v):
                    return v.rearrange("p (a b) -> p a b", a=TT)

                def t8(v):
                    return v.rearrange("p (a b) -> p a b", a=TT * GRP)

                m1, m2, mr = (rt[:, 256 + 8 * k:264 + 8 * k] for k in range(3))
                mx, sm = rt[:, 288:290], rt[:, 290:292]
                gs, gt, gr = (rt[:, 296 + 8 * k:304 + 8 * k] for k in range(3))
                w8 = w4.unsqueeze(1).to_broadcast([P, TT * GRP, GRP])
                w2 = w4.unsqueeze(1).to_broadcast([P, TT, GRP])
                name = f"lg{layer}"
                wait_full(dve, name)
                emptied(dve.tensor_tensor(t2(lg), ps(name)[:, 0:32].rearrange("p (a b) -> p a b", a=TT),
                                          rb.unsqueeze(1).to_broadcast([P, TT, NE]), ALU.add), name)
                wait_emptied(dve, name)
                step(dve.tensor_reduce(mx, t2(lg), AX_X, ALU.max))
                dve.tensor_tensor(t2(lg), t2(lg), bc(mx, NE), ALU.subtract).then_inc(Sm["logits_ready"], 1)
                dve.wait_ge(Sm["exp_done"], layer + 1)
                step(dve.tensor_reduce(sm, t2(p), AX_X, ALU.add))
                step(dve.reciprocal(sm, sm))
                step(dve.tensor_tensor(t2(p), t2(p), bc(sm, NE), ALU.mult))

                def first_best(values, best, rank, top, out_, w, n):
                    step(dve.tensor_reduce(best, values, AX_X, ALU.max))
                    step(dve.tensor_tensor(rank, values, bc(best, GRP), ALU.is_equal))
                    step(dve.tensor_tensor(rank, rank, w, ALU.mult))
                    step(dve.tensor_reduce(top, rank, AX_X, ALU.max))
                    step(dve.tensor_tensor(out_, rank, bc(top, GRP), ALU.is_equal))

                first_best(t8(p), m1, t8(a), mr, t8(b_), w8, 8)
                step(dve.scalar_tensor_tensor(c, b_, -2.0, p, ALU.mult, ALU.add))
                first_best(t8(c), m2, t8(a), mr, t8(d), w8, 8)
                step(dve.tensor_tensor(b_, b_, d, ALU.add))
                step(dve.tensor_tensor(gs, m1, m2, ALU.add))
                first_best(t2(gs), mx, t2(gt), sm, t2(gr), w2, 2)
                dve.tensor_tensor(t8(sel), t8(b_), bc(gr, GRP), ALU.mult).then_inc(Sm["sel_ready"], 1)
                dve.wait_ge(Sm["sel_ready"], layer + 1)
                step(dve.tensor_tensor(p, p, sel, ALU.mult))
                step(dve.tensor_reduce(sm, t2(p), AX_X, ALU.add))
                step(dve.reciprocal(sm, sm))
                step(dve.tensor_tensor(gate[:, :, 0:NE], t2(p), bc(sm, NE), ALU.mult))
                name = f"rk{layer}"
                wait_full(dve, name)
                step(dve.memset(RK[:, :, NE * PASSES:NE * PASSES + 2], -1.0))
                step(dve.scalar_tensor_tensor(t2(a), ps(name)[:, 0:32].rearrange("p (a b) -> p a b", a=TT), 1.0, t2(sel),
                                              ALU.add, ALU.mult))
                step(dve.tensor_reduce(mx[:, 0:1], ps(name)[:, 32:48], AX_X, ALU.max))
                step(dve.tensor_copy(flag[:, :], mx[:, 0:1]))
                dve.sem_inc(Sm["flag_ready"], 1)
                for k in range(PASSES):
                    last = dve.tensor_scalar(RK[:, :, NE * k:NE * k + NE], t2(a), 1.0 + CAP * k, None, ALU.subtract)
                emptied(last, name)
                wait_emptied(dve, name)

            def place(out_, tt, col):
                return dve.tensor_scalar(out_, iota, RK[:, tt, col], None, ALU.is_equal)

            def place_gated(out_, tt, col, e):
                return dve.tensor_scalar(out_, iota, RK[:, tt, col], gate[:, tt, e], ALU.is_equal, ALU.mult)

            def experts(layer):
                s = moe_sems[layer]
                xT_half(1 + 2 * layer)
                route(layer)
                for tt in range(TT):
                    last = place(Pb[:, 0, tt, :], tt, slice(0, 1))
                last.then_inc(s["P_built"], 1)
                with dve.Fori(0, NE // 2) as pair:
                    for par in range(2):
                        e = 2 * pair + par
                        dve.wait_ge(s["gathered"], e + 1)
                        for tt in range(TT):
                            last = place(Pb[:, 1 - par, tt, :], tt, bass.ds(e + 1, 1))
                        last.then_inc(s["P_built"], 1)
                        dve.wait_ge(s["sg_ready"], e + 1)
                        dve.tensor_tensor(hN[:, par, :], GU[par][:, 256:512], sg[:, par, :], ALU.mult).then_inc(s["h_ready"], 1)
                        if par == 0:
                            for q in range(2):
                                for tt in range(TT):
                                    last = place_gated(G2[:, tt, q * CAP:(q + 1) * CAP], tt, bass.ds(2 * pair + q, 1),
                                                       bass.ds(2 * pair + q, 1))
                            last.then_inc(s["G_built"], 1)
                        dve.wait_ge(s["ht_done"], e + 1)
                        w = 512 if par else 256
                        dve.tensor_copy(hTG[:, par, 0:w], GU[par][:, 0:w]).then_inc(s["ht_ready"], 1)
                        dve.wait_ge(s["down_done"], e + 1)
                        dve.tensor_copy(ys[CAP * par:CAP * par + CAP, 512:1024], YD[CAP:P, :]).then_inc(s["ys_ready"], 1)

                more = dve.value_load(flag[0:1, 0:1], min_val=0, max_val=T)
                with dve.If(more > CAP):
                    with dve.Fori(1, PASSES) as ps_:
                        with dve.Fori(0, NE) as ei:
                            it = (ps_ - 1) * NE + ei
                            dve.wait_ge(s["o_done"], it + 1)
                            for tt in range(TT):
                                place(Pb[:, 0, tt, :], tt, bass.ds(ps_ * NE + ei, 1))
                                last = place_gated(G2[:, tt, 0:CAP], tt, bass.ds(ps_ * NE + ei, 1), bass.ds(ei, 1))
                            last.then_inc(s["o_P"], 1)
                            dve.wait_ge(s["o_sg"], it + 1)
                            dve.tensor_tensor(hN[:, 0, :], GU[0][:, 256:512], sg[:, 0, :], ALU.mult).then_inc(s["o_h"], 1)
                            dve.wait_ge(s["o_ht"], it + 1)
                            dve.tensor_copy(hTG[:, 0, :], GU[0][:, :]).then_inc(s["o_htr"], 1)
                            dve.wait_ge(s["o_down"], it + 1)
                            dve.tensor_copy(ys[0:CAP, 512:1024], YD[CAP:P, :]).then_inc(s["o_ys"], 1)

            heads_norm(0, "a")
            layer_norm(0, "ya", lnpA)
            experts(0)
            layer_norm(1, "y0", oN)

            xT_half(2)
            dve.wait_ge(ld_att, 16 * 4)
            step(dve.tensor_tensor(lp, lam[:, 0:4:2, :], lam[:, 1:4:2, :], ALU.mult))
            dve.tensor_reduce(lam2, lp, AX_X, ALU.add).then_inc(Sm["lam_sum"], 1)
            wait_full(dve, "brow")
            dve.memset(brow[0:HB, T:REV], MASKED)
            step(dve.tensor_copy(brow[0:HB, 0:T], ps("brow")[0:HB, 0:T]))
            dve.sem_inc(free[where["brow", 0][0]], 1)
            dve.sem_inc(Sm["brow_ready"], 1)
            dve.wait_ge(Sm["lam_exp"], 1)
            step(dve.scalar_tensor_tensor(lamv, lam2[:, 1:2], LAMBDA_INIT, lam2[:, 0:1], ALU.subtract, ALU.subtract))
            for h in range(HB):
                wait_full(dve, "k", h)
                emptied(dve.tensor_copy(kT[:, h, :], ps("k", h)[:, 0:T]), "k", h)

            def difference(i):
                b, w = i % 2, (i // 8 + 1) * P
                dve.wait_ge(Sm["p_ready"], i + 1)
                step(dve.reciprocal(srec[:, b, :], ssum[:, b, :]))
                step(dve.tensor_tensor(srec[:, b, 1:2], srec[:, b, 1:2], lamv, ALU.mult))
                if i >= 2:
                    wait_full(dve, "atT", i - 2)
                step(dve.tensor_scalar(at[:, b, 0:w], pa[:, b, 0:w], srec[:, b, 0:1], None, ALU.mult))
                dve.scalar_tensor_tensor(at[:, b, 0:w], pa[:, b, T:T + w], srec[:, b, 1:2], at[:, b, 0:w], ALU.mult, ALU.add)\
                    .then_inc(Sm["at_ready"], 1)

            for i in range(4):
                wait_full(dve, "bias", i)
                emptied(dve.tensor_copy(bias[:, 2 * i:2 * i + 2, :], ps("bias", i).rearrange("p (a b) -> p a b", a=2)), "bias", i)
            wait_emptied(dve, "bias", 3)
            for i in range(16):
                qt, h = i // 8, i % 8
                b, w = i % 2, (qt + 1) * P
                wait_full(dve, "sc", i)
                s3 = sc[:, b, :].rearrange("p (a b) -> p a b", a=2)[:, :, 0:w]
                emptied(dve.tensor_tensor(s3, ps("sc", i).rearrange("p (a b) -> p a b", a=2)[:, :, 0:w],
                                          bias[:, h, T - w:T].unsqueeze(1).to_broadcast([P, 2, w]), ALU.add), "sc", i)
                wait_emptied(dve, "sc", i)
                dve.tensor_reduce(smx[:, b, :], s3, AX_X, ALU.max, negate=True).then_inc(Sm["sc_ready"], 1)
                if i >= 1:
                    difference(i - 1)
            difference(15)
            heads_norm(1, "b")
            layer_norm(2, "yb", lnpA)
            experts(1)
            layer_norm(3, "y1", oN)

        @block.gpsimd
        def _(pool):
            def step(ins):
                in_step(pool, ins, pool_step)

            def four_of(v):
                return v.unsqueeze(1).to_broadcast([P, 4, P])

            def load_lnp(dst, l, k):
                pool.dma_start(dst[:, 0, :], ln_w[l, k:k + 1, :].to_broadcast([P, D])).then_inc(ld_lnp, 16)
                pool.dma_start(dst[:, 1, :], ln_b[l, k:k + 1, :].to_broadcast([P, D])).then_inc(ld_lnp, 16)

            def layer_norm(r, lnp):
                for tt in range(TT):
                    pool.wait_ge(Sm["ln_scaled"], 2 * r + tt + 1)
                    pool.tensor_tensor(xN[:, tt, :], xN[:, tt, :], lnp[:, 1, :], ALU.add).then_inc(Sm["x_ready"], 1)

            pool.wait_ge(ld_cst, 16)
            for i in range(4):
                pool.wait_ge(Sm["dm_exp"], i + 1)
                d = Dm[:, 4 * i:4 * i + 4, :]
                pool.tensor_tensor(d, d, four_of(low), ALU.mult).then_inc(Sm["dm_ready"], 1)
            pool.wait_ge(Sm["dm_ready"], 4)
            pool.wait_ge(Sm["beta_ready"], 1)
            pool.wait_ge(Sm["silu_done"], 24)
            for b in range(4):
                m4 = Nm[:, 4 * b:4 * b + 4, :]
                nb4 = nb[:, b // 2, 4 * (b % 2):4 * (b % 2) + 4].unsqueeze(2).to_broadcast([P, 4, P])
                step(pool.tensor_tensor(m4, Dm[:, 4 * b:4 * b + 4, :], nb4, ALU.mult))
                pool.tensor_tensor(m4, m4, four_of(lows), ALU.mult).then_inc(Sm["nb_ready"], 1)
            pool.wait_ge(ld_par, 16 * 5)
            for i in range(4):
                wait_emptied(pool, "zz", i)
            for tt in range(TT):
                z3 = z[:, tt, :].rearrange("p (a b) -> p a b", a=8)
                last = pool.tensor_tensor(z3, z3, nw.unsqueeze(1).to_broadcast([P, 8, P]), ALU.mult)
            last.then_inc(Sm["z_ready"], 1)
            for i in range(4):
                wait_full(pool, "vtr", i)
            for b in range(4):
                wait_emptied(pool, "kk", b)
                t4 = Ti[:, 4 * b:4 * b + 4, :]
                step(pool.tensor_tensor(t4, Nm[:, 4 * b:4 * b + 4, :], four_of(mask(C_LEV)), ALU.mult))
                pool.tensor_tensor(t4, t4, four_of(ident), ALU.add).then_inc(Sm["T_init"], 1)
            for lev in range(1, 7):
                for b in range(4):
                    wait_full(pool, f"p{lev - 1}" if lev > 1 else "dtr", b)
                    pool.tensor_tensor(Dm[:, 4 * b:4 * b + 4, :], Nm[:, 4 * b:4 * b + 4, :], four_of(mask(C_LEV + lev)),
                                       ALU.mult).then_inc(Sm["L_ready"], 1)
            pool.wait_ge(Sm["L_ready"], 24)
            load_lnp(lnpA, 0, 0)
            layer_norm(0, lnpA)
            load_lnp(oN, 0, 1)
            layer_norm(1, oN)

            pool.memset(view(4096, HB * 2 * T), 0.0).then_inc(Sm["qz_zero"], 1)
            pool.wait_ge(ld_att, 16 * 4)
            pool.tensor_scalar(nwB, nwB, 1.0 - LAMBDA_INIT, None, ALU.mult).then_inc(Sm["nwB_ready"], 1)
            load_lnp(lnpA, 1, 0)
            pool.wait_ge(Sm["brow_ready"], 1)
            pool.dma_start(bias_rows, brow[0:HB, :]).then_inc(st_bias, 16)
            pool.wait_ge(st_bias, 16)
            pool.dma_start(braw[:, :, :], bass.AP(bias_rows.tensor, 0, [[1, P], [REV, HB], [1, T]])).then_inc(ld_bias, 16)
            layer_norm(2, lnpA)
            load_lnp(oN, 1, 1)
            layer_norm(3, oN)


_INS = ["x", "a_w_in", "a_conv", "a_A_log", "a_dt_bias", "a_norm_w", "a_w_out", "b_w_q", "b_w_kv", "b_lambda",
        "b_subln_w", "b_w_out", "rel_bias", "router_w", "router_b", "moe_w_gate", "moe_w_up", "moe_w_down", "ln_w", "ln_b"]


def kernel(**inputs):
    import concourse.bacc as bacc
    from concourse.bass_utils import run_bass_kernel_spmd

    nc = bacc.Bacc("TRN2", target_bir_lowering=False, num_devices=1)
    arrays, args = {}, []
    for name in _INS:
        arrays[f"in_{name}"] = np.ascontiguousarray(inputs[name])
    arrays["in_consts"] = constants()
    arrays["in_buckets"] = bucket_rows()
    for name, a in arrays.items():
        args.append(nc.dram_tensor(name, a.shape, mybir.dt.from_np(a.dtype), kind="ExternalInput").ap())
    args.append(nc.dram_tensor("bias_rows", [HB, REV], F32, kind="Internal").ap())
    args.append(nc.dram_tensor("out_0", (1, T, D), F32, kind="ExternalOutput").ap())
    build(nc, *args)
    r = run_bass_kernel_spmd(nc, [arrays], core_ids=[0])
    return r.results[0]["out_0"]
```

```python
from contextlib import ExitStack
import math

import numpy as np

import concourse.bass as bass
from concourse import mybir

F32 = mybir.dt.float32
I32 = mybir.dt.int32
ACT = mybir.ActivationFunctionType
ALU = mybir.AluOpType
AX_X = mybir.AxisListType.X

P = 128
T = 256
TT = T // P
D = 1024
KC = D // P
HA = 8
HB = 8
DH = 64
TAPS = 4
NE = 16
GRP = 4
FE = 512
CAP = 64
PASSES = T // CAP
DEPTH = 2
ALPHA = (2 * DEPTH) ** 0.25
LN_EPS = 1e-5
RMS_EPS = 1e-6
LAMBDA_INIT = 0.8 - 0.6 * math.exp(-0.3)
BUCKETS = 32
MAX_DIST = 128
REV = 384
MASKED = -1e30

SLOT = 4096
RING = 6
BASE_A = 0
BASE_M0 = BASE_A + 10
BASE_B = BASE_M0 + 3 * (NE - 1)
EMPTY = BASE_B + 8
BASE_M1 = EMPTY + 1

C_ID, C_ONE, C_TRI, C_TRIS, C_LOW, C_LOWS, C_LEV, C_ALPHA = 0, 1, 2, 3, 4, 5, 6, 13
C_REV = 14
C_IOTA = 15 * P
C_W4 = C_IOTA + CAP
C_COLS = C_W4 + GRP


def constants():
    i = np.arange(P)
    r, c = i[:, None], i[None, :]
    out = np.zeros((P, C_COLS), np.float32)

    def put(k, m):
        out[:, k * P:(k + 1) * P] = m

    put(C_ID, r == c)
    put(C_ONE, 1.0)
    put(C_TRI, r <= c)
    put(C_TRIS, r < c)
    put(C_LOW, r >= c)
    put(C_LOWS, r > c)
    for n in range(7):
        s = 1 << n
        put(C_LEV + n, (r // (2 * s) == c // (2 * s)) & (r // s % 2 == 1) & (c // s % 2 == 0))
    put(C_ALPHA, ALPHA * (r == c))
    put(C_REV, r + c == P - 1)
    out[:, C_IOTA:C_IOTA + CAP] = np.arange(CAP)
    out[:, C_W4:C_W4 + GRP] = GRP - np.arange(GRP)
    return out


def bucket_rows():
    out = np.zeros((BUCKETS, REV), np.float32)
    half = BUCKETS // 2
    for m in range(T):
        n = T - 1 - m
        b = n if n < half else min(BUCKETS - 1, half + int(
            np.float32(np.log(np.float32(n) / np.float32(half)) / math.log(MAX_DIST / half) * (BUCKETS - half))))
        out[b, m] = 1.0
    return out


def build(nc, x, a_w_in, a_conv, a_A_log, a_dt_bias, a_norm_w, a_w_out, b_w_q, b_w_kv, b_lambda, b_subln_w,
          b_w_out, rel_bias, router_w, router_b, moe_w_gate, moe_w_up, moe_w_down, ln_w, ln_b, consts, buckets,
          bias_rows, out):
    with ExitStack() as ctx:
        def sb(name, shape, dt=F32):
            return ctx.enter_context(nc.sbuf_tensor(name, shape, dt))

        def sem(name):
            return ctx.enter_context(nc.semaphore(name))

        ring = sb("ring", [P, RING, SLOT])
        xN = sb("xN", [P, TT, D])
        xT = sb("xT", [P, KC, T])
        oN = sb("oN", [P, TT, D])
        cst = sb("cst", [P, C_COLS])
        arena = sb("arena", [P, 19456])
        small = sb("small", [P, 768])
        flag = sb("flag", [P, 1], I32)

        def mask(k):
            return cst[:, k * P:(k + 1) * P]

        ident, ones, tri, tris, low, lows, alphaI = (mask(k) for k in (C_ID, C_ONE, C_TRI, C_TRIS, C_LOW, C_LOWS, C_ALPHA))
        reverse = mask(C_REV)
        iota = cst[:, C_IOTA:C_IOTA + CAP]
        w4 = cst[:, C_W4:C_W4 + GRP]

        taken = [0]

        def tiny(*shape):
            n = int(np.prod(shape))
            v = small[:, taken[0]:taken[0] + n]
            taken[0] += n
            assert taken[0] <= 768
            if len(shape) == 2:
                v = v.rearrange("p (a b) -> p a b", a=shape[0])
            if len(shape) == 3:
                v = v.rearrange("p (a b c) -> p a b c", a=shape[0], b=shape[1])
            return v

        def view(at, *shape):
            n = int(np.prod(shape))
            v = arena[:, at:at + n]
            if len(shape) == 2:
                v = v.rearrange("p (a b) -> p a b", a=shape[0])
            if len(shape) == 3:
                v = v.rearrange("p (a b c) -> p a b c", a=shape[0], b=shape[1])
            return v

        qkT = view(0, 16, T)
        vN = view(4096, TT, D)
        kN = view(6144, HA, P)
        z = view(7168, TT, D)
        Dm = view(9216, 16, P)
        Nm = view(11264, 16, P)
        QK = view(13312, 16, P)
        Ti = view(15360, 16, P)
        TiT = view(17408, 16, P)
        conv = view(13568, 4, T)
        vT = oN[:, :, :].rearrange("p a (b c) -> p (a b) c", b=4)
        sq = view(6144, 4, T)
        PT = xT[:, :, :].rearrange("p a (b c) -> p (a b) c", b=2)
        S = view(15360, HA, P)
        qS = view(16384, HA, P)
        oT = view(9216, KC, T)
        lnpA = view(4096, 2, D)

        kT = view(0, HB, T)
        vB = view(2048, TT, D)
        qz = view(4096, HB, 2, T)
        bias = view(8192, HB, T)
        braw = view(13312, HB, T)
        sc = view(10240, 2, 2 * T)
        pa = view(11264, 2, 2 * T)
        at = view(12288, 2, T)
        atT = view(12800, 2, TT, P)
        brow = view(10240, REV)
        oh = view(10624, REV)
        rbT = view(11008, HB)
        lam = view(11016, 4, DH)
        lp = view(11272, 2, DH)

        xeT = view(0, KC, 2 * CAP)
        xo = view(0, KC, CAP)
        sg = view(1024, 2, 256)
        hN = view(1536, 2, 256)
        hTG = view(2048, 2, 512)
        ys = view(3072, D)
        Pb = view(4096, TT, 2 * CAP)
        G2 = view(4352, TT, P)
        RK = view(4608, TT, NE * PASSES + 2)
        gate = view(4740, TT, NE + 2)
        rt = view(4800, 1024)
        ovw = view(7168, 3, SLOT)

        cw = tiny(TAPS * 24)
        wab = view(13312, KC, 16)
        cwr = view(13440, P)
        ab = tiny(TT, 16)
        alog = tiny(8)
        dtb = tiny(8)
        g = tiny(TT, HA)
        beta = tiny(TT, HA)
        gt1 = tiny(TT, HA)
        gt2 = tiny(TT, HA)
        gc = tiny(TT, HA)
        eg = tiny(TT, HA)
        kd = tiny(TT, HA)
        r2 = tiny(TT, 2 * HA)
        fq = tiny(TT, HA)
        bk = tiny(TT, HA)
        nb = tiny(TT, HA)
        nbe = tiny(TT, HA)
        ms = tiny(TT, HA)
        msB = tiny(2, 8)
        nw = tiny(P)
        nwB = nw
        st6 = tiny(TT, 2, 6)
        mv = tiny(TT, 2)
        rstd = tiny(TT)
        nmr = tiny(TT)
        rw = sb("rw", [P, KC, NE])
        rb = tiny(NE)
        lam2 = tiny(2)
        lamv = tiny(1)
        smx = tiny(2, 2)
        ssum = tiny(2, 2)
        srec = tiny(2, 2)

        bank = [ctx.enter_context(nc.psum_tensor(f"bank{b}", [P, 512], F32)) for b in range(8)]
        Y = bank[0:4]
        GU, XG, YD = bank[4:6], bank[6], bank[7]

        order = []

        def fill(name, n, banks):
            order.extend((name, i, banks[i % len(banks)]) for i in range(n))

        four, low4 = (4, 5, 6, 7), (0, 1, 2, 3)
        fill("xT0", 4, four)
        fill("cw", 1, (4,))
        fill("qk", 4, low4)
        fill("ab", 1, (5,))
        order.append(("ssq", 0, 7))
        order.extend(("qk", i, i % 4) for i in range(4, 8))
        fill("cum", 1, (6,))
        fill("grow", 4, (4, 5, 6, 4))
        fill("qk2", 8, low4)
        fill("vch", 8, low4)
        fill("kk", 4, (5, 6, 4, 5))
        fill("zz", 4, low4)
        fill("ttr", 4, (6, 7, 4, 5))
        fill("vtr", 4, (6, 7, 4, 5))
        fill("dtr", 4, (6, 7, 4, 5))
        fill("kq", 4, (6, 7, 4, 5))
        fill("ktr", 2, (6, 7))
        for lev in range(1, 7):
            fill(f"p{lev}", 4, (0, 1, 4, 5))
            if lev < 6:
                fill(f"t{lev}", 4, (2, 6))
            fill(f"tt{lev}", 4, (3, 7))
        fill("vn0", 2, (6, 7))
        fill("o0", 2, (4, 5))
        fill("s1", 2, (6, 7))
        fill("ks", 2, (4, 5))
        fill("qs", 2, (6, 7))
        fill("vn1", 2, (4, 5))
        fill("o1", 2, (6, 7))
        fill("oTa", 4, four)
        fill("ya", 4, low4)
        fill("xT1", 4, four)
        fill("lg0", 1, (4,))
        fill("rk0", 1, (5,))
        fill("y0", 4, low4)
        fill("xT2", 4, four)
        fill("brow", 1, (4,))
        fill("q", 4, (5, 6, 7, 0))
        fill("k", 4, (1, 2, 3, 5))
        fill("v", 2, (6, 7))
        fill("bias", 4, (4, 5, 6, 7))
        ITEMS = 2 * HB
        for k in range(ITEMS + 2):
            if k < ITEMS:
                order.append(("sc", k, 4 + k % 2))
            if k < 8:
                order.append(("q2" if k % 2 == 0 else "k2", k // 2, k % 4))
            elif k < 10:
                order.append(("v2", k - 8, k % 4))
            elif k == 10:
                fill("yb", 4, low4)
            elif k == 12:
                fill("oTb", 2, (6, 7))
            if 1 <= k <= ITEMS:
                order.append(("atT", k - 1, 6))
            if k >= 2:
                order.append(("av", k - 2, 7))
        order.append(("oTb", 2, 4))
        order.append(("oTb", 3, 5))
        fill("xT3", 4, four)
        fill("lg1", 1, (4,))
        fill("rk1", 1, (5,))
        fill("y1", 4, low4)
        where, per_bank = {}, [0] * 8
        for name, i, b in order:
            where[name, i] = (b, per_bank[b])
            per_bank[b] += 1
        full = [sem(f"bank{b}_full") for b in range(8)]
        free = [sem(f"bank{b}_free") for b in range(8)]

        def ps(name, i=0):
            return bank[where[name, i][0]]

        def before_fill(eng, name, i=0):
            b, k = where[name, i]
            if k:
                eng.wait_ge(free[b], k)

        def filled(ins, name, i=0):
            ins.then_inc(full[where[name, i][0]], 1)

        def wait_full(eng, name, i=0):
            b, k = where[name, i]
            eng.wait_ge(full[b], k + 1)

        def emptied(ins, name, i=0):
            ins.then_inc(free[where[name, i][0]], 1)

        def wait_emptied(eng, name, i=0):
            b, k = where[name, i]
            eng.wait_ge(free[b], k + 1)

        ld_x, ld_cst, ld_cw, ld_ab, ld_par = (sem(n) for n in ("ld_x", "ld_cst", "ld_cw", "ld_ab", "ld_par"))
        ld_att, ld_lnp, ld_bias, st_bias, st_out = (sem(n) for n in ("ld_att", "ld_lnp", "ld_bias", "st_bias", "st_out"))
        ld_first_gu, ld_first_down = sem("ld_first_gu"), sem("ld_first_down")
        ring_loaded = [sem(f"ring{s}_loaded") for s in range(RING)]
        dve_step, act_step, pool_step = sem("dve_step"), sem("act_step"), sem("pool_step")
        names = """gate_abs softplus_done gates_ready decay_in decay_ready dm_exp dm_ready silu_done
            sq_ready sq_used norm_in norm_root scales_ready z_ready nb_ready T_init L_ready r1_ready o_squared o_mean o_root o_scale o_normed
            ln_var ln_root ln_scale ln_normed ln_scaled x_ready logits_ready exp_done sel_ready flag_ready
            brow_ready sc_ready p_ready at_ready lam_sum lam_exp lam_ready qz_zero nwB_ready""".split()
        Sm = {n: sem(n) for n in names}

        moe_sems = [{n: sem(f"moe{layer}_{n}") for n in """P_built G_built gathered xe_ready gu_done sg_ready h_ready ht_done
            ht_ready down_done ys_ready scattered o_P o_gathered o_xe o_loaded o_gu o_sg o_h o_ht o_htr o_down o_ys
            o_done""".split()} for layer in range(DEPTH)]

        def signal(ins, name):
            ins.then_inc(Sm[name], 1)

        counts = {}

        def in_step(eng, ins, s):
            counts[s.name] = counts.get(s.name, 0) + 1
            ins.then_inc(s, 1)
            eng.wait_ge(s, counts[s.name])

        def loads(n):
            return 16 * (n // RING + 1) - (16 if n > EMPTY and n % RING == EMPTY % RING else 0)

        def after_load(eng, n):
            eng.wait_ge(ring_loaded[n % RING], loads(n))

        def gate_at(e):
            return 3 * e - 4 if e > 1 else 0

        def down_at(e):
            return 3 * e + 1 if e < NE - 1 else 3 * NE - 4

        def slot(n):
            return ring[:, n % RING, :].rearrange("p (k n) -> p k n", k=KC)

        def w_cols(w, c):
            return w[:, c:c + 512].rearrange("(k p) n -> p k n", p=P)

        block = ctx.enter_context(nc.Block())

        @block.sync
        def _(sp):
            def wait_released(n):
                if n < BASE_M0:
                    n -= BASE_A
                    last = (("qk", 4 * n + 3) if n < 2 else ("qk2", 4 * n - 5) if n < 4 else ("vch", 4 * n - 13) if n < 6
                            else ("zz", 2 * n - 11) if n < 8 else ("ya", n - 6))
                    wait_full(sp, *last)
                elif n == EMPTY:
                    wait_released(n - RING)
                elif n < BASE_B or n >= BASE_M1:
                    layer, base = (0, BASE_M0) if n < BASE_B else (1, BASE_M1)
                    for e in range(1, NE):
                        if n - base in (gate_at(e), gate_at(e) + 1):
                            sp.wait_ge(moe_sems[layer]["gu_done"], e + 1)
                        if n - base == down_at(e):
                            sp.wait_ge(moe_sems[layer]["down_done"], e + 1)
                else:
                    n -= BASE_B
                    last = (("q", 3), ("k", 3), ("v", 1), ("q2", 3), ("k2", 3), ("v2", 1), ("yb", 2), ("yb", 3))[n]
                    wait_full(sp, *last)

            def stream(n, src):
                if n >= RING:
                    wait_released(n - RING)
                sp.dma_start(slot(n), src).then_inc(ring_loaded[n % RING], 16)

            sp.dma_start(xN[:, :, :], x[0].rearrange("(t p) d -> p t d", p=P)).then_inc(ld_x, 16)
            for n in range(8):
                stream(BASE_A + n, w_cols(a_w_in[0], 512 * n))
            for n in range(2):
                stream(BASE_A + 8 + n, w_cols(a_w_out[0], 512 * n))

            def expert_load(layer, n, e, part):
                w = (moe_w_gate, moe_w_up, moe_w_down)[part]
                src = w[layer, bass.ds(e, 1)].rearrange("o (k p) n -> p (o k) n", p=P)
                dst = ring[:, n % RING, :].rearrange("p (k n) -> p k n", k=(KC, KC, FE // P)[part])
                sp.dma_start(dst, src).then_inc(ring_loaded[n % RING], 16)

            def experts(layer, base):
                s = moe_sems[layer]

                def first_use(e, part):
                    n = base + (gate_at(e) + part if part < 2 else down_at(e))
                    wait_released(n - RING)
                    expert_load(layer, n, e, part)

                def first_expert(part, at_, signal_):
                    w = (moe_w_gate, moe_w_up, moe_w_down)[part]
                    sp.dma_start(ovw[:, at_, :].rearrange("p (k n) -> p k n", k=(KC, KC, FE // P)[part]),
                                 w[layer, 0].rearrange("(k p) n -> p k n", p=P)).then_inc(signal_, 16)

                first_use(1, 0)
                first_use(1, 1)
                if layer == 0:
                    first_use(2, 0)
                    first_use(2, 1)
                    wait_full(sp, "o1", 0)
                    wait_full(sp, "o1", 1)
                    wait_emptied(sp, "o1", 0)
                    wait_emptied(sp, "o1", 1)
                else:
                    first_use(2, 0)
                    wait_full(sp, "av", 15)
                first_expert(0, 1, ld_first_gu)
                first_expert(1, 2, ld_first_gu)
                if layer == 0:
                    for i in range(4):
                        wait_full(sp, "ya", i)
                    sp.wait_ge(Sm["o_normed"], TT)
                first_expert(2, 0, ld_first_down)
                if layer == 1:
                    first_use(2, 1)
                first_use(1, 2)
                with sp.Fori(1, NE // 2 - 1) as pair:
                    for j in range(2):
                        e = 2 * pair + 1 + j
                        n = base + gate_at(3 + j)
                        for part in range(2):
                            sp.wait_ge(s["gu_done"], e - 1)
                            expert_load(layer, n + part, e, part)
                        sp.wait_ge(s["down_done"], e - 2)
                        expert_load(layer, n + 2, e - 1, 2)
                first_use(NE - 1, 0)
                first_use(NE - 1, 1)
                first_use(NE - 2, 2)
                first_use(NE - 1, 2)

            experts(0, BASE_M0)
            for half in range(2):
                stream(BASE_B + 3 * half, w_cols(b_w_q[0], 512 * half))
                stream(BASE_B + 3 * half + 1, w_cols(b_w_kv, 512 * half))
                stream(BASE_B + 3 * half + 2, w_cols(b_w_kv, 1024 + 512 * half))
            for n in range(2):
                stream(BASE_B + 6 + n, w_cols(b_w_out[0], 512 * n))
            experts(1, BASE_M1)
            sp.wait_ge(Sm["x_ready"], 4 * TT)
            sp.dma_start(out[0].rearrange("(t p) d -> p t d", p=P), xN[:, :, :]).then_inc(st_out, 16)
            sp.wait_ge(st_out, 16)

        @block.tensor
        def _(pe):
            def transposes(name, i, parts):
                before_fill(pe, name, i)
                for j, src in enumerate(parts):
                    last = pe.transpose(ps(name, i)[:, j * P:(j + 1) * P], src, ident)
                filled(last, name, i)

            def transpose_x(r):
                for i in range(4):
                    transposes(f"xT{r}", i, [xN[:, tt, kc * P:(kc + 1) * P] for kc in (2 * i, 2 * i + 1) for tt in range(TT)])

            def xT_made(r):
                for i in range(4):
                    wait_emptied(pe, f"xT{r}", i)

            def columns(name, i, n, ct):
                before_fill(pe, name, i)
                for kc in range(KC):
                    last = pe.matmul(ps(name, i)[:, 0:T], slot(n)[:, kc, ct * P:(ct + 1) * P], xT[:, kc, :],
                                     start=kc == 0, stop=kc == KC - 1)
                filled(last, name, i)
                return last

            def rows(name, i, n, tt):
                before_fill(pe, name, i)
                for kc in range(KC):
                    last = pe.matmul(ps(name, i)[:, :], xT[:, kc, tt * P:(tt + 1) * P], slot(n)[:, kc, :],
                                     start=kc == 0, stop=kc == KC - 1)
                filled(last, name, i)
                return last

            pe.wait_ge(ld_x, 16)
            pe.wait_ge(ld_cst, 16)
            transpose_x(0)
            pe.wait_ge(ld_cw, 16)
            before_fill(pe, "cw")
            filled(pe.transpose(ps("cw")[:, 0:96], cwr[0:96, :], ident[0:96, 0:96]), "cw")
            xT_made(0)

            def ssq(t):
                pe.wait_ge(Sm["sq_ready"], t + 1)
                for tt in range(TT):
                    at_ = 16 * tt + t
                    last = pe.matmul(ps("ssq")[:, at_:at_ + 1], sq[:, t % 4, tt * P:(tt + 1) * P], ones[:, 0:1],
                                     start=True, stop=True)
                last.then_inc(Sm["sq_used"], 1)

            after_load(pe, 0)
            for ct in range(4):
                columns("qk", ct, 0, ct)
                if ct >= 2:
                    ssq(ct - 2)
            pe.wait_ge(ld_ab, 16)
            before_fill(pe, "ab")
            for tt in range(TT):
                for kc in range(KC):
                    last = pe.matmul(ps("ab")[:, tt * 16:(tt + 1) * 16], xT[:, kc, tt * P:(tt + 1) * P], wab[:, kc, :],
                                     start=kc == 0, stop=kc == KC - 1)
            filled(last, "ab")
            after_load(pe, 1)
            for ct in range(4):
                columns("qk", 4 + ct, 1, ct)
                ssq(2 + ct)
            pe.wait_ge(Sm["gates_ready"], 1)
            before_fill(pe, "cum")
            gall = g[:, :, :].rearrange("p a b -> p (a b)")
            pe.matmul(ps("cum")[:, 0:16], tri, gall, start=True, stop=True)
            filled(pe.matmul(ps("cum")[:, 16:32], ones, gall, start=True, stop=True), "cum")
            for i in range(4):
                before_fill(pe, "grow", i)
                for j in range(4):
                    ch = 4 * i + j
                    last = pe.matmul(ps("grow", i)[:, j * P:(j + 1) * P], gall[:, ch:ch + 1].to_broadcast([P, P]), tri,
                                     start=True, stop=True)
                filled(last, "grow", i)
            for n in range(2, 4):
                after_load(pe, n)
                for ct in range(4):
                    columns("qk2", 4 * (n % 2) + ct, n, ct)
                    ssq(4 * n - 2 + ct)

            def raw_products(name, q0, b):
                before_fill(pe, name, b)
                for j in range(4):
                    h, t0 = 4 * (b % 2) + j, (b // 2) * P
                    last = pe.matmul(ps(name, b)[:, j * P:(j + 1) * P], qkT[:, 8 + h, t0:t0 + P],
                                     qkT[:, q0 + h, t0:t0 + P], start=True, stop=True)
                filled(last, name, b)

            for t in range(8):
                n = 4 + t // 4
                after_load(pe, n)
                columns("vch", t, n, t % 4)
                if t < 2:
                    ssq(14 + t)
                    if t == 1:
                        pe.wait_ge(Sm["sq_used"], 16)
                        pe.sem_inc(full[where["ssq", 0][0]], 1)
                elif t in (4, 5):
                    raw_products("kk", 8, 2 * (t - 4))
                    raw_products("kk", 8, 2 * (t - 4) + 1)

            def turn_T(b):
                pe.wait_ge(Sm["T_init"], b + 1)
                transposes("ttr", b, [Ti[:, 4 * b + j, :] for j in range(4)])

            def turn_v(i):
                tt, hg = i // 2, i % 2
                pe.wait_ge(Sm["silu_done"], 24)
                transposes("vtr", i, [vT[:, 4 * hg + j, tt * P:(tt + 1) * P] for j in range(4)])

            for i in range(4):
                n, tt = 6 + i // 2, i % 2
                after_load(pe, n)
                rows("zz", i, n, tt)
                if i == 0:
                    for b in range(4):
                        turn_T(b)
                elif i == 1:
                    for b in range(4):
                        turn_v(b)
                elif i == 2:
                    pe.wait_ge(Sm["dm_ready"], 4)
                    for b in range(4):
                        transposes("dtr", b, [Dm[:, 4 * b + j, :] for j in range(4)])
            for b in range(4):
                raw_products("kq", 0, b)
            for i in range(2):
                transposes("ktr", i, [qkT[:, 8 + 4 * i + j, 0:P] for j in range(4)])
            for lev in range(1, 7):
                for b in range(4):
                    pe.wait_ge(Sm["L_ready"], 4 * (lev - 1) + b + 1)
                    wait_emptied(pe, f"tt{lev - 1}" if lev > 1 else "ttr", b)
                    before_fill(pe, f"p{lev}", b)
                    for j in range(4):
                        m = 4 * b + j
                        last = pe.matmul(ps(f"p{lev}", b)[:, j * P:(j + 1) * P], Dm[:, m, :], TiT[:, m, :],
                                         start=True, stop=True)
                    filled(last, f"p{lev}", b)
                for b in range(4):
                    wait_emptied(pe, f"p{lev}", b)
                    if lev > 1:
                        wait_emptied(pe, f"t{lev - 1}", b)
                    if lev < 6:
                        before_fill(pe, f"t{lev}", b)
                        for j in range(4):
                            m = 4 * b + j
                            last = pe.matmul(ps(f"t{lev}", b)[:, j * P:(j + 1) * P], PT[:, m, :], Ti[:, m, :],
                                             start=True, stop=True)
                        filled(last, f"t{lev}", b)
                    before_fill(pe, f"tt{lev}", b)
                    for j in range(4):
                        m = 4 * b + j
                        last = pe.matmul(ps(f"tt{lev}", b)[:, j * P:(j + 1) * P], Ti[:, m, :], PT[:, m, :],
                                         start=True, stop=True)
                    filled(last, f"tt{lev}", b)

            def by_head(name, i, lhsT, rhs):
                before_fill(pe, name, i)
                for j in range(4):
                    h = 4 * i + j
                    last = pe.matmul(ps(name, i)[:, j * P:(j + 1) * P], lhsT(h), rhs(h), start=True, stop=True)
                filled(last, name, i)

            for b in range(4):
                wait_emptied(pe, "tt6", b)
                wait_emptied(pe, "kq", b)
                wait_emptied(pe, "vtr", b)
            for i in range(2):
                by_head("vn0", i, lambda h: TiT[:, h, :], lambda h: vN[:, 0, h * P:(h + 1) * P])
            for i in range(2):
                wait_emptied(pe, "vn0", i)
                wait_emptied(pe, "ktr", i)
                by_head("o0", i, lambda h: QK[:, h, :], lambda h: vN[:, 0, h * P:(h + 1) * P])
                by_head("s1", i, lambda h: kN[:, h, :], lambda h: vN[:, 0, h * P:(h + 1) * P])
            for i in range(2):
                wait_emptied(pe, "s1", i)
                by_head("ks", i, lambda h: qkT[:, 8 + h, P:T], lambda h: S[:, h, :])
                by_head("qs", i, lambda h: qkT[:, h, P:T], lambda h: S[:, h, :])
            for i in range(2):
                pe.wait_ge(Sm["r1_ready"], i + 1)
                by_head("vn1", i, lambda h: TiT[:, 8 + h, :], lambda h: vN[:, 1, h * P:(h + 1) * P])
            for i in range(2):
                wait_emptied(pe, "vn1", i)
                by_head("o1", i, lambda h: QK[:, 8 + h, :], lambda h: vN[:, 1, h * P:(h + 1) * P])

            def residual(name, alone=False):
                for i in range(4):
                    tt, n = i // 2, i % 2
                    before_fill(pe, name, i)
                    pe.matmul(ps(name, i)[:, :], alphaI, xN[:, tt, n * 512:(n + 1) * 512], start=True, stop=alone)

            def project_out(base, src, oname):
                residual(f"y{oname}")
                for i in range(4):
                    pe.wait_ge(Sm["o_normed"], 2)
                    transposes(f"oT{oname}", i, [oN[:, tt, kc * P:(kc + 1) * P] for kc in (2 * i, 2 * i + 1) for tt in range(TT)])
                for i in range(4):
                    wait_emptied(pe, f"oT{oname}", i)
                for n in range(2):
                    after_load(pe, base + n)
                    for tt in range(TT):
                        i = 2 * tt + n
                        for kc in range(KC):
                            last = pe.matmul(ps(f"y{oname}", i)[:, :], src[:, kc, tt * P:(tt + 1) * P],
                                             slot(base + n)[:, kc, :], start=False, stop=kc == KC - 1)
                        last.then_inc(full[where[f"y{oname}", i][0]], 1)

            project_out(BASE_A + 8, oT, "a")

            def route(layer):
                pe.wait_ge(Sm["x_ready"], (4 * layer + 2))
                transpose_x(1 + 2 * layer)
                xT_made(1 + 2 * layer)
                lg = f"lg{layer}"
                before_fill(pe, lg)
                for tt in range(TT):
                    for kc in range(KC):
                        last = pe.matmul(ps(lg)[:, tt * NE:(tt + 1) * NE], xT[:, kc, tt * P:(tt + 1) * P], rw[:, kc, :],
                                         start=kc == 0, stop=kc == KC - 1)
                filled(last, lg)
                residual(f"y{layer}", alone=True)
                pe.wait_ge(Sm["sel_ready"], layer + 1)
                rk = f"rk{layer}"
                before_fill(pe, rk)
                sel = rt[:, 0:2 * NE]
                pe.matmul(ps(rk)[:, 0:NE], tris, sel[:, 0:NE], start=True, stop=True)
                pe.matmul(ps(rk)[:, NE:2 * NE], ones, sel[:, 0:NE], start=True, stop=False)
                pe.matmul(ps(rk)[:, NE:2 * NE], tris, sel[:, NE:2 * NE], start=False, stop=True)
                pe.matmul(ps(rk)[:, 2 * NE:3 * NE], ones, sel[:, 0:NE], start=True, stop=False)
                filled(pe.matmul(ps(rk)[:, 2 * NE:3 * NE], ones, sel[:, NE:2 * NE], start=False, stop=True), rk)

            def experts(layer, base):
                s = moe_sems[layer]

                def weights(n, pair):
                    pe.wait_ge(ring_loaded[n % RING], loads(n) + 16 * pair)

                def tokens(half):
                    for kc in range(4 * half, 4 * half + 4):
                        for tt in range(TT):
                            last = pe.matmul(XG[:, (kc % 4) * P:(kc % 4 + 1) * P], xN[:, tt, kc * P:(kc + 1) * P],
                                             Pb[:, tt, :], start=tt == 0, stop=tt == TT - 1)
                    last.then_inc(s["gathered"], 1)

                def gate_up(e, par, n, pair, own=False):
                    if par == 0:
                        pe.wait_ge(s["xe_ready"], e + 2)
                    if own:
                        pe.wait_ge(ld_first_gu, 32 * (layer + 1))
                        w = ovw[:, 1:3, :]
                    else:
                        weights(n, pair)
                        weights(n + 1, pair)
                        w = ring[:, n % RING:n % RING + 2, :]
                    w = w.rearrange("p s (k n) -> p s k n", k=KC)
                    for kc in range(KC):
                        for half in range(2):
                            last = pe.matmul(GU[par][64 * half:64 * half + 64, :], xeT[:, kc, par * CAP:(par + 1) * CAP],
                                             w[:, :, kc, 256 * half:256 * half + 256], start=kc == 0, stop=kc == KC - 1)
                    last.then_inc(s["gu_done"], 1)

                def turn_hidden(e, par, pair):
                    pe.wait_ge(s["h_ready"], e + 1)
                    for c in range(2):
                        last = pe.transpose(GU[par][:, c * P:(c + 1) * P], hN[:, par, c * P:(c + 1) * P], ident)
                    if par == 1:
                        pe.wait_ge(s["G_built"], pair + 1)
                        for tt in range(TT):
                            last = pe.transpose(GU[1][:, 256 + tt * P:256 + (tt + 1) * P], G2[:, tt, :], ident)
                    last.then_inc(s["ht_done"], 1)

                def down(e, par, n, pair, own=False):
                    pe.wait_ge(s["ht_ready"], e + 1)
                    if own:
                        pe.wait_ge(ld_first_down, 16 * (layer + 1))
                    else:
                        weights(n, pair)
                    dn = (ovw[:, 0, :] if own else ring[:, n % RING, :]).rearrange("p (k n) -> p k n", k=FE // P)
                    for fc in range(4):
                        lhs = hTG[:, par, (fc % 2) * P + (fc // 2) * CAP:(fc % 2) * P + (fc // 2) * CAP + CAP]
                        for c in range(2):
                            last = pe.matmul(YD[64 * c:64 * c + 64, :], lhs, dn[:, fc, c * 512:(c + 1) * 512],
                                             start=fc == 0, stop=fc == 3)
                    last.then_inc(s["down_done"], 1)

                def scatter(pair):
                    pe.wait_ge(s["ys_ready"], 4 * pair + 4)
                    for i in range(4):
                        tt, c = i // 2, i % 2
                        last = pe.matmul(Y[i][:, :], hTG[:, 1, 256 + tt * P:256 + (tt + 1) * P], ys[:, c * 512:(c + 1) * 512],
                                         start=False, stop=True, skip_group_check=True)
                    last.then_inc(s["scattered"], 1)

                def two_experts(pair, first=False, last=False):
                    a = 2 * pair
                    k, rounds = (a, 0) if last or first else (2, pair - 1)
                    gate_up(a + 1, 1, base + gate_at(k + 1), rounds)
                    turn_hidden(a, 0, pair)
                    if not last:
                        pe.wait_ge(s["P_built"], pair + 2)
                        tokens(0)
                    if not first:
                        scatter(pair - 1)
                    if not last:
                        pe.wait_ge(s["xe_ready"], a + 3)
                        tokens(1)
                    down(a, 0, base + down_at(k), rounds, own=first)
                    turn_hidden(a + 1, 1, pair)
                    if not last:
                        gate_up(a + 2, 0, base + gate_at(k + 2), rounds)
                    pe.wait_ge(s["ys_ready"], 4 * pair + 2)
                    down(a + 1, 1, base + down_at(k + 1), rounds)

                pe.wait_ge(s["P_built"], 1)
                tokens(0)
                wait_emptied(pe, f"rk{layer}")
                pe.wait_ge(s["xe_ready"], 1)
                tokens(1)
                gate_up(0, 0, base, 0, own=True)
                two_experts(0, first=True)
                with pe.Fori(1, NE // 2 - 1) as pair:
                    two_experts(pair)
                two_experts(NE // 2 - 1, last=True)
                scatter(NE // 2 - 1)
                pe.wait_ge(s["scattered"], NE // 2)

            def overflow(layer):
                s = moe_sems[layer]
                pe.wait_ge(Sm["flag_ready"], layer + 1)
                more = pe.value_load(flag[0:1, 0:1], min_val=0, max_val=T)
                with pe.If(more > CAP):
                    pe.sem_inc(s["o_done"], 1)
                    with pe.Fori(1, PASSES) as ps_:
                        with pe.Fori(0, NE) as ei:
                            it = (ps_ - 1) * NE + ei
                            pe.wait_ge(s["o_P"], it + 1)
                            for kc in range(KC):
                                for tt in range(TT):
                                    last = pe.matmul(XG[:, kc * CAP:(kc + 1) * CAP], xN[:, tt, kc * P:(kc + 1) * P],
                                                     Pb[:, tt, 0:CAP], start=tt == 0, stop=tt == TT - 1)
                            last.then_inc(s["o_gathered"], 1)
                            pe.wait_ge(s["o_xe"], it + 1)
                            pe.wait_ge(s["o_loaded"], 48 * it + 48)
                            wv = ovw[:, 1:3, :].rearrange("p s (k n) -> p s k n", k=KC)
                            for kc in range(KC):
                                for half in range(2):
                                    last = pe.matmul(GU[0][64 * half:64 * half + 64, :], xo[:, kc, :],
                                                     wv[:, :, kc, 256 * half:256 * half + 256], start=kc == 0, stop=kc == KC - 1)
                            last.then_inc(s["o_gu"], 1)
                            pe.wait_ge(s["o_h"], it + 1)
                            for c in range(2):
                                pe.transpose(GU[0][:, c * P:(c + 1) * P], hN[:, 0, c * P:(c + 1) * P], ident)
                            for tt in range(TT):
                                last = pe.transpose(GU[0][:, 256 + tt * P:256 + (tt + 1) * P], G2[:, tt, :], ident)
                            last.then_inc(s["o_ht"], 1)
                            pe.wait_ge(s["o_htr"], it + 1)
                            dn = ovw[:, 0, :].rearrange("p (k n) -> p k n", k=FE // P)
                            for fc in range(4):
                                lhs = hTG[:, 0, (fc % 2) * P + (fc // 2) * CAP:(fc % 2) * P + (fc // 2) * CAP + CAP]
                                for n in range(2):
                                    last = pe.matmul(YD[64 * n:64 * n + 64, :], lhs, dn[:, fc, n * 512:(n + 1) * 512],
                                                     start=fc == 0, stop=fc == 3)
                            last.then_inc(s["o_down"], 1)
                            pe.wait_ge(s["o_ys"], 2 * it + 2)
                            for i in range(4):
                                tt, n = i // 2, i % 2
                                last = pe.matmul(Y[i][:, :], hTG[0:CAP, 0, 256 + tt * P:256 + (tt + 1) * P],
                                                 ys[0:CAP, n * 512:(n + 1) * 512], start=False, stop=True,
                                                 skip_group_check=True)
                            last.then_inc(s["o_done"], 1)
                    pe.wait_ge(s["o_done"], NE * (PASSES - 1) + 1)
                for i in range(4):
                    pe.sem_inc(full[where[f"y{layer}", i][0]], 1)

            route(0)
            experts(0, BASE_M0)
            overflow(0)

            pe.wait_ge(Sm["x_ready"], 4)
            transpose_x(2)
            pe.wait_ge(ld_att, 16 * 4)
            before_fill(pe, "brow")
            filled(pe.matmul(ps("brow")[0:HB, 0:REV], rbT[0:BUCKETS, :], oh[0:BUCKETS, :], start=True, stop=True), "brow")
            xT_made(2)
            after_load(pe, BASE_B)
            for ct in range(4):
                columns("q", ct, BASE_B, ct)
            after_load(pe, BASE_B + 1)
            for ct in range(4):
                columns("k", ct, BASE_B + 1, ct)
            after_load(pe, BASE_B + 2)
            for tt in range(TT):
                rows("v", tt, BASE_B + 2, tt)
            pe.wait_ge(ld_bias, 16)
            for i in range(4):
                before_fill(pe, "bias", i)
                filled(pe.matmul(ps("bias", i)[:, :], reverse, braw[:, 2 * i:2 * i + 2, :], start=True, stop=True), "bias", i)

            def scores(i):
                h, qt = i // 2, i % 2
                before_fill(pe, "sc", i)
                if qt == 0:
                    wait_emptied(pe, "q" if h < 4 else "q2", h % 4)
                    wait_emptied(pe, "k" if h < 4 else "k2", h % 4)
                for half in range(2):
                    last = pe.matmul(ps("sc", i)[:, half * T:half * T + (qt + 1) * P], qz[:, h, half, qt * P:(qt + 1) * P],
                                     kT[:, h, 0:(qt + 1) * P], start=True, stop=True)
                filled(last, "sc", i)

            def turn_attention(i):
                qt = i % 2
                pe.wait_ge(Sm["at_ready"], i + 1)
                before_fill(pe, "atT", i)
                for kt in range(qt + 1):
                    last = pe.transpose(ps("atT", i)[:, kt * P:(kt + 1) * P], at[:, i % 2, kt * P:(kt + 1) * P], ident)
                filled(last, "atT", i)

            def values(i):
                h, qt = i // 2, i % 2
                wait_emptied(pe, "atT", i)
                if i == 0 or i == ITEMS // 2:
                    for tt in range(TT):
                        wait_emptied(pe, "v" if i == 0 else "v2", tt)
                before_fill(pe, "av", i)
                for kt in range(qt + 1):
                    last = pe.matmul(ps("av", i)[:, 0:P], atT[:, i % 2, kt, :], vB[:, kt, h * P:(h + 1) * P],
                                     start=kt == 0, stop=kt == qt)
                filled(last, "av", i)

            def turn_heads(i):
                pe.wait_ge(Sm["o_normed"], 3 + i // 2)
                transposes("oTb", i, [oN[:, tt, kc * P:(kc + 1) * P] for kc in (2 * i, 2 * i + 1) for tt in range(TT)])

            def half_out(i, half):
                tt, n = i // 2, i % 2
                after_load(pe, BASE_B + 6 + n)
                for j in (0, 1):
                    wait_emptied(pe, "oTb", 2 * half + j)
                for kc in range(4 * half, 4 * half + 4):
                    last = pe.matmul(ps("yb", i)[:, :], kT[:, kc, tt * P:(tt + 1) * P], slot(BASE_B + 6 + n)[:, kc, :],
                                     start=False, stop=kc == KC - 1)
                if half:
                    last.then_inc(full[where["yb", i][0]], 1)

            for k in range(ITEMS + 2):
                if k < ITEMS:
                    scores(k)
                if k < 8 and k % 2 == 0:
                    after_load(pe, BASE_B + 3)
                    columns("q2", k // 2, BASE_B + 3, k // 2)
                elif k < 8:
                    after_load(pe, BASE_B + 4)
                    columns("k2", k // 2, BASE_B + 4, k // 2)
                elif k < 10:
                    after_load(pe, BASE_B + 5)
                    rows("v2", k - 8, BASE_B + 5, k - 8)
                elif k == 10:
                    residual("yb")
                elif k == 12:
                    for i in range(2):
                        turn_heads(i)
                elif 13 <= k < 17:
                    half_out(k - 13, 0)
                if 1 <= k <= ITEMS:
                    turn_attention(k - 1)
                if k >= 2:
                    values(k - 2)
            for i in (2, 3):
                turn_heads(i)
            for i in range(4):
                half_out(i, 1)
            route(1)
            experts(1, BASE_M1)
            overflow(1)

        @block.scalar
        def _(act):
            def go(out_, in_, f, **kw):
                return act.activation(out_, in_, f, **kw)

            act.dma_start(cst[:, :], consts).then_inc(ld_cst, 16)
            act.dma_start(cwr[0:96, :], a_conv[0].rearrange("i (t c) -> (i t) c", c=P)).then_inc(ld_cw, 16)
            act.dma_start(wab[:, :, :], a_w_in[0, :, 4096:4112].rearrange("(k p) n -> p k n", p=P)).then_inc(ld_ab, 16)
            for dst, src in ((alog, a_A_log), (dtb, a_dt_bias), (nw, a_norm_w)):
                act.dma_start(dst, src.to_broadcast([P, src.shape[1]])).then_inc(ld_par, 16)
            act.dma_start(rb, router_b.rearrange("(a n) -> a n", a=1).to_broadcast([P, NE])).then_inc(ld_par, 16)
            act.dma_start(rw[:, :, :], router_w.rearrange("(k p) n -> p k n", p=P)).then_inc(ld_par, 16)

            def xT_half(r):
                for i in (0, 2):
                    wait_full(act, f"xT{r}", i)
                    emptied(go(xT[:, 2 * i:2 * i + 2, :], ps(f"xT{r}", i).rearrange("p (a b) -> p a b", a=2), ACT.Copy),
                            f"xT{r}", i)

            xT_half(0)
            def silu(t):
                name = ("qk", "qk2", "vch")[t // 8]
                wait_emptied(act, name, t % 8)
                if t < 16:
                    go(qkT[:, t, :], conv[:, t % 4, :], ACT.Silu).then_inc(Sm["silu_done"], 1)
                    if t >= 4:
                        act.wait_ge(Sm["sq_used"], t - 3)
                    act.wait_ge(Sm["silu_done"], t + 1)
                    go(sq[:, t % 4, :], qkT[:, t, :], ACT.Square).then_inc(Sm["sq_ready"], 1)
                else:
                    go(vT[:, t - 16, :], conv[:, t % 4, :], ACT.Silu).then_inc(Sm["silu_done"], 1)

            for t in range(4):
                silu(t)
            act.wait_ge(Sm["gate_abs"], 1)
            in_step(act, go(gt2, gt2, ACT.Exp, scale=-1.0), act_step)
            act.wait_ge(ld_par, 16 * 5)
            go(alog, alog, ACT.Exp)
            go(beta, ab[:, :, HA:2 * HA], ACT.Exp, scale=-1.0)
            go(gt2, gt2, ACT.Ln, bias=1.0).then_inc(Sm["softplus_done"], 1)
            for t in range(4, 8):
                silu(t)
            act.wait_ge(Sm["decay_in"], 1)
            go(eg, gc, ACT.Exp)
            go(kd, kd, ACT.Exp).then_inc(Sm["decay_ready"], 1)
            for i in range(4):
                wait_emptied(act, "grow", i)
                d = Dm[:, 4 * i:4 * i + 4, :]
                go(d, d, ACT.Exp, scale=-1.0).then_inc(Sm["dm_exp"], 1)
            for t in range(8, 18):
                silu(t)
            act.wait_ge(Sm["norm_in"], 1)
            go(fq, r2[:, :, 0:HA], ACT.Sqrt, scale=1.0 / P)
            go(bk, r2[:, :, HA:2 * HA], ACT.Sqrt).then_inc(Sm["norm_root"], 1)
            for t in range(18, 24):
                silu(t)

            def silu_z(i):
                wait_full(act, "zz", i)
                emptied(go(z[:, i % 2, 512 * (i // 2):512 * (i // 2) + 512], ps("zz", i)[:, :], ACT.Silu), "zz", i)

            silu_z(0)
            for b in range(4):
                wait_full(act, "ttr", b)
                emptied(go(TiT[:, 4 * b:4 * b + 4, :], ps("ttr", b).rearrange("p (a b) -> p a b", a=4), ACT.Copy), "ttr", b)
            silu_z(1)
            silu_z(2)
            for b in range(4):
                wait_full(act, "dtr", b)
                emptied(go(QK[:, 4 * b:4 * b + 4, :], ps("dtr", b).rearrange("p (a b) -> p a b", a=4), ACT.Copy), "dtr", b)
            silu_z(3)
            for lev in range(1, 7):
                for b in range(4):
                    if lev > 1:
                        wait_full(act, f"tt{lev - 1}", b)
                    wait_full(act, f"p{lev}", b)
                    emptied(go(PT[:, 4 * b:4 * b + 4, :], ps(f"p{lev}", b).rearrange("p (a b) -> p a b", a=4), ACT.Copy),
                            f"p{lev}", b)
            for i in range(2):
                wait_full(act, "vn0", i)
                emptied(go(vN[:, 0, 512 * i:512 * i + 512], ps("vn0", i)[:, :], ACT.Copy), "vn0", i)
            for i in range(2):
                wait_full(act, "o0", i)
                emptied(go(oN[:, 0, 512 * i:512 * i + 512], ps("o0", i)[:, :], ACT.Copy), "o0", i)
            for i in range(2):
                wait_full(act, "vn1", i)
                emptied(go(vN[:, 1, 512 * i:512 * i + 512], ps("vn1", i)[:, :], ACT.Copy), "vn1", i)

            def heads_norm():
                for tt in range(TT):
                    for i in range(2):
                        wait_emptied(act, f"o{tt}", i)
                    go(xT[:, 4 * tt:4 * tt + 4, :], oN[:, tt, :].rearrange("p (a b) -> p a b", a=4), ACT.Square)\
                        .then_inc(Sm["o_squared"], 1)
                for tt in range(TT):
                    act.wait_ge(Sm["o_mean"], tt + 1)
                    go(ms[:, tt, :], ms[:, tt, :], ACT.Sqrt, scale=1.0 / P, bias=RMS_EPS).then_inc(Sm["o_root"], 1)
                for i in (0, 2):
                    wait_full(act, "oTa", i)
                    emptied(go(oT[:, 2 * i:2 * i + 2, :], ps("oTa", i).rearrange("p (a b) -> p a b", a=2), ACT.Copy), "oTa", i)

            def layer_norm(r, y):
                for tt in range(TT):
                    act.wait_ge(Sm["ln_var"], 2 * r + tt + 1)
                    go(rstd[:, tt:tt + 1], mv[:, tt, 1:2], ACT.Sqrt, bias=LN_EPS).then_inc(Sm["ln_root"], 1)
                    act.wait_ge(Sm["ln_scale"], 2 * r + tt + 1)
                    for n in range(2):
                        emptied(go(xN[:, tt, n * 512:(n + 1) * 512], ps(y, 2 * tt + n)[:, :], ACT.Identity,
                                   scale=rstd[:, tt:tt + 1], bias=nmr[:, tt:tt + 1]), y, 2 * tt + n)

            def experts(layer):
                s = moe_sems[layer]

                def tokens(half, count):
                    act.wait_ge(s["gathered"], count)
                    go(xeT[:, 4 * half:4 * half + 4, :], XG[:, :].rearrange("p (a b) -> p a b", a=4), ACT.Copy)\
                        .then_inc(s["xe_ready"], 1)

                xT_half(1 + 2 * layer)
                act.wait_ge(Sm["logits_ready"], layer + 1)
                go(rt[:, 64:96], rt[:, 32:64], ACT.Exp).then_inc(Sm["exp_done"], 1)
                def silu_gate(e, par):
                    act.wait_ge(s["gu_done"], e + 1)
                    go(sg[:, par, :], GU[par][:, 0:256], ACT.Silu).then_inc(s["sg_ready"], 1)

                def result(e, par):
                    act.wait_ge(s["down_done"], e + 1)
                    go(ys[CAP * par:CAP * par + CAP, 0:512], YD[0:CAP, :], ACT.Copy).then_inc(s["ys_ready"], 1)

                def two_experts(pair, last=False):
                    a = 2 * pair
                    silu_gate(a + 1, 1)
                    if not last:
                        tokens(0, a + 3)
                        tokens(1, a + 4)
                    result(a, 0)
                    if not last:
                        silu_gate(a + 2, 0)
                    result(a + 1, 1)

                tokens(0, 1)
                tokens(1, 2)
                silu_gate(0, 0)
                with act.Fori(0, NE // 2 - 1) as pair:
                    two_experts(pair)
                two_experts(NE // 2 - 1, last=True)

                act.wait_ge(Sm["flag_ready"], layer + 1)
                more = act.value_load(flag[0:1, 0:1], min_val=0, max_val=T)
                with act.If(more > CAP):
                    with act.Fori(1, PASSES) as ps_:
                        with act.Fori(0, NE) as ei:
                            it = (ps_ - 1) * NE + ei
                            act.wait_ge(s["o_done"], it + 1)
                            for j, w in enumerate((moe_w_down, moe_w_gate, moe_w_up)):
                                act.dma_start(ovw[:, j, :].rearrange("p (k n) -> p k n", k=(FE // P, KC, KC)[j]),
                                              w[layer, bass.ds(ei, 1)].rearrange("o (k p) n -> p (o k) n", p=P))\
                                    .then_inc(s["o_loaded"], 16)
                            act.wait_ge(s["o_gathered"], it + 1)
                            go(xo, XG[:, :].rearrange("p (a b) -> p a b", a=KC), ACT.Copy).then_inc(s["o_xe"], 1)
                            act.wait_ge(s["o_gu"], it + 1)
                            go(sg[:, 0, :], GU[0][:, 0:256], ACT.Silu).then_inc(s["o_sg"], 1)
                            act.wait_ge(s["o_down"], it + 1)
                            go(ys[0:CAP, 0:512], YD[0:CAP, :], ACT.Copy).then_inc(s["o_ys"], 1)

            heads_norm()
            layer_norm(0, "ya")
            experts(0)
            layer_norm(1, "y0")

            act.dma_start(rbT[0:BUCKETS, :], rel_bias).then_inc(ld_att, 16)
            act.dma_start(oh[0:BUCKETS, :], buckets).then_inc(ld_att, 16)
            act.dma_start(lam, b_lambda.rearrange("a i d -> a (i d)").to_broadcast([P, 4 * DH]).rearrange("p (a b) -> p a b", a=4))\
                .then_inc(ld_att, 16)
            act.dma_start(nwB, b_subln_w.to_broadcast([P, P])).then_inc(ld_att, 16)
            xT_half(2)
            act.wait_ge(Sm["lam_sum"], 1)
            go(lam2, lam2, ACT.Exp).then_inc(Sm["lam_exp"], 1)
            act.wait_ge(Sm["qz_zero"], 1)

            def take_q(name, i, h):
                wait_full(act, name, i)
                go(qz[0:DH, h, 0, :], ps(name, i)[0:DH, 0:T], ACT.Copy, scale=DH ** -0.5)
                emptied(go(qz[DH:P, h, 1, :], ps(name, i)[DH:P, 0:T], ACT.Copy, scale=DH ** -0.5), name, i)

            def take_v(name, tt, n):
                wait_full(act, name, tt)
                emptied(go(vB[:, tt, 512 * n:512 * n + 512], ps(name, tt)[:, :], ACT.Copy), name, tt)

            for h in range(4):
                take_q("q", h, h)
            for tt in range(TT):
                take_v("v", tt, 0)

            def exponentials(i):
                w = (i % 2 + 1) * P
                act.wait_ge(Sm["sc_ready"], i + 1)
                for half in range(2):
                    last = go(pa[:, i % 2, half * T:half * T + w], sc[:, i % 2, half * T:half * T + w], ACT.Exp, scale=-1.0,
                              bias=smx[:, i % 2, half:half + 1], accum_out=ssum[:, i % 2, half:half + 1])
                last.then_inc(Sm["p_ready"], 1)

            def take_turned(i):
                qt = i % 2
                wait_full(act, "atT", i)
                emptied(go(atT[:, i % 2, 0:qt + 1, :], ps("atT", i)[:, 0:(qt + 1) * P].rearrange("p (a b) -> p a b", b=P),
                           ACT.Copy), "atT", i)

            def take_values(i):
                h, qt = i // 2, i % 2
                wait_full(act, "av", i)
                emptied(go(oN[:, qt, h * P:(h + 1) * P], ps("av", i)[:, 0:P], ACT.Copy), "av", i)

            def square_heads(half):
                if half == 0:
                    for tt in range(TT):
                        wait_full(act, "v2", tt)
                for i in range(8 * half, 8 * half + 8):
                    wait_emptied(act, "av", i)
                go(xT[:, 4 * half:4 * half + 4, :].rearrange("p a (b c) -> p (a b) c", b=2),
                   oN[:, :, 512 * half:512 * half + 512].rearrange("p t (h c) -> p t h c", h=4), ACT.Square)\
                    .then_inc(Sm["o_squared"], 1)

            def root_heads(half):
                act.wait_ge(Sm["o_mean"], 3 + half)
                go(msB[:, half, :], msB[:, half, :], ACT.Sqrt, scale=1.0 / P, bias=RMS_EPS).then_inc(Sm["o_root"], 1)

            def take_heads(i):
                wait_full(act, "oTb", i)
                emptied(go(kT[:, 2 * i:2 * i + 2, :], ps("oTb", i).rearrange("p (a b) -> p a b", a=2), ACT.Copy), "oTb", i)

            for k in range(ITEMS + 2):
                if k < ITEMS:
                    exponentials(k)
                if k < 8 and k % 2 == 0:
                    take_q("q2", k // 2, 4 + k // 2)
                elif 8 <= k < 10:
                    take_v("v2", k - 8, 1)
                elif k == 10:
                    square_heads(0)
                elif k == 11:
                    root_heads(0)
                elif k == 12:
                    take_heads(0)
                if 1 <= k <= ITEMS:
                    take_turned(k - 1)
                if k >= 2:
                    take_values(k - 2)
            square_heads(1)
            root_heads(1)
            take_heads(2)
            layer_norm(2, "yb")
            experts(1)
            layer_norm(3, "y1")

        @block.vector
        def _(dve):
            def step(ins):
                in_step(dve, ins, dve_step)

            def xT_half(r):
                for i in (1, 3):
                    wait_full(dve, f"xT{r}", i)
                    emptied(dve.tensor_copy(xT[:, 2 * i:2 * i + 2, :], ps(f"xT{r}", i).rearrange("p (a b) -> p a b", a=2)),
                            f"xT{r}", i)

            def bc(v, n):
                return v.unsqueeze(2).to_broadcast([P, v.shape[1], n])

            def quad(name, i):
                return ps(name, i).rearrange("p (a b) -> p a b", a=4)

            xT_half(0)
            wait_full(dve, "cw")
            emptied(dve.tensor_copy(cw, ps("cw")[:, 0:96]), "cw")

            def convolve(t):
                name = ("qk", "qk2", "vch")[t // 8]
                src, dst = ps(name, t % 8), conv[:, t % 4, :]
                wait_full(dve, name, t % 8)
                if t >= 4:
                    dve.wait_ge(Sm["silu_done"], t - 3)
                step(dve.tensor_scalar(dst, src[:, 0:T], cw[:, 3 * 24 + t:3 * 24 + t + 1], None, ALU.mult))
                for s in (1, 2, 3):
                    tap = (3 - s) * 24 + t
                    ins = dve.scalar_tensor_tensor(dst[:, s:T], src[:, 0:T - s], cw[:, tap:tap + 1], dst[:, s:T],
                                                   ALU.mult, ALU.add)
                    if s < 3:
                        step(ins)
                    else:
                        emptied(ins, name, t % 8)

            wait_emptied(dve, "cw")
            for t in range(4):
                convolve(t)
            wait_full(dve, "ab")
            dve.wait_ge(ld_par, 16 * 5)
            emptied(dve.tensor_copy(ab, ps("ab")[:, 0:32].rearrange("p (a b) -> p a b", a=2)), "ab")
            wait_emptied(dve, "ab")
            dtb2 = dtb.unsqueeze(1).to_broadcast([P, TT, HA])
            step(dve.tensor_tensor(gt1, ab[:, :, 0:HA], dtb2, ALU.add))
            dve.scalar_tensor_tensor(gt2, gt1, -1.0, gt1, ALU.mult, ALU.max).then_inc(Sm["gate_abs"], 1)
            dve.wait_ge(Sm["softplus_done"], 1)
            step(dve.scalar_tensor_tensor(gt1, gt1, 0.0, gt2, ALU.max, ALU.add))
            alog2 = alog.unsqueeze(1).to_broadcast([P, TT, HA])
            dve.scalar_tensor_tensor(g, gt1, -1.0, alog2, ALU.mult, ALU.mult).then_inc(Sm["gates_ready"], 1)
            step(dve.tensor_scalar(beta, beta, 1.0, None, ALU.add))
            step(dve.reciprocal(beta, beta))
            for t in range(4, 8):
                convolve(t)
            wait_full(dve, "cum")
            gcf = gc[:, :, :].rearrange("p a b -> p (a b)")
            step(dve.tensor_copy(gcf, ps("cum")[:, 0:16]))
            step(dve.tensor_tensor(kd[:, :, :].rearrange("p a b -> p (a b)"), ps("cum")[:, 16:32], gcf, ALU.subtract))
            dve.sem_inc(free[where["cum", 0][0]], 1)
            dve.sem_inc(Sm["decay_in"], 1)
            for i in range(4):
                wait_full(dve, "grow", i)
                for j in range(4):
                    m = 4 * i + j
                    last = dve.tensor_scalar(Dm[:, m, :], ps("grow", i)[:, j * P:(j + 1) * P], gcf[:, m:m + 1], 0.0,
                                             ALU.subtract, ALU.max)
                emptied(last, "grow", i)
            for t in range(8, 18):
                convolve(t)
            wait_full(dve, "ssq")
            step(dve.tensor_scalar(r2, ps("ssq")[:, 0:32].rearrange("p (a b) -> p a b", a=TT), RMS_EPS, None, ALU.add))
            dve.reciprocal(r2, r2).then_inc(Sm["norm_in"], 1)
            dve.sem_inc(free[where["ssq", 0][0]], 1)
            dve.wait_ge(Sm["norm_in"], 1)
            step(dve.scalar_tensor_tensor(nb, r2[:, :, HA:2 * HA], -1.0, beta, ALU.mult, ALU.mult))
            dve.wait_ge(Sm["decay_ready"], 1)
            dve.tensor_tensor(nbe, nb, eg, ALU.mult).then_inc(Sm["scales_ready"], 1)
            for t in range(18, 21):
                convolve(t)
            dve.wait_ge(Sm["norm_root"], 1)
            step(dve.tensor_tensor(bk, bk, beta, ALU.mult))
            for t in range(21, 22):
                convolve(t)
            for b in range(4):
                wait_full(dve, "kk", b)
                dve.wait_ge(Sm["nb_ready"], b + 1)
                m4 = Nm[:, 4 * b:4 * b + 4, :]
                emptied(dve.tensor_tensor(m4, quad("kk", b), m4, ALU.mult), "kk", b)
                if b % 2 == 0:
                    convolve(22 + b // 2)
            for i in range(4):
                tt, hg = i // 2, i % 2
                wait_full(dve, "vtr", i)
                emptied(dve.tensor_tensor(vN[:, tt, 512 * hg:512 * hg + 512].rearrange("p (a b) -> p a b", a=4),
                                          quad("vtr", i), bc(bk[:, tt, 4 * hg:4 * hg + 4], P), ALU.mult), "vtr", i)
            for b in range(4):
                wait_full(dve, "kq", b)
                wait_emptied(dve, "dtr", b)
                m4 = QK[:, 4 * b:4 * b + 4, :]
                emptied(dve.tensor_tensor(m4, quad("kq", b), m4, ALU.mult), "kq", b)
            for i in range(2):
                wait_full(dve, "ktr", i)
                emptied(dve.tensor_tensor(kN[:, 4 * i:4 * i + 4, :], quad("ktr", i), bc(kd[:, 0, 4 * i:4 * i + 4], P),
                                          ALU.mult), "ktr", i)
            for lev in range(1, 7):
                for b in range(4):
                    wait_full(dve, f"tt{lev}", b)
                    if lev < 6:
                        wait_full(dve, f"t{lev}", b)
                        m4 = Ti[:, 4 * b:4 * b + 4, :]
                        emptied(dve.tensor_tensor(m4, quad(f"t{lev}", b), m4, ALU.add), f"t{lev}", b)
                    m4 = TiT[:, 4 * b:4 * b + 4, :]
                    emptied(dve.tensor_tensor(m4, quad(f"tt{lev}", b), m4, ALU.add), f"tt{lev}", b)
            for i in range(2):
                wait_full(dve, "s1", i)
                emptied(dve.tensor_copy(S[:, 4 * i:4 * i + 4, :], quad("s1", i)), "s1", i)
            for i in range(2):
                wait_full(dve, "ks", i)
                tmp = PT[:, 4 * i:4 * i + 4, :]
                emptied(dve.tensor_tensor(tmp, quad("ks", i), bc(nbe[:, 1, 4 * i:4 * i + 4], P), ALU.mult), "ks", i)
                wait_emptied(dve, "ks", i)
                v1 = vN[:, 1, 512 * i:512 * i + 512].rearrange("p (a b) -> p a b", a=4)
                dve.tensor_tensor(v1, v1, tmp, ALU.add).then_inc(Sm["r1_ready"], 1)
                wait_full(dve, "qs", i)
                emptied(dve.tensor_tensor(qS[:, 4 * i:4 * i + 4, :], quad("qs", i), bc(eg[:, 1, 4 * i:4 * i + 4], P),
                                          ALU.mult), "qs", i)
            for i in range(2):
                wait_full(dve, "o1", i)
                wait_emptied(dve, "qs", i)
                emptied(dve.tensor_tensor(oN[:, 1, 512 * i:512 * i + 512].rearrange("p (a b) -> p a b", a=4),
                                          quad("o1", i), qS[:, 4 * i:4 * i + 4, :], ALU.add), "o1", i)

            def heads_norm():
                for tt in range(TT):
                    dve.wait_ge(Sm["o_squared"], tt + 1)
                    step(dve.tensor_reduce(ms[:, tt, :], xT[:, 4 * tt:4 * tt + 4, :].rearrange("p a (b c) -> p (a b) c", b=2),
                                           AX_X, ALU.add))
                    dve.scalar_tensor_tensor(ms[:, tt, :], ms[:, tt, :], 1.0 / P, r2[:, tt, 0:HA], ALU.mult, ALU.mult)\
                        .then_inc(Sm["o_mean"], 1)
                dve.wait_ge(Sm["z_ready"], 1)
                for tt in range(TT):
                    dve.wait_ge(Sm["o_root"], tt + 1)
                    step(dve.reciprocal(ms[:, tt, :], ms[:, tt, :]))
                    step(dve.tensor_tensor(ms[:, tt, :], ms[:, tt, :], fq[:, tt, :], ALU.mult))
                    o3 = oN[:, tt, :].rearrange("p (a b) -> p a b", a=8)
                    step(dve.tensor_tensor(o3, o3, bc(ms[:, tt, :], P), ALU.mult))
                    dve.tensor_tensor(o3, o3, z[:, tt, :].rearrange("p (a b) -> p a b", a=8), ALU.mult)\
                        .then_inc(Sm["o_normed"], 1)
                for i in (1, 3):
                    wait_full(dve, "oTa", i)
                    emptied(dve.tensor_copy(oT[:, 2 * i:2 * i + 2, :], ps("oTa", i).rearrange("p (a b) -> p a b", a=2)),
                            "oTa", i)

            def layer_norm(r, y, lnp):
                for tt in range(TT):
                    for n in range(2):
                        wait_full(dve, y, 2 * tt + n)
                        last = dve.bn_stats(st6[:, tt, n, :], ps(y, 2 * tt + n)[:, :])
                    step(last)
                    dve.bn_aggr(mv[:, tt, :], st6[:, tt, :, :].rearrange("p a b -> p (a b)")).then_inc(Sm["ln_var"], 1)
                for tt in range(TT):
                    dve.wait_ge(Sm["ln_root"], 2 * r + tt + 1)
                    step(dve.reciprocal(rstd[:, tt:tt + 1], rstd[:, tt:tt + 1]))
                    dve.scalar_tensor_tensor(nmr[:, tt:tt + 1], mv[:, tt, 0:1], -1.0, rstd[:, tt:tt + 1], ALU.mult, ALU.mult)\
                        .then_inc(Sm["ln_scale"], 1)
                dve.wait_ge(ld_lnp, 32 * (r + 1))
                for tt in range(TT):
                    for n in range(2):
                        wait_emptied(dve, y, 2 * tt + n)
                    dve.tensor_tensor(xN[:, tt, :], xN[:, tt, :], lnp[:, 0, :], ALU.mult).then_inc(Sm["ln_scaled"], 1)

            def route(layer):
                lg, p, a, b_, c, d = (rt[:, 32 * k:32 * k + 32] for k in range(1, 7))
                sel = rt[:, 0:32]

                def t2(v):
                    return v.rearrange("p (a b) -> p a b", a=TT)

                def t8(v):
                    return v.rearrange("p (a b) -> p a b", a=TT * GRP)

                m1, m2, mr = (rt[:, 256 + 8 * k:264 + 8 * k] for k in range(3))
                mx, sm = rt[:, 288:290], rt[:, 290:292]
                gs, gt, gr = (rt[:, 296 + 8 * k:304 + 8 * k] for k in range(3))
                w8 = w4.unsqueeze(1).to_broadcast([P, TT * GRP, GRP])
                w2 = w4.unsqueeze(1).to_broadcast([P, TT, GRP])
                name = f"lg{layer}"
                wait_full(dve, name)
                emptied(dve.tensor_tensor(t2(lg), ps(name)[:, 0:32].rearrange("p (a b) -> p a b", a=TT),
                                          rb.unsqueeze(1).to_broadcast([P, TT, NE]), ALU.add), name)
                wait_emptied(dve, name)
                step(dve.tensor_reduce(mx, t2(lg), AX_X, ALU.max))
                dve.tensor_tensor(t2(lg), t2(lg), bc(mx, NE), ALU.subtract).then_inc(Sm["logits_ready"], 1)
                dve.wait_ge(Sm["exp_done"], layer + 1)
                step(dve.tensor_reduce(sm, t2(p), AX_X, ALU.add))
                step(dve.reciprocal(sm, sm))
                step(dve.tensor_tensor(t2(p), t2(p), bc(sm, NE), ALU.mult))

                def first_best(values, best, rank, top, out_, w, n):
                    step(dve.tensor_reduce(best, values, AX_X, ALU.max))
                    step(dve.tensor_tensor(rank, values, bc(best, GRP), ALU.is_equal))
                    step(dve.tensor_tensor(rank, rank, w, ALU.mult))
                    step(dve.tensor_reduce(top, rank, AX_X, ALU.max))
                    step(dve.tensor_tensor(out_, rank, bc(top, GRP), ALU.is_equal))

                first_best(t8(p), m1, t8(a), mr, t8(b_), w8, 8)
                step(dve.scalar_tensor_tensor(c, b_, -2.0, p, ALU.mult, ALU.add))
                first_best(t8(c), m2, t8(a), mr, t8(d), w8, 8)
                step(dve.tensor_tensor(b_, b_, d, ALU.add))
                step(dve.tensor_tensor(gs, m1, m2, ALU.add))
                first_best(t2(gs), mx, t2(gt), sm, t2(gr), w2, 2)
                dve.tensor_tensor(t8(sel), t8(b_), bc(gr, GRP), ALU.mult).then_inc(Sm["sel_ready"], 1)
                dve.wait_ge(Sm["sel_ready"], layer + 1)
                step(dve.tensor_tensor(p, p, sel, ALU.mult))
                step(dve.tensor_reduce(sm, t2(p), AX_X, ALU.add))
                step(dve.reciprocal(sm, sm))
                step(dve.tensor_tensor(gate[:, :, 0:NE], t2(p), bc(sm, NE), ALU.mult))
                name = f"rk{layer}"
                wait_full(dve, name)
                step(dve.memset(RK[:, :, NE * PASSES:NE * PASSES + 2], -1.0))
                step(dve.scalar_tensor_tensor(t2(a), ps(name)[:, 0:32].rearrange("p (a b) -> p a b", a=TT), 1.0, t2(sel),
                                              ALU.add, ALU.mult))
                step(dve.tensor_reduce(mx[:, 0:1], ps(name)[:, 32:48], AX_X, ALU.max))
                step(dve.tensor_copy(flag[:, :], mx[:, 0:1]))
                dve.sem_inc(Sm["flag_ready"], 1)
                for k in range(PASSES):
                    last = dve.tensor_scalar(RK[:, :, NE * k:NE * k + NE], t2(a), 1.0 + CAP * k, None, ALU.subtract)
                emptied(last, name)
                wait_emptied(dve, name)

            def place(out_, tt, col):
                return dve.tensor_scalar(out_, iota, RK[:, tt, col], None, ALU.is_equal)

            def place_gated(out_, tt, col, e):
                return dve.tensor_scalar(out_, iota, RK[:, tt, col], gate[:, tt, e], ALU.is_equal, ALU.mult)

            def experts(layer):
                s = moe_sems[layer]
                xT_half(1 + 2 * layer)
                route(layer)

                def build_gather(pair):
                    for q in range(2):
                        for tt in range(TT):
                            last = place(Pb[:, tt, q * CAP:(q + 1) * CAP], tt, bass.ds(2 * pair + q, 1))
                    last.then_inc(s["P_built"], 1)

                def hidden(e, par):
                    dve.wait_ge(s["sg_ready"], e + 1)
                    dve.tensor_tensor(hN[:, par, :], GU[par][:, 256:512], sg[:, par, :], ALU.mult).then_inc(s["h_ready"], 1)

                def turned(e, par):
                    dve.wait_ge(s["ht_done"], e + 1)
                    w = 512 if par else 256
                    dve.tensor_copy(hTG[:, par, 0:w], GU[par][:, 0:w]).then_inc(s["ht_ready"], 1)

                def result(e, par):
                    dve.wait_ge(s["down_done"], e + 1)
                    dve.tensor_copy(ys[CAP * par:CAP * par + CAP, 512:1024], YD[CAP:P, :]).then_inc(s["ys_ready"], 1)

                def two_experts(pair, last=False):
                    a = 2 * pair
                    turned(a, 0)
                    hidden(a + 1, 1)
                    for q in range(2):
                        for tt in range(TT):
                            built = place_gated(G2[:, tt, q * CAP:(q + 1) * CAP], tt, bass.ds(a + q, 1), bass.ds(a + q, 1))
                    built.then_inc(s["G_built"], 1)
                    result(a, 0)
                    turned(a + 1, 1)
                    if not last:
                        dve.wait_ge(s["gathered"], a + 4)
                        build_gather(pair + 2)
                        hidden(a + 2, 0)
                    result(a + 1, 1)

                build_gather(0)
                dve.wait_ge(s["gathered"], 2)
                build_gather(1)
                hidden(0, 0)
                with dve.Fori(0, NE // 2 - 1) as pair:
                    two_experts(pair)
                two_experts(NE // 2 - 1, last=True)

                more = dve.value_load(flag[0:1, 0:1], min_val=0, max_val=T)
                with dve.If(more > CAP):
                    with dve.Fori(1, PASSES) as ps_:
                        with dve.Fori(0, NE) as ei:
                            it = (ps_ - 1) * NE + ei
                            dve.wait_ge(s["o_done"], it + 1)
                            for tt in range(TT):
                                place(Pb[:, tt, 0:CAP], tt, bass.ds(ps_ * NE + ei, 1))
                                last = place_gated(G2[:, tt, 0:CAP], tt, bass.ds(ps_ * NE + ei, 1), bass.ds(ei, 1))
                            last.then_inc(s["o_P"], 1)
                            dve.wait_ge(s["o_sg"], it + 1)
                            dve.tensor_tensor(hN[:, 0, :], GU[0][:, 256:512], sg[:, 0, :], ALU.mult).then_inc(s["o_h"], 1)
                            dve.wait_ge(s["o_ht"], it + 1)
                            dve.tensor_copy(hTG[:, 0, :], GU[0][:, :]).then_inc(s["o_htr"], 1)
                            dve.wait_ge(s["o_down"], it + 1)
                            dve.tensor_copy(ys[0:CAP, 512:1024], YD[CAP:P, :]).then_inc(s["o_ys"], 1)

            heads_norm()
            layer_norm(0, "ya", lnpA)
            experts(0)
            layer_norm(1, "y0", oN)

            xT_half(2)
            dve.wait_ge(ld_att, 16 * 4)
            step(dve.tensor_tensor(lp, lam[:, 0:4:2, :], lam[:, 1:4:2, :], ALU.mult))
            dve.tensor_reduce(lam2, lp, AX_X, ALU.add).then_inc(Sm["lam_sum"], 1)
            wait_full(dve, "brow")
            dve.memset(brow[0:HB, T:REV], MASKED)
            step(dve.tensor_copy(brow[0:HB, 0:T], ps("brow")[0:HB, 0:T]))
            dve.sem_inc(free[where["brow", 0][0]], 1)
            dve.sem_inc(Sm["brow_ready"], 1)
            dve.wait_ge(Sm["lam_exp"], 1)
            step(dve.scalar_tensor_tensor(lamv, lam2[:, 1:2], LAMBDA_INIT, lam2[:, 0:1], ALU.subtract, ALU.subtract))

            def take_k(name, i, h):
                wait_full(dve, name, i)
                emptied(dve.tensor_copy(kT[:, h, :], ps(name, i)[:, 0:T]), name, i)

            for h in range(4):
                take_k("k", h, h)
            for i in range(4):
                wait_full(dve, "bias", i)
                emptied(dve.tensor_copy(bias[:, 2 * i:2 * i + 2, :], ps("bias", i).rearrange("p (a b) -> p a b", a=2)), "bias", i)
            wait_emptied(dve, "bias", 3)

            def add_bias(i):
                h, qt = i // 2, i % 2
                b, w = i % 2, (qt + 1) * P
                wait_full(dve, "sc", i)
                for half in range(2):
                    last = dve.tensor_tensor_reduce(sc[:, b, half * T:half * T + w], ps("sc", i)[:, half * T:half * T + w],
                                                    bias[:, h, T - w:T], -1.0, 3e38, ALU.add, ALU.min,
                                                    smx[:, b, half:half + 1])
                    if half:
                        emptied(last, "sc", i)
                wait_emptied(dve, "sc", i)
                dve.sem_inc(Sm["sc_ready"], 1)

            def difference(i):
                b, w = i % 2, (i % 2 + 1) * P
                dve.wait_ge(Sm["p_ready"], i + 1)
                step(dve.reciprocal(srec[:, b, :], ssum[:, b, :]))
                step(dve.tensor_tensor(srec[:, b, 1:2], srec[:, b, 1:2], lamv, ALU.mult))
                if i >= 2:
                    wait_full(dve, "atT", i - 2)
                step(dve.tensor_scalar(at[:, b, 0:w], pa[:, b, 0:w], srec[:, b, 0:1], None, ALU.mult))
                dve.scalar_tensor_tensor(at[:, b, 0:w], pa[:, b, T:T + w], srec[:, b, 1:2], at[:, b, 0:w], ALU.mult, ALU.add)\
                    .then_inc(Sm["at_ready"], 1)

            def mean_squares(half):
                dve.wait_ge(Sm["o_squared"], 3 + half)
                dve.tensor_reduce(msB[:, half, :], xT[:, 4 * half:4 * half + 4, :].rearrange("p a (b c) -> p (a b) c", b=2),
                                  AX_X, ALU.add).then_inc(Sm["o_mean"], 1)

            def heads_scale(half):
                dve.wait_ge(Sm["o_root"], 3 + half)
                dve.reciprocal(msB[:, half, :], msB[:, half, :]).then_inc(Sm["o_scale"], 1)

            def take_heads(i):
                wait_full(dve, "oTb", i)
                emptied(dve.tensor_copy(kT[:, 2 * i:2 * i + 2, :], ps("oTb", i).rearrange("p (a b) -> p a b", a=2)), "oTb", i)

            for k in range(ITEMS + 1):
                if k < ITEMS:
                    add_bias(k)
                if k >= 1:
                    difference(k - 1)
                if k < 8 and k % 2 == 1:
                    take_k("k2", k // 2, 4 + k // 2)
                elif k == 10:
                    mean_squares(0)
                elif k == 11:
                    heads_scale(0)
                elif k == 12:
                    take_heads(1)
            mean_squares(1)
            heads_scale(1)
            take_heads(3)
            layer_norm(2, "yb", lnpA)
            experts(1)
            layer_norm(3, "y1", oN)

        @block.gpsimd
        def _(pool):
            def step(ins):
                in_step(pool, ins, pool_step)

            def four_of(v):
                return v.unsqueeze(1).to_broadcast([P, 4, P])

            def load_lnp(dst, l, k):
                pool.dma_start(dst[:, 0, :], ln_w[l, k:k + 1, :].to_broadcast([P, D])).then_inc(ld_lnp, 16)
                pool.dma_start(dst[:, 1, :], ln_b[l, k:k + 1, :].to_broadcast([P, D])).then_inc(ld_lnp, 16)

            def layer_norm(r, lnp):
                for tt in range(TT):
                    pool.wait_ge(Sm["ln_scaled"], 2 * r + tt + 1)
                    pool.tensor_tensor(xN[:, tt, :], xN[:, tt, :], lnp[:, 1, :], ALU.add).then_inc(Sm["x_ready"], 1)

            pool.wait_ge(ld_cst, 16)
            for i in range(4):
                pool.wait_ge(Sm["dm_exp"], i + 1)
                d = Dm[:, 4 * i:4 * i + 4, :]
                pool.tensor_tensor(d, d, four_of(low), ALU.mult).then_inc(Sm["dm_ready"], 1)
            pool.wait_ge(Sm["dm_ready"], 4)
            pool.wait_ge(Sm["scales_ready"], 1)
            for b in range(4):
                m4 = Nm[:, 4 * b:4 * b + 4, :]
                nb4 = nb[:, b // 2, 4 * (b % 2):4 * (b % 2) + 4].unsqueeze(2).to_broadcast([P, 4, P])
                pool.tensor_tensor(m4, Dm[:, 4 * b:4 * b + 4, :], nb4, ALU.mult).then_inc(Sm["nb_ready"], 1)
            for b in range(4):
                wait_emptied(pool, "kk", b)
                t4 = Ti[:, 4 * b:4 * b + 4, :]
                step(pool.tensor_tensor(t4, Nm[:, 4 * b:4 * b + 4, :], four_of(mask(C_LEV)), ALU.mult))
                pool.tensor_tensor(t4, t4, four_of(ident), ALU.add).then_inc(Sm["T_init"], 1)
            for lev in range(1, 7):
                for b in range(4):
                    wait_full(pool, f"p{lev - 1}" if lev > 1 else "dtr", b)
                    pool.tensor_tensor(Dm[:, 4 * b:4 * b + 4, :], Nm[:, 4 * b:4 * b + 4, :], four_of(mask(C_LEV + lev)),
                                       ALU.mult).then_inc(Sm["L_ready"], 1)
            pool.wait_ge(Sm["L_ready"], 24)
            pool.wait_ge(ld_par, 16 * 5)
            for i in range(4):
                wait_emptied(pool, "zz", i)
            for tt in range(TT):
                z3 = z[:, tt, :].rearrange("p (a b) -> p a b", a=8)
                last = pool.tensor_tensor(z3, z3, nw.unsqueeze(1).to_broadcast([P, 8, P]), ALU.mult)
            last.then_inc(Sm["z_ready"], 1)
            for i in range(2):
                wait_full(pool, "o1", i)
            load_lnp(lnpA, 0, 0)
            layer_norm(0, lnpA)
            load_lnp(oN, 0, 1)
            layer_norm(1, oN)

            pool.memset(view(4096, HB * 2 * T), 0.0).then_inc(Sm["qz_zero"], 1)
            pool.wait_ge(ld_att, 16 * 4)
            pool.tensor_scalar(nwB, nwB, 1.0 - LAMBDA_INIT, None, ALU.mult).then_inc(Sm["nwB_ready"], 1)
            pool.wait_ge(Sm["brow_ready"], 1)
            pool.dma_start(bias_rows, brow[0:HB, :]).then_inc(st_bias, 16)
            pool.wait_ge(st_bias, 16)
            pool.dma_start(braw[:, :, :], bass.AP(bias_rows.tensor, 0, [[1, P], [REV, HB], [1, T]])).then_inc(ld_bias, 16)

            def scale_heads(half):
                pool.wait_ge(Sm["o_scale"], half + 1)
                o4 = oN[:, :, 512 * half:512 * half + 512].rearrange("p t (h c) -> p t h c", h=4)
                r4 = msB[:, half, :].rearrange("p (t h) -> p t h", t=TT).unsqueeze(3).to_broadcast([P, TT, 4, P])
                step(pool.tensor_tensor(o4, o4, r4, ALU.mult))
                w4_ = nwB.unsqueeze(1).unsqueeze(1).to_broadcast([P, TT, 4, P])
                pool.tensor_tensor(o4, o4, w4_, ALU.mult).then_inc(Sm["o_normed"], 1)

            scale_heads(0)
            wait_full(pool, "sc", 15)
            load_lnp(lnpA, 1, 0)
            scale_heads(1)
            layer_norm(2, lnpA)
            load_lnp(oN, 1, 1)
            layer_norm(3, oN)


_INS = ["x", "a_w_in", "a_conv", "a_A_log", "a_dt_bias", "a_norm_w", "a_w_out", "b_w_q", "b_w_kv", "b_lambda",
        "b_subln_w", "b_w_out", "rel_bias", "router_w", "router_b", "moe_w_gate", "moe_w_up", "moe_w_down", "ln_w", "ln_b"]


def kernel(**inputs):
    import concourse.bacc as bacc
    from concourse.bass_utils import run_bass_kernel_spmd

    nc = bacc.Bacc("TRN2", target_bir_lowering=False, num_devices=1)
    arrays, args = {}, []
    for name in _INS:
        arrays[f"in_{name}"] = np.ascontiguousarray(inputs[name])
    arrays["in_consts"] = constants()
    arrays["in_buckets"] = bucket_rows()
    for name, a in arrays.items():
        args.append(nc.dram_tensor(name, a.shape, mybir.dt.from_np(a.dtype), kind="ExternalInput").ap())
    args.append(nc.dram_tensor("bias_rows", [HB, REV], F32, kind="Internal").ap())
    args.append(nc.dram_tensor("out_0", (1, T, D), F32, kind="ExternalOutput").ap())
    build(nc, *args)
    r = run_bass_kernel_spmd(nc, [arrays], core_ids=[0])
    return r.results[0]["out_0"]
```

```python
from contextlib import ExitStack
import math

import numpy as np

import concourse.bass as bass
from concourse import mybir

F32 = mybir.dt.float32
I32 = mybir.dt.int32
ACT = mybir.ActivationFunctionType
ALU = mybir.AluOpType
AX_X = mybir.AxisListType.X

P = 128
T = 256
TT = T // P
D = 1024
KC = D // P
HA = 8
HB = 8
DH = 64
TAPS = 4
NE = 16
GRP = 4
FE = 512
CAP = 64
PASSES = T // CAP
DEPTH = 2
ALPHA = (2 * DEPTH) ** 0.25
LN_EPS = 1e-5
RMS_EPS = 1e-6
LAMBDA_INIT = 0.8 - 0.6 * math.exp(-0.3)
BUCKETS = 32
MAX_DIST = 128
REV = 384
MASKED = -1e30

SLOT = 4096
RING = 6
OWN, SPARE = 2, 3
BASE_A = 0
BASE_M0 = BASE_A + 10
BASE_B = BASE_M0 + 3 * NE - 4
BASE_M1 = BASE_B + 8

C_ID, C_ONE, C_TRI, C_TRIS, C_LOW, C_LOWS, C_LEV, C_ALPHA = 0, 1, 2, 3, 4, 5, 6, 13
C_REV = 14
C_IOTA = 15 * P
C_W4 = C_IOTA + CAP
C_BEFORE = C_W4 + GRP
C_COLS = C_BEFORE + GRP * GRP


def constants():
    i = np.arange(P)
    r, c = i[:, None], i[None, :]
    out = np.zeros((P, C_COLS), np.float32)

    def put(k, m):
        out[:, k * P:(k + 1) * P] = m

    put(C_ID, r == c)
    put(C_ONE, 1.0)
    put(C_TRI, r <= c)
    put(C_TRIS, r < c)
    put(C_LOW, r >= c)
    put(C_LOWS, r > c)
    for n in range(7):
        s = 1 << n
        put(C_LEV + n, (r // (2 * s) == c // (2 * s)) & (r // s % 2 == 1) & (c // s % 2 == 0))
    put(C_ALPHA, ALPHA * (r == c))
    put(C_REV, r + c == P - 1)
    out[:, C_IOTA:C_IOTA + CAP] = np.arange(CAP) + 1
    out[:, C_W4:C_W4 + GRP] = GRP - np.arange(GRP)
    j = np.arange(GRP)
    out[:, C_BEFORE:C_COLS] = (j[:, None] > j[None, :]).reshape(-1)
    return out


def bucket_rows():
    out = np.zeros((BUCKETS, REV), np.float32)
    half = BUCKETS // 2
    for m in range(T):
        n = T - 1 - m
        b = n if n < half else min(BUCKETS - 1, half + int(
            np.float32(np.log(np.float32(n) / np.float32(half)) / math.log(MAX_DIST / half) * (BUCKETS - half))))
        out[b, m] = 1.0
    return out


def build(nc, x, a_w_in, a_conv, a_A_log, a_dt_bias, a_norm_w, a_w_out, b_w_q, b_w_kv, b_lambda, b_subln_w,
          b_w_out, rel_bias, router_w, router_b, moe_w_gate, moe_w_up, moe_w_down, ln_w, ln_b, consts, buckets,
          bias_rows, out):
    with ExitStack() as ctx:
        def sb(name, shape, dt=F32):
            return ctx.enter_context(nc.sbuf_tensor(name, shape, dt))

        def sem(name):
            return ctx.enter_context(nc.semaphore(name))

        ring = sb("ring", [P, RING, SLOT])
        xN = sb("xN", [P, TT, D])
        xT = sb("xT", [P, KC, T])
        oN = sb("oN", [P, TT, D])
        xTh = xT[:, :, :].rearrange("p (f a) b -> p f (a b)", f=2)
        cst = sb("cst", [P, C_COLS])
        arena = sb("arena", [P, 19456])
        small = sb("small", [P, 768])
        flag = sb("flag", [P, 1], I32)

        def mask(k):
            return cst[:, k * P:(k + 1) * P]

        ident, ones, tri, tris, low, lows, alphaI = (mask(k) for k in (C_ID, C_ONE, C_TRI, C_TRIS, C_LOW, C_LOWS, C_ALPHA))
        reverse = mask(C_REV)
        iota = cst[:, C_IOTA:C_IOTA + CAP]
        w4 = cst[:, C_W4:C_W4 + GRP]
        before = cst[:, C_BEFORE:C_COLS].rearrange("p (a b) -> p a b", a=GRP)

        taken = [0]

        def tiny(*shape):
            n = int(np.prod(shape))
            v = small[:, taken[0]:taken[0] + n]
            taken[0] += n
            assert taken[0] <= 768
            if len(shape) == 2:
                v = v.rearrange("p (a b) -> p a b", a=shape[0])
            if len(shape) == 3:
                v = v.rearrange("p (a b c) -> p a b c", a=shape[0], b=shape[1])
            return v

        def view(at, *shape):
            n = int(np.prod(shape))
            v = arena[:, at:at + n]
            if len(shape) == 2:
                v = v.rearrange("p (a b) -> p a b", a=shape[0])
            if len(shape) == 3:
                v = v.rearrange("p (a b c) -> p a b c", a=shape[0], b=shape[1])
            return v

        qkT = view(0, 16, T)
        vN = view(4096, TT, D)
        kN = view(6144, HA, P)
        z = view(7168, TT, D)
        Dm = view(9216, 16, P)
        Nm = view(11264, 16, P)
        QK = view(13312, 16, P)
        Ti = view(15360, 16, P)
        TiT = view(17408, 16, P)
        conv = view(13568, 4, T)
        vT = oN[:, :, :].rearrange("p a (b c) -> p (a b) c", b=4)
        sq = view(6144, 4, T)
        PT = xT[:, :, :].rearrange("p a (b c) -> p (a b) c", b=2)
        S = view(15360, HA, P)
        qS = view(16384, HA, P)
        oT = view(9216, KC, T)
        lnp = view(5120, 2, D)

        kT = view(0, HB, T)
        vB = view(2048, TT, D)
        qz = view(4096, HB, 2, T)
        bias = view(8192, HB, T)
        braw = view(13312, HB, T)
        sc = view(10240, 2, 2 * T)
        pa = view(11264, 2, 2 * T)
        at = view(12288, 2, T)
        atT = view(12800, 2, TT, P)
        junk = mask(C_LEV)
        brow = view(10240, REV)
        oh = view(10624, REV)
        rbT = view(11008, HB)
        lam = view(11016, 4, DH)
        lp = view(11272, 2, DH)

        xeT = view(0, KC, 2 * CAP)
        xo = view(0, KC, CAP)
        sg = view(1024, 2, 256)
        hN = view(1536, 2, 256)
        hTG = view(2048, 2, 512)
        ys = view(3072, D)
        Pb = view(4096, TT, 2 * CAP)
        G2 = view(4352, TT, P)
        RK = view(4608, TT, NE * PASSES + 2)
        gate = view(4740, TT, NE + 2)
        rt = view(4800, 320)
        rtw = view(3072, 256)
        ovw = view(7168, 3, SLOT)

        cw = tiny(TAPS * 24)
        wab = view(13312, KC, 16)
        cwr = view(13440, P)
        lnr = view(14592, P)
        ab = tiny(TT, 16)
        alog = tiny(8)
        dtb = tiny(8)
        g = tiny(TT, HA)
        beta = tiny(TT, HA)
        gt1 = tiny(TT, HA)
        gt2 = tiny(TT, HA)
        gc = tiny(TT, HA)
        eg = tiny(TT, HA)
        kd = tiny(TT, HA)
        r2 = tiny(TT, 2 * HA)
        fq = tiny(TT, HA)
        bk = tiny(TT, HA)
        nb = tiny(TT, HA)
        nbe = tiny(TT, HA)
        ms = tiny(TT, HA)
        msB = tiny(2, 8)
        lnc = tiny(2, 4, KC)
        nw = tiny(P)
        nwB = nw[:, 0:1]
        st6 = tiny(TT, 2, 6)
        mv = tiny(TT, 2)
        rstd = tiny(TT)
        nmr = tiny(TT)
        rw = sb("rw", [P, KC, NE])
        rb = tiny(NE)
        lam2 = tiny(2)
        lamv = tiny(1)
        smx = tiny(2, 2)
        ssum = tiny(2, 2)
        srec = tiny(2, 2)

        bank = [ctx.enter_context(nc.psum_tensor(f"bank{b}", [P, 512], F32)) for b in range(8)]
        Y = bank[0:4]
        GU, XG, YD = bank[4:6], bank[6], bank[7]

        order = []

        def fill(name, n, banks):
            order.extend((name, i, banks[i % len(banks)]) for i in range(n))

        four, low4 = (4, 5, 6, 7), (0, 1, 2, 3)
        fill("xT0", 4, four)
        fill("cw", 1, (4,))
        fill("qk", 4, low4)
        fill("ab", 1, (5,))
        order.append(("ssq", 0, 7))
        order.extend(("qk", i, i % 4) for i in range(4, 8))
        fill("cum", 1, (6,))
        fill("grow", 4, (4, 5, 6, 4))
        fill("qk2", 8, low4)
        fill("lnc", 1, (4,))
        fill("vch", 8, low4)
        fill("kk", 4, (5, 6, 4, 5))
        fill("zz", 4, low4)
        fill("vtr", 4, (6, 7, 4, 5))
        fill("ttr", 4, (6, 7, 4, 5))
        fill("dtr", 4, (6, 7, 4, 5))
        fill("kq", 4, (6, 7, 4, 5))
        fill("ktr", 2, (6, 7))
        for lev in range(1, 7):
            fill(f"p{lev}", 4, (0, 1, 4, 5))
            if lev < 6:
                fill(f"t{lev}", 4, (2, 6))
            fill(f"tt{lev}", 4, (3, 7))
        fill("vn0", 2, (6, 7))
        fill("o0", 2, (4, 5))
        fill("s1", 2, (6, 7))
        fill("ks", 2, (4, 5))
        fill("qs", 2, (6, 7))
        fill("vn1", 2, (4, 5))
        fill("o1", 2, (6, 7))
        fill("oTa", 4, four)
        fill("ya", 4, low4)
        fill("xT1", 4, four)
        fill("lg0", 1, (4,))
        fill("rk0", 1, (5,))
        fill("y0", 4, low4)
        fill("xT2", 4, four)
        fill("q", 4, (5, 6, 7, 0))
        fill("brow", 1, (4,))
        fill("k", 4, (1, 2, 3, 5))
        fill("v", 2, (6, 7))
        fill("bias", 4, (4, 5, 6, 7))
        ITEMS = 2 * HB
        for k in range(ITEMS + 2):
            if k < ITEMS:
                order.append(("sc", k, 4 + k % 2))
            if k < 8:
                order.append(("q2" if k % 2 == 0 else "k2", k // 2, k % 4))
            elif k in (8, 10):
                order.append(("v2", k // 2 - 4, k // 2 - 4))
            elif k == 12:
                fill("yb", 4, low4)
            elif k == 13:
                fill("oTb", 2, (6, 7))
            if 1 <= k <= ITEMS:
                order.append(("atT", k - 1, 6))
            if k >= 2:
                order.append(("av", k - 2, 7))
        order.append(("oTb", 2, 4))
        order.append(("oTb", 3, 5))
        fill("xT3", 4, four)
        fill("lg1", 1, (4,))
        fill("rk1", 1, (5,))
        fill("y1", 4, low4)
        where, per_bank = {}, [0] * 8
        for name, i, b in order:
            where[name, i] = (b, per_bank[b])
            per_bank[b] += 1
        full = [sem(f"bank{b}_full") for b in range(8)]
        free = [sem(f"bank{b}_free") for b in range(8)]

        def ps(name, i=0):
            return bank[where[name, i][0]]

        def before_fill(eng, name, i=0):
            b, k = where[name, i]
            if k:
                eng.wait_ge(free[b], k)

        def filled(ins, name, i=0):
            ins.then_inc(full[where[name, i][0]], 1)

        def wait_full(eng, name, i=0):
            b, k = where[name, i]
            eng.wait_ge(full[b], k + 1)

        def emptied(ins, name, i=0):
            ins.then_inc(free[where[name, i][0]], 1)

        def wait_emptied(eng, name, i=0):
            b, k = where[name, i]
            eng.wait_ge(free[b], k + 1)

        ld_x, ld_cst, ld_cw, ld_ab, ld_par = (sem(n) for n in ("ld_x", "ld_cst", "ld_cw", "ld_ab", "ld_par"))
        ld_att, ld_lnp, ld_bias, st_bias, st_out = (sem(n) for n in ("ld_att", "ld_lnp", "ld_bias", "st_bias", "st_out"))
        ld_lnr, ld_id, ld_gates = sem("ld_lnr"), sem("ld_id"), sem("ld_gates")
        ld_own_gu, ld_own_down, ld_spare = sem("ld_own_gu"), sem("ld_own_down"), sem("ld_spare")
        ring_loaded = [sem(f"ring{s}_loaded") for s in range(RING)]
        dve_step, act_step, pool_step = sem("dve_step"), sem("act_step"), sem("pool_step")
        names = """gate_abs softplus_done gates_ready decay_in decay_ready dm_exp dm_ready silu_done
            sq_ready sq_used norm_in norm_root scales_ready z_ready nb_ready T_init L_ready r1_ready o_squared o_mean o_root o_scale first_scale first_normed o_normed
            ln_var ln_root ln_scale ln_normed ln_scaled x_ready out_ready exp_done sel_ready flag_ready
            brow_ready sc_ready p_ready at_ready lam_sum lam_exp lam_ready qz_zero nwB_ready""".split()
        Sm = {n: sem(n) for n in names}

        moe_sems = [{n: sem(f"moe{layer}_{n}") for n in """P_built G_built gathered xe_ready gu_done sg_ready h_ready ht_done
            ht_ready down_done ys_ready scattered o_P o_gathered o_xe o_loaded o_gu o_sg o_h o_ht o_htr o_down o_ys
            o_done""".split()} for layer in range(DEPTH)]

        def signal(ins, name):
            ins.then_inc(Sm[name], 1)

        counts = {}

        def in_step(eng, ins, s):
            counts[s.name] = counts.get(s.name, 0) + 1
            ins.then_inc(s, 1)
            eng.wait_ge(s, counts[s.name])

        def loads(n):
            return 16 * (n // RING + 1)

        def after_load(eng, n):
            eng.wait_ge(ring_loaded[n % RING], loads(n))

        def gate_at(e):
            return (0, 2, None, 6, 8)[e] if e < 5 else 3 * e - 5

        def down_at(e):
            return (4, 5, None, None)[e] if e < 4 else 3 * e if e < NE - 1 else 3 * NE - 5

        def slot(n):
            return ring[:, n % RING, :].rearrange("p (k n) -> p k n", k=KC)

        def w_cols(w, c):
            return w[:, c:c + 512].rearrange("(k p) n -> p k n", p=P)

        block = ctx.enter_context(nc.Block())

        @block.sync
        def _(sp):
            def wait_released(n):
                if n < BASE_M0:
                    n -= BASE_A
                    last = (("qk", 4 * n + 3) if n < 2 else ("qk2", 4 * n - 5) if n < 4 else ("vch", 4 * n - 13) if n < 6
                            else ("zz", 2 * n - 11) if n < 8 else ("ya", n - 6))
                    wait_full(sp, *last)
                elif n < BASE_B or n >= BASE_M1:
                    layer, base = (0, BASE_M0) if n < BASE_B else (1, BASE_M1)
                    for e in range(NE):
                        if e != OWN and n - base in (gate_at(e), gate_at(e) + 1):
                            sp.wait_ge(moe_sems[layer]["gu_done"], e + 1)
                        if n - base == down_at(e):
                            sp.wait_ge(moe_sems[layer]["down_done"], e + 1)
                else:
                    n -= BASE_B
                    last = (("q", 3), ("k", 3), ("v", 1), ("q2", 3), ("k2", 3), ("v2", 1), ("yb", 2), ("yb", 3))[n]
                    wait_full(sp, *last)

            def stream(n, src):
                if n >= RING:
                    wait_released(n - RING)
                sp.dma_start(slot(n), src).then_inc(ring_loaded[n % RING], 16)

            sp.dma_start(xN[:, :, :], x[0].rearrange("(t p) d -> p t d", p=P)).then_inc(ld_x, 16)
            for n in range(8):
                stream(BASE_A + n, w_cols(a_w_in[0], 512 * n))
            for n in range(2):
                stream(BASE_A + 8 + n, w_cols(a_w_out[0], 512 * n))

            def expert_load(layer, n, e, part):
                w = (moe_w_gate, moe_w_up, moe_w_down)[part]
                src = w[layer, bass.ds(e, 1)].rearrange("o (k p) n -> p (o k) n", p=P)
                dst = ring[:, n % RING, :].rearrange("p (k n) -> p k n", k=(KC, KC, FE // P)[part])
                sp.dma_start(dst, src).then_inc(ring_loaded[n % RING], 16)

            def in_order(n, parts):
                return parts if len(parts) == 1 or n % RING < RING - 1 else parts[::-1]

            def experts(layer, base):
                s = moe_sems[layer]

                def first_use(e, *parts):
                    n = base + (gate_at(e) if parts[0] < 2 else down_at(e))
                    for i, part in enumerate(in_order(n, parts)):
                        wait_released(n + i - RING)
                        expert_load(layer, n + i, e, part)

                def own_expert(part, at_, signal_):
                    w = (moe_w_gate, moe_w_up, moe_w_down)[part]
                    sp.dma_start(ovw[:, at_, :].rearrange("p (k n) -> p k n", k=(KC, KC, FE // P)[part]),
                                 w[layer, OWN].rearrange("(k p) n -> p k n", p=P)).then_inc(signal_, 16)

                def spare_down(half, dst):
                    w = moe_w_down[layer, SPARE, half * 2 * P:(half + 1) * 2 * P, :]
                    sp.dma_start(dst, w.rearrange("(k p) n -> p k n", p=P)).then_inc(ld_spare, 16)

                first_use(0, 0, 1)
                if layer == 0:
                    first_use(1, 0, 1)
                    for i in range(2):
                        wait_emptied(sp, "o1", i)
                else:
                    wait_full(sp, "av", 2 * HB - 1)
                own_expert(0, 1, ld_own_gu)
                own_expert(1, 2, ld_own_gu)
                for i in range(4):
                    wait_full(sp, "oTb" if layer else "oTa", i)
                spare_down(0, oN[:, :, :])
                if layer == 1:
                    first_use(1, 0, 1)
                first_use(0, 2)
                first_use(1, 2)
                if layer == 0:
                    for i in range(4):
                        wait_full(sp, "ya", i)
                    sp.wait_ge(Sm["first_normed"], 2)
                    sp.wait_ge(Sm["o_normed"], 2)
                own_expert(2, 0, ld_own_down)
                wait_full(sp, f"lg{layer}")
                spare_down(1, xTh)
                first_use(3, 0, 1)
                first_use(4, 0, 1)
                for e in (5, 6):
                    first_use(e, 0, 1)
                    first_use(e - 1, 2)
                with sp.Fori(3, NE // 2 - 1) as pair:
                    for j in range(2):
                        e = 2 * pair + 1 + j
                        n = base + gate_at(7 + j)
                        for i, part in enumerate(in_order(n, (0, 1))):
                            sp.wait_ge(s["gu_done"], e - 1)
                            expert_load(layer, n + i, e, part)
                        sp.wait_ge(s["down_done"], e - 2)
                        expert_load(layer, n + 2, e - 1, 2)
                first_use(NE - 1, 0, 1)
                first_use(NE - 2, 2)
                first_use(NE - 1, 2)

            experts(0, BASE_M0)
            for half in range(2):
                stream(BASE_B + 3 * half, w_cols(b_w_q[0], 512 * half))
                stream(BASE_B + 3 * half + 1, w_cols(b_w_kv, 512 * half))
                stream(BASE_B + 3 * half + 2, w_cols(b_w_kv, 1024 + 512 * half))
            for n in range(2):
                stream(BASE_B + 6 + n, w_cols(b_w_out[0], 512 * n))
            experts(1, BASE_M1)
            for tt in range(TT):
                sp.wait_ge(Sm["x_ready"], 12 + tt + 1)
                sp.wait_ge(Sm["out_ready"], tt + 1)
                sp.dma_start(out[0, tt * P:(tt + 1) * P, :], xN[:, tt, :]).then_inc(st_out, 16)
            sp.wait_ge(st_out, 16 * TT)

        @block.tensor
        def _(pe):
            def stay_warm(n, b):
                for _ in range(n):
                    pe.matmul(bank[b][:, 0:256], ident, cst[:, 0:256], start=True, stop=True)

            def transposes(name, i, parts):
                before_fill(pe, name, i)
                for j, src in enumerate(parts):
                    last = pe.transpose(ps(name, i)[:, j * P:(j + 1) * P], src, ident)
                filled(last, name, i)

            def transpose_x(r):
                if r:
                    before_fill(pe, f"xT{r}", 3)
                    stay_warm((6, 12, 6)[r - 1], 7)
                    for i in range(4):
                        wait_emptied(pe, ("ya", "y0", "yb")[r - 1], i)
                for i in range(4):
                    transposes(f"xT{r}", i, [xN[:, tt, kc * P:(kc + 1) * P] for kc in (2 * i, 2 * i + 1) for tt in range(TT)])

            def xT_made(r):
                for i in range(4):
                    wait_emptied(pe, f"xT{r}", i)

            def columns(name, i, n, ct):
                before_fill(pe, name, i)
                for kc in range(KC):
                    last = pe.matmul(ps(name, i)[:, 0:T], slot(n)[:, kc, ct * P:(ct + 1) * P], xT[:, kc, :],
                                     start=kc == 0, stop=kc == KC - 1)
                filled(last, name, i)
                return last

            def rows(name, i, n, tt):
                before_fill(pe, name, i)
                for kc in range(KC):
                    last = pe.matmul(ps(name, i)[:, :], xT[:, kc, tt * P:(tt + 1) * P], slot(n)[:, kc, :],
                                     start=kc == 0, stop=kc == KC - 1)
                filled(last, name, i)
                return last

            pe.wait_ge(ld_x, 16)
            pe.wait_ge(ld_id, 16)
            transpose_x(0)
            pe.wait_ge(ld_cw, 16)
            before_fill(pe, "cw")
            filled(pe.transpose(ps("cw")[:, 0:96], cwr[0:96, :], ident[0:96, 0:96]), "cw")
            xT_made(0)

            def ssq(t):
                pe.wait_ge(Sm["sq_ready"], t + 1)
                for tt in range(TT):
                    at_ = 16 * tt + t
                    last = pe.matmul(ps("ssq")[:, at_:at_ + 1], sq[:, t % 4, tt * P:(tt + 1) * P], ones[:, 0:1],
                                     start=True, stop=True)
                last.then_inc(Sm["sq_used"], 1)

            after_load(pe, 0)
            for ct in range(4):
                columns("qk", ct, 0, ct)
                if ct >= 2:
                    ssq(ct - 2)
            pe.wait_ge(ld_ab, 16)
            before_fill(pe, "ab")
            for tt in range(TT):
                for kc in range(KC):
                    last = pe.matmul(ps("ab")[:, tt * 16:(tt + 1) * 16], xT[:, kc, tt * P:(tt + 1) * P], wab[:, kc, :],
                                     start=kc == 0, stop=kc == KC - 1)
            filled(last, "ab")
            after_load(pe, 1)
            for ct in range(4):
                columns("qk", 4 + ct, 1, ct)
                ssq(2 + ct)
            gall = g[:, :, :].rearrange("p a b -> p (a b)")

            def sum_gates():
                pe.wait_ge(ld_cst, 16)
                pe.wait_ge(Sm["gates_ready"], 1)
                before_fill(pe, "cum")
                pe.matmul(ps("cum")[:, 0:16], tri, gall, start=True, stop=True)
                filled(pe.matmul(ps("cum")[:, 16:32], ones, gall, start=True, stop=True), "cum")
                for i in range(4):
                    before_fill(pe, "grow", i)
                    for j in range(4):
                        ch = 4 * i + j
                        last = pe.matmul(ps("grow", i)[:, j * P:(j + 1) * P], gall[:, ch:ch + 1].to_broadcast([P, P]), tri,
                                         start=True, stop=True)
                    filled(last, "grow", i)

            for n in range(2, 4):
                after_load(pe, n)
                for ct in range(4):
                    columns("qk2", 4 * (n % 2) + ct, n, ct)
                    ssq(4 * n - 2 + ct)
                    if n == 2 and ct == 1:
                        sum_gates()

            pe.wait_ge(ld_lnr, 32)
            before_fill(pe, "lnc")
            filled(pe.transpose(ps("lnc")[:, 0:64], lnr[0:64, :], ident[0:64, 0:64]), "lnc")

            def raw_products(name, q0, b):
                before_fill(pe, name, b)
                for j in range(4):
                    h, t0 = 4 * (b % 2) + j, (b // 2) * P
                    last = pe.matmul(ps(name, b)[:, j * P:(j + 1) * P], qkT[:, 8 + h, t0:t0 + P],
                                     qkT[:, q0 + h, t0:t0 + P], start=True, stop=True)
                filled(last, name, b)

            for t in range(8):
                n = 4 + t // 4
                after_load(pe, n)
                columns("vch", t, n, t % 4)
                if t < 2:
                    ssq(14 + t)
                    if t == 1:
                        pe.wait_ge(Sm["sq_used"], 16)
                        pe.sem_inc(full[where["ssq", 0][0]], 1)
                elif t in (4, 5):
                    raw_products("kk", 8, 2 * (t - 4))
                    raw_products("kk", 8, 2 * (t - 4) + 1)

            def turn_T(b):
                pe.wait_ge(Sm["T_init"], b + 1)
                transposes("ttr", b, [Ti[:, 4 * b + j, :] for j in range(4)])

            def turn_v(i):
                tt, hg = i // 2, i % 2
                pe.wait_ge(Sm["silu_done"], 24)
                transposes("vtr", i, [vT[:, 4 * hg + j, tt * P:(tt + 1) * P] for j in range(4)])

            for i in range(4):
                n, tt = 6 + i // 2, i % 2
                after_load(pe, n)
                rows("zz", i, n, tt)
                if i == 0:
                    for b in range(4):
                        turn_v(b)
                elif i == 1:
                    for b in range(4):
                        turn_T(b)
                elif i == 2:
                    pe.wait_ge(Sm["dm_ready"], 4)
                    for b in range(4):
                        transposes("dtr", b, [Dm[:, 4 * b + j, :] for j in range(4)])
            for b in range(4):
                raw_products("kq", 0, b)
            for i in range(2):
                transposes("ktr", i, [qkT[:, 8 + 4 * i + j, 0:P] for j in range(4)])
            for lev in range(1, 7):
                for b in range(4):
                    pe.wait_ge(Sm["L_ready"], 4 * (lev - 1) + b + 1)
                    wait_emptied(pe, f"tt{lev - 1}" if lev > 1 else "ttr", b)
                    before_fill(pe, f"p{lev}", b)
                    for j in range(4):
                        m = 4 * b + j
                        last = pe.matmul(ps(f"p{lev}", b)[:, j * P:(j + 1) * P], Dm[:, m, :], TiT[:, m, :],
                                         start=True, stop=True)
                    filled(last, f"p{lev}", b)
                for b in range(4):
                    wait_emptied(pe, f"p{lev}", b)
                    if lev > 1:
                        wait_emptied(pe, f"t{lev - 1}", b)
                    if lev < 6:
                        before_fill(pe, f"t{lev}", b)
                        for j in range(4):
                            m = 4 * b + j
                            last = pe.matmul(ps(f"t{lev}", b)[:, j * P:(j + 1) * P], PT[:, m, :], Ti[:, m, :],
                                             start=True, stop=True)
                        filled(last, f"t{lev}", b)
                    before_fill(pe, f"tt{lev}", b)
                    for j in range(4):
                        m = 4 * b + j
                        last = pe.matmul(ps(f"tt{lev}", b)[:, j * P:(j + 1) * P], Ti[:, m, :], PT[:, m, :],
                                         start=True, stop=True)
                    filled(last, f"tt{lev}", b)

            def by_head(name, i, lhsT, rhs):
                before_fill(pe, name, i)
                for j in range(4):
                    h = 4 * i + j
                    last = pe.matmul(ps(name, i)[:, j * P:(j + 1) * P], lhsT(h), rhs(h), start=True, stop=True)
                filled(last, name, i)

            before_fill(pe, "o0", 0)
            stay_warm(3, 4)
            for b in range(4):
                wait_emptied(pe, "tt6", b)
                wait_emptied(pe, "kq", b)
                wait_emptied(pe, "vtr", b)
            for i in range(2):
                by_head("vn0", i, lambda h: TiT[:, h, :], lambda h: vN[:, 0, h * P:(h + 1) * P])
            for i in range(2):
                wait_emptied(pe, "vn0", i)
                wait_emptied(pe, "ktr", i)
                by_head("o0", i, lambda h: QK[:, h, :], lambda h: vN[:, 0, h * P:(h + 1) * P])
                by_head("s1", i, lambda h: kN[:, h, :], lambda h: vN[:, 0, h * P:(h + 1) * P])
            for i in range(2):
                wait_emptied(pe, "s1", i)
                by_head("ks", i, lambda h: qkT[:, 8 + h, P:T], lambda h: S[:, h, :])
                by_head("qs", i, lambda h: qkT[:, h, P:T], lambda h: S[:, h, :])
            for i in range(2):
                pe.wait_ge(Sm["r1_ready"], i + 1)
                by_head("vn1", i, lambda h: TiT[:, 8 + h, :], lambda h: vN[:, 1, h * P:(h + 1) * P])
            for i in range(2):
                wait_emptied(pe, "vn1", i)
                by_head("o1", i, lambda h: QK[:, 8 + h, :], lambda h: vN[:, 1, h * P:(h + 1) * P])

            def residual(name, which=range(4), alone=False):
                for i in which:
                    tt, n = i // 2, i % 2
                    before_fill(pe, name, i)
                    pe.matmul(ps(name, i)[:, :], alphaI, xN[:, tt, n * 512:(n + 1) * 512], start=True, stop=alone)

            def project_out(base, src, oname):
                residual(f"y{oname}")
                before_fill(pe, "oTa", 3)
                for i in range(4):
                    if i % 2 == 0:
                        stay_warm((3, 1)[i // 2], 7)
                    pe.wait_ge(Sm["first_normed"], 1 + i // 2)
                    pe.wait_ge(Sm["o_normed"], 1 + i // 2)
                    transposes(f"oT{oname}", i, [oN[:, tt, kc * P:(kc + 1) * P] for kc in (2 * i, 2 * i + 1) for tt in range(TT)])
                for i in range(4):
                    wait_emptied(pe, f"oT{oname}", i)
                for n in range(2):
                    after_load(pe, base + n)
                    for tt in range(TT):
                        i = 2 * tt + n
                        for kc in range(KC):
                            last = pe.matmul(ps(f"y{oname}", i)[:, :], src[:, kc, tt * P:(tt + 1) * P],
                                             slot(base + n)[:, kc, :], start=False, stop=kc == KC - 1)
                        last.then_inc(full[where[f"y{oname}", i][0]], 1)

            project_out(BASE_A + 8, oT, "a")

            def route(layer):
                r = 1 + 2 * layer
                transpose_x(r)
                pe.wait_ge(ld_par, 16 * 3)
                lg = f"lg{layer}"
                before_fill(pe, lg)
                for tt in range(TT):
                    for kc in range(KC):
                        if tt == 0 and kc % 2 == 0:
                            wait_emptied(pe, f"xT{r}", kc // 2)
                        last = pe.matmul(ps(lg)[:, tt * NE:(tt + 1) * NE], xT[:, kc, tt * P:(tt + 1) * P], rw[:, kc, :],
                                         start=kc == 0, stop=kc == KC - 1)
                filled(last, lg)
                stay_warm(4, 7)
                pe.wait_ge(Sm["x_ready"], 8 * layer + 2)
                residual(f"y{layer}", range(2), alone=True)
                pe.wait_ge(Sm["sel_ready"], layer + 1)
                rk = f"rk{layer}"
                before_fill(pe, rk)
                sel = rt[:, 0:2 * NE]
                pe.matmul(ps(rk)[:, 0:NE], tris, sel[:, 0:NE], start=True, stop=True)
                pe.matmul(ps(rk)[:, NE:2 * NE], ones, sel[:, 0:NE], start=True, stop=False)
                filled(pe.matmul(ps(rk)[:, NE:2 * NE], tris, sel[:, NE:2 * NE], start=False, stop=True), rk)
                pe.wait_ge(Sm["x_ready"], 8 * layer + 3)
                residual(f"y{layer}", (2,), alone=True)

            def experts(layer, base):
                s = moe_sems[layer]

                def weights(n, pair):
                    pe.wait_ge(ring_loaded[n % RING], loads(n) + 16 * pair)

                def tokens(half, to=XG):
                    for kc in range(4 * half, 4 * half + 4):
                        for tt in range(TT):
                            last = pe.matmul(to[:, (kc % 4) * P:(kc % 4 + 1) * P], xN[:, tt, kc * P:(kc + 1) * P],
                                             Pb[:, tt, :], start=tt == 0, stop=tt == TT - 1)
                    last.then_inc(s["gathered"], 1)

                def gate_up(e, par, n, pair, own=False):
                    if par == 0:
                        pe.wait_ge(s["xe_ready"], e + 2)
                    if own:
                        pe.wait_ge(ld_own_gu, 32 * (layer + 1))
                        w = ovw[:, 1:3, :]
                    else:
                        weights(n, pair)
                        weights(n + 1, pair)
                        w = ring[:, n % RING:n % RING + 2, :] if n % RING < RING - 1 else ring[:, 0:RING:RING - 1, :]
                    w = w.rearrange("p s (k n) -> p s k n", k=KC)
                    for kc in range(KC):
                        for half in range(2):
                            last = pe.matmul(GU[par][64 * half:64 * half + 64, :], xeT[:, kc, par * CAP:(par + 1) * CAP],
                                             w[:, :, kc, 256 * half:256 * half + 256], start=kc == 0, stop=kc == KC - 1)
                    last.then_inc(s["gu_done"], 1)

                def turn_hidden(e, par, pair):
                    pe.wait_ge(s["h_ready"], e + 1)
                    for c in range(2):
                        last = pe.transpose(GU[par][:, c * P:(c + 1) * P], hN[:, par, c * P:(c + 1) * P], ident)
                    if par == 1:
                        pe.wait_ge(s["G_built"], pair + 1)
                        for tt in range(TT):
                            last = pe.transpose(GU[1][:, 256 + tt * P:256 + (tt + 1) * P], G2[:, tt, :], ident)
                    last.then_inc(s["ht_done"], 1)

                def down(e, par, n, pair, own=False, spare=False):
                    pe.wait_ge(s["ht_ready"], e + 1)
                    if own:
                        pe.wait_ge(ld_own_down, 16 * (layer + 1))
                        dn = ovw[:, 0, :]
                    elif spare:
                        pe.wait_ge(ld_spare, 32 * (layer + 1))
                    else:
                        weights(n, pair)
                        dn = ring[:, n % RING, :]
                    if not spare:
                        dn = dn.rearrange("p (k n) -> p k n", k=FE // P)
                    for fc in range(4):
                        lhs = hTG[:, par, (fc % 2) * P + (fc // 2) * CAP:(fc % 2) * P + (fc // 2) * CAP + CAP]
                        w = dn[:, fc, :] if not spare else oN[:, fc, :] if fc < 2 else xTh[:, fc - 2, :]
                        for c in range(2):
                            last = pe.matmul(YD[64 * c:64 * c + 64, :], lhs, w[:, c * 512:(c + 1) * 512],
                                             start=fc == 0, stop=fc == 3)
                    last.then_inc(s["down_done"], 1)

                def scatter(pair):
                    pe.wait_ge(s["ys_ready"], 4 * pair + 4)
                    for i in range(4):
                        tt, c = i // 2, i % 2
                        last = pe.matmul(Y[i][:, :], hTG[:, 1, 256 + tt * P:256 + (tt + 1) * P], ys[:, c * 512:(c + 1) * 512],
                                         start=False, stop=True, skip_group_check=True)
                    last.then_inc(s["scattered"], 1)

                def two_experts(pair, first=False, last=False):
                    a = 2 * pair
                    k, rounds = (a, 0) if isinstance(pair, int) else (4, pair - 2)
                    gate_up(a + 1, 1, base + gate_at(k + 1), rounds)
                    turn_hidden(a, 0, pair)
                    if not last:
                        pe.wait_ge(s["P_built"], pair + 2)
                        tokens(0)
                    if not first:
                        scatter(pair - 1)
                    if not last:
                        pe.wait_ge(s["xe_ready"], a + 3)
                        tokens(1)
                    down(a, 0, base + (down_at(k) or 0), rounds, own=k == OWN)
                    turn_hidden(a + 1, 1, pair)
                    if not last:
                        gate_up(a + 2, 0, base + (gate_at(k + 2) or 0), rounds, own=k + 2 == OWN)
                    pe.wait_ge(s["ys_ready"], 4 * pair + 2)
                    down(a + 1, 1, base + (down_at(k + 1) or 0), rounds, spare=k + 1 == SPARE)

                stay_warm(2, 7)
                pe.wait_ge(s["P_built"], 1)
                pe.wait_ge(Sm["x_ready"], 8 * layer + 4)
                tokens(0)
                tokens(1, to=YD)
                residual(f"y{layer}", (3,), alone=True)
                gate_up(0, 0, base, 0)
                wait_emptied(pe, f"rk{layer}")
                two_experts(0, first=True)
                two_experts(1)
                with pe.Fori(2, NE // 2 - 1) as pair:
                    two_experts(pair)
                two_experts(NE // 2 - 1, last=True)
                scatter(NE // 2 - 1)
                pe.wait_ge(s["scattered"], NE // 2)

            def overflow(layer):
                s = moe_sems[layer]
                pe.wait_ge(Sm["flag_ready"], layer + 1)
                more = pe.value_load(flag[P - 1:P, 0:1], min_val=0, max_val=T)
                with pe.If(more > CAP):
                    pe.sem_inc(s["o_done"], 1)
                    with pe.Fori(1, PASSES) as ps_:
                        with pe.Fori(0, NE) as ei:
                            it = (ps_ - 1) * NE + ei
                            pe.wait_ge(s["o_P"], it + 1)
                            for kc in range(KC):
                                for tt in range(TT):
                                    last = pe.matmul(XG[:, kc * CAP:(kc + 1) * CAP], xN[:, tt, kc * P:(kc + 1) * P],
                                                     Pb[:, tt, 0:CAP], start=tt == 0, stop=tt == TT - 1)
                            last.then_inc(s["o_gathered"], 1)
                            pe.wait_ge(s["o_xe"], it + 1)
                            pe.wait_ge(s["o_loaded"], 48 * it + 48)
                            wv = ovw[:, 1:3, :].rearrange("p s (k n) -> p s k n", k=KC)
                            for kc in range(KC):
                                for half in range(2):
                                    last = pe.matmul(GU[0][64 * half:64 * half + 64, :], xo[:, kc, :],
                                                     wv[:, :, kc, 256 * half:256 * half + 256], start=kc == 0, stop=kc == KC - 1)
                            last.then_inc(s["o_gu"], 1)
                            pe.wait_ge(s["o_h"], it + 1)
                            for c in range(2):
                                pe.transpose(GU[0][:, c * P:(c + 1) * P], hN[:, 0, c * P:(c + 1) * P], ident)
                            for tt in range(TT):
                                last = pe.transpose(GU[0][:, 256 + tt * P:256 + (tt + 1) * P], G2[:, tt, :], ident)
                            last.then_inc(s["o_ht"], 1)
                            pe.wait_ge(s["o_htr"], it + 1)
                            dn = ovw[:, 0, :].rearrange("p (k n) -> p k n", k=FE // P)
                            for fc in range(4):
                                lhs = hTG[:, 0, (fc % 2) * P + (fc // 2) * CAP:(fc % 2) * P + (fc // 2) * CAP + CAP]
                                for n in range(2):
                                    last = pe.matmul(YD[64 * n:64 * n + 64, :], lhs, dn[:, fc, n * 512:(n + 1) * 512],
                                                     start=fc == 0, stop=fc == 3)
                            last.then_inc(s["o_down"], 1)
                            pe.wait_ge(s["o_ys"], 2 * it + 2)
                            for i in range(4):
                                tt, n = i // 2, i % 2
                                last = pe.matmul(Y[i][:, :], hTG[0:CAP, 0, 256 + tt * P:256 + (tt + 1) * P],
                                                 ys[0:CAP, n * 512:(n + 1) * 512], start=False, stop=True,
                                                 skip_group_check=True)
                            last.then_inc(s["o_done"], 1)
                    pe.wait_ge(s["o_done"], NE * (PASSES - 1) + 1)
                for i in range(4):
                    pe.sem_inc(full[where[f"y{layer}", i][0]], 1)

            route(0)
            experts(0, BASE_M0)
            overflow(0)

            transpose_x(2)
            before_fill(pe, "q", 3)
            stay_warm(3, 0)
            xT_made(2)
            after_load(pe, BASE_B)
            for ct in range(4):
                columns("q", ct, BASE_B, ct)
            pe.wait_ge(ld_att, 16 * 4)
            before_fill(pe, "brow")
            filled(pe.matmul(ps("brow")[0:HB, 0:REV], rbT[0:BUCKETS, :], oh[0:BUCKETS, :], start=True, stop=True), "brow")
            after_load(pe, BASE_B + 1)
            for ct in range(4):
                columns("k", ct, BASE_B + 1, ct)
            after_load(pe, BASE_B + 2)
            for tt in range(TT):
                rows("v", tt, BASE_B + 2, tt)
            pe.wait_ge(ld_bias, 16)
            for i in range(4):
                before_fill(pe, "bias", i)
                filled(pe.matmul(ps("bias", i)[:, :], reverse, braw[:, 2 * i:2 * i + 2, :], start=True, stop=True), "bias", i)

            def scores(i):
                h, qt = i // 2, i % 2
                before_fill(pe, "sc", i)
                if qt == 0:
                    wait_emptied(pe, "q" if h < 4 else "q2", h % 4)
                    wait_emptied(pe, "k" if h < 4 else "k2", h % 4)
                for half in range(2):
                    last = pe.matmul(ps("sc", i)[:, half * T:half * T + (qt + 1) * P], qz[:, h, half, qt * P:(qt + 1) * P],
                                     kT[:, h, 0:(qt + 1) * P], start=True, stop=True)
                filled(last, "sc", i)

            def turn_attention(i):
                qt = i % 2
                pe.wait_ge(Sm["at_ready"], i + 1)
                before_fill(pe, "atT", i)
                for kt in range(qt + 1):
                    last = pe.transpose(ps("atT", i)[:, kt * P:(kt + 1) * P], at[:, i % 2, kt * P:(kt + 1) * P], ident)
                filled(last, "atT", i)

            def values(i):
                h, qt = i // 2, i % 2
                wait_emptied(pe, "atT", i)
                if i % (ITEMS // 2) < TT:
                    wait_emptied(pe, "v" if i < ITEMS // 2 else "v2", i % 2)
                before_fill(pe, "av", i)
                for kt in range(qt + 1):
                    last = pe.matmul(ps("av", i)[:, 0:P], atT[:, i % 2, kt, :], vB[:, kt, h * P:(h + 1) * P],
                                     start=kt == 0, stop=kt == qt)
                filled(last, "av", i)

            def turn_heads(i):
                pe.wait_ge(Sm["o_normed"], 3 + i // 2)
                transposes("oTb", i, [oN[:, tt, kc * P:(kc + 1) * P] for kc in (2 * i, 2 * i + 1) for tt in range(TT)])

            def half_rows(name, tt, n, half):
                if half == 0:
                    before_fill(pe, name, tt)
                for kc in range(4 * half, 4 * half + 4):
                    last = pe.matmul(ps(name, tt)[:, :], xT[:, kc, tt * P:(tt + 1) * P], slot(n)[:, kc, :],
                                     start=kc == 0, stop=kc == KC - 1)
                if half:
                    filled(last, name, tt)

            def half_out(i, half):
                tt, n = i // 2, i % 2
                after_load(pe, BASE_B + 6 + n)
                for j in (0, 1):
                    wait_emptied(pe, "oTb", 2 * half + j)
                for kc in range(4 * half, 4 * half + 4):
                    last = pe.matmul(ps("yb", i)[:, :], kT[:, kc, tt * P:(tt + 1) * P], slot(BASE_B + 6 + n)[:, kc, :],
                                     start=False, stop=kc == KC - 1)
                if half:
                    last.then_inc(full[where["yb", i][0]], 1)

            for k in range(ITEMS + 2):
                if k < ITEMS:
                    scores(k)
                if k < 8 and k % 2 == 0:
                    after_load(pe, BASE_B + 3)
                    columns("q2", k // 2, BASE_B + 3, k // 2)
                elif k < 8:
                    after_load(pe, BASE_B + 4)
                    columns("k2", k // 2, BASE_B + 4, k // 2)
                elif k < 12:
                    after_load(pe, BASE_B + 5)
                    half_rows("v2", k // 2 - 4, BASE_B + 5, k % 2)
                elif k == 12:
                    pe.wait_ge(Sm["x_ready"], 8)
                    residual("yb", (0, 1))
                elif k == 13:
                    residual("yb", (2, 3))
                    for i in range(2):
                        turn_heads(i)
                elif k >= 14:
                    half_out(k - 14, 0)
                if 1 <= k <= ITEMS:
                    turn_attention(k - 1)
                if k >= 2:
                    values(k - 2)
            before_fill(pe, "oTb", 2)
            stay_warm(6, 4)
            for i in (2, 3):
                turn_heads(i)
            before_fill(pe, "xT3", 2)
            stay_warm(2, 6)
            for i in range(4):
                half_out(i, 1)
            route(1)
            experts(1, BASE_M1)
            overflow(1)

        @block.scalar
        def _(act):
            def go(out_, in_, f, **kw):
                return act.activation(out_, in_, f, **kw)

            act.dma_start(cst[:, 0:2 * P], consts[:, 0:2 * P]).then_inc(ld_id, 16)
            act.dma_start(cwr[0:96, :], a_conv[0].rearrange("i (t c) -> (i t) c", c=P)).then_inc(ld_cw, 16)
            act.dma_start(wab[:, :, :], a_w_in[0, :, 4096:4112].rearrange("(k p) n -> p k n", p=P)).then_inc(ld_ab, 16)
            for dst, src in ((alog, a_A_log), (dtb, a_dt_bias)):
                act.dma_start(dst, src.to_broadcast([P, HA])).then_inc(ld_gates, 16)
            act.wait_ge(ld_x, 16)
            act.dma_start(cst[:, 2 * P:], consts[:, 2 * P:]).then_inc(ld_cst, 16)
            act.dma_start(lnr[0:32, :], ln_w.rearrange("l k (t c) -> (l k t) c", c=P)).then_inc(ld_lnr, 16)
            act.dma_start(lnr[32:64, :], ln_b.rearrange("l k (t c) -> (l k t) c", c=P)).then_inc(ld_lnr, 16)
            act.dma_start(nw, a_norm_w.to_broadcast([P, P])).then_inc(ld_par, 16)
            act.dma_start(rb, router_b.rearrange("(a n) -> a n", a=1).to_broadcast([P, NE])).then_inc(ld_par, 16)
            act.dma_start(rw[:, :, :], router_w.rearrange("(k p) n -> p k n", p=P)).then_inc(ld_par, 16)

            def xT_half(r):
                for i in (0, 2):
                    wait_full(act, f"xT{r}", i)
                    if r == 0:
                        emptied(go(xT[:, 2 * i:2 * i + 2, :], ps(f"xT{r}", i).rearrange("p (a b) -> p a b", a=2), ACT.Copy),
                                f"xT{r}", i)
                        continue
                    for kc in (2 * i, 2 * i + 1):
                        last = go(xT[:, kc, :], ps(f"xT{r}", i)[:, (kc % 2) * T:(kc % 2 + 1) * T], ACT.Identity,
                                  scale=lnc[:, 0, r - 1, kc:kc + 1], bias=lnc[:, 1, r - 1, kc:kc + 1])
                    emptied(last, f"xT{r}", i)

            xT_half(0)
            def silu(t):
                name = ("qk", "qk2", "vch")[t // 8]
                wait_emptied(act, name, t % 8)
                if t < 16:
                    go(qkT[:, t, :], conv[:, t % 4, :], ACT.Silu).then_inc(Sm["silu_done"], 1)
                    if t >= 4:
                        act.wait_ge(Sm["sq_used"], t - 3)
                    act.wait_ge(Sm["silu_done"], t + 1)
                    go(sq[:, t % 4, :], qkT[:, t, :], ACT.Square).then_inc(Sm["sq_ready"], 1)
                else:
                    go(vT[:, t - 16, :], conv[:, t % 4, :], ACT.Silu).then_inc(Sm["silu_done"], 1)

            for t in range(4):
                silu(t)
            act.wait_ge(Sm["gate_abs"], 1)
            in_step(act, go(gt2, gt2, ACT.Exp, scale=-1.0), act_step)
            act.wait_ge(ld_gates, 32)
            go(alog, alog, ACT.Exp)
            go(beta, ab[:, :, HA:2 * HA], ACT.Exp, scale=-1.0)
            go(gt2, gt2, ACT.Ln, bias=1.0).then_inc(Sm["softplus_done"], 1)
            for t in range(4, 10):
                silu(t)
            act.wait_ge(Sm["decay_in"], 1)
            go(eg, gc, ACT.Exp)
            go(kd, kd, ACT.Exp).then_inc(Sm["decay_ready"], 1)
            for i in range(4):
                wait_emptied(act, "grow", i)
                d = Dm[:, 4 * i:4 * i + 4, :]
                go(d, d, ACT.Exp, scale=-1.0).then_inc(Sm["dm_exp"], 1)
            for t in range(10, 18):
                silu(t)
            act.wait_ge(Sm["norm_in"], 1)
            go(fq, r2[:, :, 0:HA], ACT.Sqrt, scale=1.0 / P)
            go(bk, r2[:, :, HA:2 * HA], ACT.Sqrt).then_inc(Sm["norm_root"], 1)
            for t in range(18, 24):
                silu(t)

            def silu_z(i):
                wait_full(act, "zz", i)
                emptied(go(z[:, i % 2, 512 * (i // 2):512 * (i // 2) + 512], ps("zz", i)[:, :], ACT.Silu), "zz", i)

            silu_z(0)
            silu_z(1)
            for b in range(4):
                wait_full(act, "ttr", b)
                emptied(go(TiT[:, 4 * b:4 * b + 4, :], ps("ttr", b).rearrange("p (a b) -> p a b", a=4), ACT.Copy), "ttr", b)
            silu_z(2)
            for b in range(4):
                wait_full(act, "dtr", b)
                emptied(go(QK[:, 4 * b:4 * b + 4, :], ps("dtr", b).rearrange("p (a b) -> p a b", a=4), ACT.Copy), "dtr", b)
            silu_z(3)
            for lev in range(1, 7):
                for b in range(4):
                    if lev > 1:
                        wait_full(act, f"tt{lev - 1}", b)
                    wait_full(act, f"p{lev}", b)
                    emptied(go(PT[:, 4 * b:4 * b + 4, :], ps(f"p{lev}", b).rearrange("p (a b) -> p a b", a=4), ACT.Copy),
                            f"p{lev}", b)
            for i in range(2):
                wait_full(act, "vn0", i)
                emptied(go(vN[:, 0, 512 * i:512 * i + 512], ps("vn0", i)[:, :], ACT.Copy), "vn0", i)
            for i in range(2):
                wait_full(act, "o0", i)
                emptied(go(oN[:, 0, 512 * i:512 * i + 512], ps("o0", i)[:, :], ACT.Copy), "o0", i)
            def new_v1(i):
                wait_full(act, "vn1", i)
                emptied(go(vN[:, 1, 512 * i:512 * i + 512], ps("vn1", i)[:, :], ACT.Copy), "vn1", i)

            def squares(tt):
                for hg in range(2):
                    wait_emptied(act, f"o{tt}", hg)
                    if tt:
                        act.wait_ge(Sm["o_mean"], 2)
                    go(xT[:, 4 + 2 * hg:6 + 2 * hg, :], oN[:, tt, 512 * hg:512 * hg + 512].rearrange("p (a b) -> p a b", a=2),
                       ACT.Square).then_inc(Sm["o_squared"], 1)

            def roots(tt):
                for hg in range(2):
                    act.wait_ge(Sm["o_mean"], 2 * tt + hg + 1)
                    m4 = ms[:, tt, 4 * hg:4 * hg + 4]
                    go(m4, m4, ACT.Sqrt, bias=RMS_EPS).then_inc(Sm["o_root"], 1)

            def layer_norm(r, y):
                for tt in range(TT):
                    act.wait_ge(Sm["ln_var"], 2 * r + tt + 1)
                    go(rstd[:, tt:tt + 1], mv[:, tt, 1:2], ACT.Sqrt, bias=LN_EPS).then_inc(Sm["ln_root"], 1)
                    act.wait_ge(Sm["ln_scale"], 2 * r + tt + 1)
                    emptied(go(xN[:, tt, 0:512], ps(y, 2 * tt)[:, :], ACT.Identity,
                               scale=rstd[:, tt:tt + 1], bias=nmr[:, tt:tt + 1]), y, 2 * tt)

            def experts(layer):
                s = moe_sems[layer]

                def tokens(half, count):
                    act.wait_ge(s["gathered"], count)
                    go(xeT[:, 4 * half:4 * half + 4, :], XG[:, :].rearrange("p (a b) -> p a b", a=4), ACT.Copy)\
                        .then_inc(s["xe_ready"], 1)

                xT_half(1 + 2 * layer)
                wait_emptied(act, f"lg{layer}")
                for tt in range(TT):
                    last = go(rt[:, 64 + NE * tt:64 + NE * (tt + 1)], rt[:, 32 + NE * tt:32 + NE * (tt + 1)], ACT.Exp,
                              scale=-1.0, bias=rt[:, 224 + tt:225 + tt])
                last.then_inc(Sm["exp_done"], 1)
                def silu_gate(e, par):
                    act.wait_ge(s["gu_done"], e + 1)
                    go(sg[:, par, :], GU[par][:, 0:256], ACT.Silu).then_inc(s["sg_ready"], 1)

                def result(e, par):
                    act.wait_ge(s["down_done"], e + 1)
                    go(ys[CAP * par:CAP * par + CAP, 0:512], YD[0:CAP, :], ACT.Copy).then_inc(s["ys_ready"], 1)

                def two_experts(pair, last=False):
                    a = 2 * pair
                    silu_gate(a + 1, 1)
                    if not last:
                        tokens(0, a + 3)
                        tokens(1, a + 4)
                    result(a, 0)
                    if not last:
                        silu_gate(a + 2, 0)
                    result(a + 1, 1)

                tokens(0, 1)
                silu_gate(0, 0)
                with act.Fori(0, NE // 2 - 1) as pair:
                    two_experts(pair)
                two_experts(NE // 2 - 1, last=True)

                act.wait_ge(Sm["flag_ready"], layer + 1)
                more = act.value_load(flag[P - 1:P, 0:1], min_val=0, max_val=T)
                with act.If(more > CAP):
                    with act.Fori(1, PASSES) as ps_:
                        with act.Fori(0, NE) as ei:
                            it = (ps_ - 1) * NE + ei
                            act.wait_ge(s["o_done"], it + 1)
                            for j, w in enumerate((moe_w_down, moe_w_gate, moe_w_up)):
                                act.dma_start(ovw[:, j, :].rearrange("p (k n) -> p k n", k=(FE // P, KC, KC)[j]),
                                              w[layer, bass.ds(ei, 1)].rearrange("o (k p) n -> p (o k) n", p=P))\
                                    .then_inc(s["o_loaded"], 16)
                            act.wait_ge(s["o_gathered"], it + 1)
                            go(xo, XG[:, :].rearrange("p (a b) -> p a b", a=KC), ACT.Copy).then_inc(s["o_xe"], 1)
                            act.wait_ge(s["o_gu"], it + 1)
                            go(sg[:, 0, :], GU[0][:, 0:256], ACT.Silu).then_inc(s["o_sg"], 1)
                            act.wait_ge(s["o_down"], it + 1)
                            go(ys[0:CAP, 0:512], YD[0:CAP, :], ACT.Copy).then_inc(s["o_ys"], 1)

            squares(0)
            for i in range(2):
                new_v1(i)
            roots(0)
            squares(1)
            roots(1)
            for i in (0, 2):
                wait_full(act, "oTa", i)
                emptied(go(oT[:, 2 * i:2 * i + 2, :], ps("oTa", i).rearrange("p (a b) -> p a b", a=2), ACT.Copy), "oTa", i)
            layer_norm(0, "ya")
            experts(0)
            layer_norm(1, "y0")

            act.dma_start(rbT[0:BUCKETS, :], rel_bias).then_inc(ld_att, 16)
            act.dma_start(oh[0:BUCKETS, :], buckets).then_inc(ld_att, 16)
            act.dma_start(lam, b_lambda.rearrange("a i d -> a (i d)").to_broadcast([P, 4 * DH]).rearrange("p (a b) -> p a b", a=4))\
                .then_inc(ld_att, 16)
            act.dma_start(nwB, b_subln_w.rearrange("o p -> p o")).then_inc(ld_att, 16)
            xT_half(2)
            act.wait_ge(Sm["qz_zero"], 1)

            def take_q(name, i, h):
                wait_full(act, name, i)
                go(qz[0:DH, h, 0, :], ps(name, i)[0:DH, 0:T], ACT.Copy, scale=DH ** -0.5)
                emptied(go(qz[DH:P, h, 1, :], ps(name, i)[DH:P, 0:T], ACT.Copy, scale=DH ** -0.5), name, i)

            def take_v(name, tt, n):
                wait_full(act, name, tt)
                emptied(go(vB[:, tt, 512 * n:512 * n + 512], ps(name, tt)[:, :], ACT.Copy), name, tt)

            for h in range(4):
                take_q("q", h, h)
            act.wait_ge(Sm["lam_sum"], 1)
            go(lam2, lam2, ACT.Exp).then_inc(Sm["lam_exp"], 1)
            for tt in range(TT):
                take_v("v", tt, 0)

            def exponentials(i):
                w = (i % 2 + 1) * P
                act.wait_ge(Sm["sc_ready"], i + 1)
                for half in range(2):
                    last = go(pa[:, i % 2, half * T:half * T + w], sc[:, i % 2, half * T:half * T + w], ACT.Exp, scale=-1.0,
                              bias=smx[:, i % 2, half:half + 1], accum_out=ssum[:, i % 2, half:half + 1])
                last.then_inc(Sm["p_ready"], 1)

            def take_turned(i):
                qt = i % 2
                wait_full(act, "atT", i)
                emptied(go(atT[:, i % 2, 0:qt + 1, :], ps("atT", i)[:, 0:(qt + 1) * P].rearrange("p (a b) -> p a b", b=P),
                           ACT.Copy), "atT", i)

            def take_values(i):
                h, qt = i // 2, i % 2
                wait_full(act, "av", i)
                emptied(go(oN[:, qt, h * P:(h + 1) * P], ps("av", i)[:, 0:P], ACT.Copy), "av", i)

            def square(i):
                h, qt = i // 2, i % 2
                wait_emptied(act, "av", i)
                ins = go(junk, oN[:, qt, h * P:(h + 1) * P], ACT.Square,
                         accum_out=msB[:, h // 4, 4 * qt + h % 4:4 * qt + h % 4 + 1])
                if i % 8 == 7:
                    ins.then_inc(Sm["o_squared"], 1)

            def root_heads(half):
                act.wait_ge(Sm["o_squared"], 5 + half)
                go(msB[:, half, :], msB[:, half, :], ACT.Sqrt, scale=1.0 / P, bias=RMS_EPS).then_inc(Sm["o_root"], 1)

            def take_heads(i):
                wait_full(act, "oTb", i)
                act.wait_ge(Sm["nwB_ready"], 1)
                emptied(go(kT[:, 2 * i:2 * i + 2, :], ps("oTb", i).rearrange("p (a b) -> p a b", a=2), ACT.Identity,
                           scale=nwB), "oTb", i)

            for k in range(ITEMS + 2):
                if k < ITEMS:
                    exponentials(k)
                if k < 8 and k % 2 == 0:
                    take_q("q2", k // 2, 4 + k // 2)
                elif k in (9, 11):
                    take_v("v2", (k - 9) // 2, 1)
                elif k == 10:
                    root_heads(0)
                elif k == ITEMS:
                    go(mask(C_LEV + 1)[:, 0:1], ones[:, 0:1], ACT.Sqrt)
                elif k == 13:
                    take_heads(0)
                if 1 <= k <= ITEMS:
                    take_turned(k - 1)
                if k >= 2:
                    take_values(k - 2)
                    square(k - 2)
            root_heads(1)
            take_heads(2)
            layer_norm(2, "yb")
            experts(1)
            layer_norm(3, "y1")

        @block.vector
        def _(dve):
            def step(ins):
                in_step(dve, ins, dve_step)

            def xT_half(r):
                for i in (1, 3):
                    wait_full(dve, f"xT{r}", i)
                    if r == 0:
                        emptied(dve.tensor_copy(xT[:, 2 * i:2 * i + 2, :], ps(f"xT{r}", i).rearrange("p (a b) -> p a b", a=2)),
                                f"xT{r}", i)
                        continue
                    for kc in (2 * i, 2 * i + 1):
                        last = dve.tensor_scalar(xT[:, kc, :], ps(f"xT{r}", i)[:, (kc % 2) * T:(kc % 2 + 1) * T],
                                                 lnc[:, 0, r - 1, kc:kc + 1], lnc[:, 1, r - 1, kc:kc + 1], ALU.mult, ALU.add)
                    emptied(last, f"xT{r}", i)

            def bc(v, n):
                return v.unsqueeze(2).to_broadcast([P, v.shape[1], n])

            def quad(name, i):
                return ps(name, i).rearrange("p (a b) -> p a b", a=4)

            xT_half(0)
            wait_full(dve, "cw")
            emptied(dve.tensor_copy(cw, ps("cw")[:, 0:96]), "cw")

            def convolve(t):
                name = ("qk", "qk2", "vch")[t // 8]
                src, dst = ps(name, t % 8), conv[:, t % 4, :]
                wait_full(dve, name, t % 8)
                if t >= 4:
                    dve.wait_ge(Sm["silu_done"], t - 3)
                step(dve.tensor_scalar(dst, src[:, 0:T], cw[:, 3 * 24 + t:3 * 24 + t + 1], None, ALU.mult))
                for s in (1, 2, 3):
                    tap = (3 - s) * 24 + t
                    ins = dve.scalar_tensor_tensor(dst[:, s:T], src[:, 0:T - s], cw[:, tap:tap + 1], dst[:, s:T],
                                                   ALU.mult, ALU.add)
                    if s < 3:
                        step(ins)
                    else:
                        emptied(ins, name, t % 8)

            wait_emptied(dve, "cw")
            for t in range(4):
                convolve(t)
            wait_full(dve, "ab")
            dve.wait_ge(ld_gates, 32)
            emptied(dve.tensor_copy(ab, ps("ab")[:, 0:32].rearrange("p (a b) -> p a b", a=2)), "ab")
            wait_emptied(dve, "ab")
            dtb2 = dtb.unsqueeze(1).to_broadcast([P, TT, HA])
            step(dve.tensor_tensor(gt1, ab[:, :, 0:HA], dtb2, ALU.add))
            dve.scalar_tensor_tensor(gt2, gt1, -1.0, gt1, ALU.mult, ALU.max).then_inc(Sm["gate_abs"], 1)
            dve.wait_ge(Sm["softplus_done"], 1)
            step(dve.scalar_tensor_tensor(gt1, gt1, 0.0, gt2, ALU.max, ALU.add))
            alog2 = alog.unsqueeze(1).to_broadcast([P, TT, HA])
            dve.scalar_tensor_tensor(g, gt1, -1.0, alog2, ALU.mult, ALU.mult).then_inc(Sm["gates_ready"], 1)
            step(dve.tensor_scalar(beta, beta, 1.0, None, ALU.add))
            step(dve.reciprocal(beta, beta))
            for t in range(4, 10):
                convolve(t)
            wait_full(dve, "cum")
            gcf = gc[:, :, :].rearrange("p a b -> p (a b)")
            step(dve.tensor_copy(gcf, ps("cum")[:, 0:16]))
            step(dve.tensor_tensor(kd[:, :, :].rearrange("p a b -> p (a b)"), ps("cum")[:, 16:32], gcf, ALU.subtract))
            dve.sem_inc(free[where["cum", 0][0]], 1)
            dve.sem_inc(Sm["decay_in"], 1)
            for i in range(4):
                wait_full(dve, "grow", i)
                for j in range(4):
                    m = 4 * i + j
                    last = dve.tensor_scalar(Dm[:, m, :], ps("grow", i)[:, j * P:(j + 1) * P], gcf[:, m:m + 1], 0.0,
                                             ALU.subtract, ALU.max)
                emptied(last, "grow", i)
            for t in range(10, 18):
                convolve(t)
            wait_full(dve, "ssq")
            step(dve.tensor_scalar(r2, ps("ssq")[:, 0:32].rearrange("p (a b) -> p a b", a=TT), RMS_EPS, None, ALU.add))
            dve.reciprocal(r2, r2).then_inc(Sm["norm_in"], 1)
            dve.sem_inc(free[where["ssq", 0][0]], 1)
            dve.wait_ge(Sm["norm_in"], 1)
            step(dve.scalar_tensor_tensor(nb, r2[:, :, HA:2 * HA], -1.0, beta, ALU.mult, ALU.mult))
            dve.wait_ge(Sm["decay_ready"], 1)
            dve.tensor_tensor(nbe, nb, eg, ALU.mult).then_inc(Sm["scales_ready"], 1)
            wait_full(dve, "lnc")
            emptied(dve.tensor_copy(lnc, ps("lnc")[:, 0:64].rearrange("p (a b c) -> p a b c", a=2, b=4)), "lnc")
            for t in range(18, 21):
                convolve(t)
            dve.wait_ge(Sm["norm_root"], 1)
            step(dve.tensor_tensor(bk, bk, beta, ALU.mult))
            for b in range(4):
                wait_full(dve, "kk", b)
                dve.wait_ge(Sm["nb_ready"], b + 1)
                m4 = Nm[:, 4 * b:4 * b + 4, :]
                emptied(dve.tensor_tensor(m4, quad("kk", b), m4, ALU.mult), "kk", b)
                if b >= 1:
                    convolve(20 + b)
            for i in range(4):
                tt, hg = i // 2, i % 2
                wait_full(dve, "vtr", i)
                emptied(dve.tensor_tensor(vN[:, tt, 512 * hg:512 * hg + 512].rearrange("p (a b) -> p a b", a=4),
                                          quad("vtr", i), bc(bk[:, tt, 4 * hg:4 * hg + 4], P), ALU.mult), "vtr", i)
            for b in range(4):
                wait_full(dve, "kq", b)
                wait_emptied(dve, "dtr", b)
                m4 = QK[:, 4 * b:4 * b + 4, :]
                emptied(dve.tensor_tensor(m4, quad("kq", b), m4, ALU.mult), "kq", b)
            for i in range(2):
                wait_full(dve, "ktr", i)
                emptied(dve.tensor_tensor(kN[:, 4 * i:4 * i + 4, :], quad("ktr", i), bc(kd[:, 0, 4 * i:4 * i + 4], P),
                                          ALU.mult), "ktr", i)
            for lev in range(1, 7):
                for b in range(4):
                    wait_full(dve, f"tt{lev}", b)
                    if lev < 6:
                        wait_full(dve, f"t{lev}", b)
                        m4 = Ti[:, 4 * b:4 * b + 4, :]
                        emptied(dve.tensor_tensor(m4, quad(f"t{lev}", b), m4, ALU.add), f"t{lev}", b)
                    m4 = TiT[:, 4 * b:4 * b + 4, :]
                    emptied(dve.tensor_tensor(m4, quad(f"tt{lev}", b), m4, ALU.add), f"tt{lev}", b)
            for i in range(2):
                wait_full(dve, "s1", i)
                emptied(dve.tensor_copy(S[:, 4 * i:4 * i + 4, :], quad("s1", i)), "s1", i)
            for i in range(2):
                wait_full(dve, "ks", i)
                tmp = PT[:, 4 * i:4 * i + 4, :]
                emptied(dve.tensor_tensor(tmp, quad("ks", i), bc(nbe[:, 1, 4 * i:4 * i + 4], P), ALU.mult), "ks", i)
                wait_emptied(dve, "ks", i)
                v1 = vN[:, 1, 512 * i:512 * i + 512].rearrange("p (a b) -> p a b", a=4)
                dve.tensor_tensor(v1, v1, tmp, ALU.add).then_inc(Sm["r1_ready"], 1)
                wait_full(dve, "qs", i)
                emptied(dve.tensor_tensor(qS[:, 4 * i:4 * i + 4, :], quad("qs", i), bc(eg[:, 1, 4 * i:4 * i + 4], P),
                                          ALU.mult), "qs", i)

            def heads_mean(tt, hg):
                dve.wait_ge(Sm["o_squared"], 2 * tt + hg + 1)
                m4 = ms[:, tt, 4 * hg:4 * hg + 4]
                step(dve.tensor_reduce(m4, xT[:, 4 + 2 * hg:6 + 2 * hg, :].rearrange("p a (b c) -> p (a b) c", b=2),
                                       AX_X, ALU.add))
                dve.scalar_tensor_tensor(m4, m4, 1.0 / P / P, r2[:, tt, 4 * hg:4 * hg + 4], ALU.mult, ALU.mult)\
                    .then_inc(Sm["o_mean"], 1)

            def heads_scale(tt, hg):
                dve.wait_ge(Sm["o_root"], 2 * tt + hg + 1)
                m4 = ms[:, tt, 4 * hg:4 * hg + 4]
                step(dve.reciprocal(m4, m4))
                ins = dve.tensor_tensor(m4, m4, fq[:, tt, 4 * hg:4 * hg + 4], ALU.mult)
                if tt == 0:
                    ins.then_inc(Sm["first_scale"], 1)
                    return
                step(ins)
                o3 = oN[:, tt, 512 * hg:512 * hg + 512].rearrange("p (a b) -> p a b", a=4)
                step(dve.tensor_tensor(o3, o3, bc(m4, P), ALU.mult))
                dve.tensor_tensor(o3, o3, z[:, tt, 512 * hg:512 * hg + 512].rearrange("p (a b) -> p a b", a=4), ALU.mult)\
                    .then_inc(Sm["o_normed"], 1)

            for hg in range(2):
                heads_mean(0, hg)
            for hg in range(2):
                heads_scale(0, hg)
            for i in range(2):
                wait_full(dve, "o1", i)
                wait_emptied(dve, "qs", i)
                emptied(dve.tensor_tensor(oN[:, 1, 512 * i:512 * i + 512].rearrange("p (a b) -> p a b", a=4),
                                          quad("o1", i), qS[:, 4 * i:4 * i + 4, :], ALU.add), "o1", i)
            dve.wait_ge(Sm["z_ready"], 1)
            for hg in range(2):
                heads_mean(1, hg)
            for hg in range(2):
                heads_scale(1, hg)
            for i in (1, 3):
                wait_full(dve, "oTa", i)
                emptied(dve.tensor_copy(oT[:, 2 * i:2 * i + 2, :], ps("oTa", i).rearrange("p (a b) -> p a b", a=2)), "oTa", i)

            def weigh(y, tt, n):
                wait_emptied(dve, y, 2 * tt + n)
                x2 = xN[:, tt, 512 * n:512 * n + 512]
                dve.tensor_tensor(x2, x2, lnp[:, 0, 512 * n:512 * n + 512], ALU.mult).then_inc(Sm["ln_scaled"], 1)

            def layer_norm(r, y, lnp):
                def stats(tt, n):
                    wait_full(dve, y, 2 * tt + n)
                    ins = dve.bn_stats(st6[:, tt, n, :], ps(y, 2 * tt + n)[:, :])
                    if n:
                        step(ins)
                        dve.bn_aggr(mv[:, tt, :], st6[:, tt, :, :].rearrange("p a b -> p (a b)")).then_inc(Sm["ln_var"], 1)

                def scales(tt):
                    dve.wait_ge(Sm["ln_root"], 2 * r + tt + 1)
                    step(dve.reciprocal(rstd[:, tt:tt + 1], rstd[:, tt:tt + 1]))
                    dve.scalar_tensor_tensor(nmr[:, tt:tt + 1], mv[:, tt, 0:1], -1.0, rstd[:, tt:tt + 1], ALU.mult, ALU.mult)\
                        .then_inc(Sm["ln_scale"], 1)

                def normalise(tt):
                    src, dst = ps(y, 2 * tt + 1)[:, :], xN[:, tt, 512:1024]
                    if r < 3:
                        dve.wait_ge(Sm["ln_scale"], 2 * r + tt + 1)
                        emptied(dve.tensor_scalar(dst, src, rstd[:, tt:tt + 1], nmr[:, tt:tt + 1], ALU.mult, ALU.add),
                                y, 2 * tt + 1)
                    else:
                        emptied(dve.scalar_tensor_tensor(dst, src, mv[:, tt, 0:1], lnp[:, 0, 512:1024],
                                                         ALU.subtract, ALU.mult), y, 2 * tt + 1)
                        wait_emptied(dve, y, 2 * tt + 1)
                        dve.scalar_tensor_tensor(dst, dst, rstd[:, tt:tt + 1], lnp[:, 1, 512:1024], ALU.mult, ALU.add)\
                            .then_inc(Sm["out_ready"], 1)

                stats(0, 0)
                stats(0, 1)
                stats(1, 0)
                scales(0)
                stats(1, 1)
                if r == 3:
                    dve.wait_ge(ld_lnp, 32 * (r + 1))
                    normalise(0)
                    scales(1)
                    weigh(y, 0, 0)
                    normalise(1)
                    weigh(y, 1, 0)
                    return
                normalise(0)
                scales(1)
                normalise(1)
                xT_half(r + 1)
                for i in range(4):
                    wait_full(dve, f"xT{r + 1}", i)
                dve.wait_ge(ld_lnp, 32 * (r + 1))
                for tt in range(TT if r == 1 else 1):
                    for n in range(2):
                        weigh(y, tt, n)

            def route(layer):
                lg, p, a, b_, c, d = (rt[:, 32 * k:32 * k + 32] for k in range(1, 7))
                sel = rt[:, 0:32]

                def t2(v):
                    return v.rearrange("p (a b) -> p a b", a=TT)

                def t8(v):
                    return v.rearrange("p (a b) -> p a b", a=TT * GRP)

                mx, sm = rt[:, 224:226], rt[:, 226:228]
                gs, gt, gr = (rt[:, 232 + 8 * k:240 + 8 * k] for k in range(3))
                above, tie = rtw[:, 0:128], rtw[:, 128:256]
                w2 = w4.unsqueeze(1).to_broadcast([P, TT, GRP])

                def pairs(v):
                    return v.rearrange("p (g a b) -> p g a b", g=TT * GRP, a=GRP)

                name = f"lg{layer}"
                dve.wait_ge(ld_par, 16 * 3)
                wait_full(dve, name)
                for tt in range(TT):
                    last = dve.tensor_tensor_reduce(lg[:, tt * NE:(tt + 1) * NE], ps(name)[:, tt * NE:(tt + 1) * NE], rb, -1.0,
                                                    3e38, ALU.add, ALU.min, mx[:, tt:tt + 1])
                emptied(last, name)
                weigh("yb" if layer else "ya", 1, 0)
                dve.wait_ge(Sm["exp_done"], layer + 1)
                this = t8(p).unsqueeze(3).to_broadcast([P, TT * GRP, GRP, GRP])
                other = t8(p).unsqueeze(2).to_broadcast([P, TT * GRP, GRP, GRP])
                dve.tensor_tensor(pairs(above), other, this, ALU.is_gt)
                step(dve.tensor_tensor(pairs(tie), other, this, ALU.is_equal))
                step(dve.tensor_tensor(pairs(tie), pairs(tie), before.unsqueeze(1).to_broadcast([P, TT * GRP, GRP, GRP]),
                                       ALU.mult))
                step(dve.tensor_tensor(above, above, tie, ALU.add))
                step(dve.tensor_reduce(a, above.rearrange("p (a b) -> p a b", b=GRP), AX_X, ALU.add))
                step(dve.tensor_scalar(b_, a, 1.5, None, ALU.is_lt))
                step(dve.tensor_tensor(c, b_, p, ALU.mult))
                step(dve.tensor_reduce(gs, t8(c), AX_X, ALU.add))
                step(dve.tensor_reduce(mx, t2(gs), AX_X, ALU.max))
                step(dve.tensor_tensor(t2(gt), t2(gs), bc(mx, GRP), ALU.is_equal))
                step(dve.tensor_tensor(t2(gt), t2(gt), w2, ALU.mult))
                step(dve.tensor_reduce(sm, t2(gt), AX_X, ALU.max))
                step(dve.tensor_tensor(t2(gr), t2(gt), bc(sm, GRP), ALU.is_equal))
                dve.tensor_tensor(t8(sel), t8(b_), bc(gr, GRP), ALU.mult).then_inc(Sm["sel_ready"], 1)
                weigh("yb" if layer else "ya", 1, 1)
                dve.wait_ge(Sm["sel_ready"], layer + 1)
                step(dve.tensor_tensor(p, p, sel, ALU.mult))
                step(dve.tensor_reduce(sm, t2(p), AX_X, ALU.add))
                step(dve.reciprocal(sm, sm))
                step(dve.tensor_tensor(gate[:, :, 0:NE], t2(p), bc(sm, NE), ALU.mult))
                name = f"rk{layer}"
                wait_full(dve, name)
                step(dve.scalar_tensor_tensor(RK[:, :, 0:NE], ps(name)[:, 0:32].rearrange("p (a b) -> p a b", a=TT), 1.0,
                                              t2(sel), ALU.add, ALU.mult))

            def route_passes(layer):
                c, mx = rt[:, 160:176], rt[:, 224:226]
                name = f"rk{layer}"
                emptied(dve.tensor_tensor(c, ps(name)[:, NE:2 * NE], rt[:, NE:2 * NE], ALU.add), name)
                wait_emptied(dve, name)
                step(dve.tensor_reduce(mx[:, 0:1], c, AX_X, ALU.max))
                dve.tensor_copy(flag[:, :], mx[:, 0:1]).then_inc(Sm["flag_ready"], 1)
                dve.memset(RK[:, :, NE * PASSES:NE * PASSES + 2], -1.0)
                for k in range(1, PASSES):
                    last = dve.tensor_scalar(RK[:, :, NE * k:NE * k + NE], RK[:, :, 0:NE], float(CAP * k), None, ALU.subtract)
                step(last)

            def place(out_, tt, col):
                return dve.tensor_scalar(out_, iota, RK[:, tt, col], None, ALU.is_equal)

            def place_gated(out_, tt, col, e):
                return dve.tensor_scalar(out_, iota, RK[:, tt, col], gate[:, tt, e], ALU.is_equal, ALU.mult)

            def experts(layer):
                s = moe_sems[layer]
                route(layer)

                def build_gather(pair):
                    for q in range(2):
                        for tt in range(TT):
                            last = place(Pb[:, tt, q * CAP:(q + 1) * CAP], tt, bass.ds(2 * pair + q, 1))
                    last.then_inc(s["P_built"], 1)

                def hidden(e, par):
                    dve.wait_ge(s["sg_ready"], e + 1)
                    dve.tensor_tensor(hN[:, par, :], GU[par][:, 256:512], sg[:, par, :], ALU.mult).then_inc(s["h_ready"], 1)

                def turned(e, par):
                    dve.wait_ge(s["ht_done"], e + 1)
                    w = 512 if par else 256
                    dve.tensor_copy(hTG[:, par, 0:w], GU[par][:, 0:w]).then_inc(s["ht_ready"], 1)

                def result(e, par):
                    dve.wait_ge(s["down_done"], e + 1)
                    dve.tensor_copy(ys[CAP * par:CAP * par + CAP, 512:1024], YD[CAP:P, :]).then_inc(s["ys_ready"], 1)

                def two_experts(pair, last=False):
                    a = 2 * pair
                    turned(a, 0)
                    hidden(a + 1, 1)
                    for q in range(2):
                        for tt in range(TT):
                            built = place_gated(G2[:, tt, q * CAP:(q + 1) * CAP], tt, bass.ds(a + q, 1), bass.ds(a + q, 1))
                    built.then_inc(s["G_built"], 1)
                    result(a, 0)
                    turned(a + 1, 1)
                    if not last:
                        dve.wait_ge(s["gathered"], a + 4)
                        build_gather(pair + 2)
                        hidden(a + 2, 0)
                    result(a + 1, 1)

                dve.tensor_tensor(Pb[:, :, :].rearrange("p t (q j) -> p t q j", q=2),
                                  iota.unsqueeze(1).unsqueeze(1).to_broadcast([P, TT, 2, CAP]),
                                  RK[:, :, 0:2].unsqueeze(3).to_broadcast([P, TT, 2, CAP]), ALU.is_equal)\
                    .then_inc(s["P_built"], 1)
                dve.wait_ge(s["gathered"], 2)
                dve.tensor_copy(xeT[:, 4:8, :], YD[:, :].rearrange("p (a b) -> p a b", a=4)).then_inc(s["xe_ready"], 1)
                route_passes(layer)
                build_gather(1)
                hidden(0, 0)
                with dve.Fori(0, NE // 2 - 1) as pair:
                    two_experts(pair)
                two_experts(NE // 2 - 1, last=True)

                more = dve.value_load(flag[P - 1:P, 0:1], min_val=0, max_val=T)
                with dve.If(more > CAP):
                    with dve.Fori(1, PASSES) as ps_:
                        with dve.Fori(0, NE) as ei:
                            it = (ps_ - 1) * NE + ei
                            dve.wait_ge(s["o_done"], it + 1)
                            for tt in range(TT):
                                place(Pb[:, tt, 0:CAP], tt, bass.ds(ps_ * NE + ei, 1))
                                last = place_gated(G2[:, tt, 0:CAP], tt, bass.ds(ps_ * NE + ei, 1), bass.ds(ei, 1))
                            last.then_inc(s["o_P"], 1)
                            dve.wait_ge(s["o_sg"], it + 1)
                            dve.tensor_tensor(hN[:, 0, :], GU[0][:, 256:512], sg[:, 0, :], ALU.mult).then_inc(s["o_h"], 1)
                            dve.wait_ge(s["o_ht"], it + 1)
                            dve.tensor_copy(hTG[:, 0, :], GU[0][:, :]).then_inc(s["o_htr"], 1)
                            dve.wait_ge(s["o_down"], it + 1)
                            dve.tensor_copy(ys[0:CAP, 512:1024], YD[CAP:P, :]).then_inc(s["o_ys"], 1)

            layer_norm(0, "ya", lnp)
            experts(0)
            layer_norm(1, "y0", lnp)

            dve.wait_ge(ld_att, 16 * 4)
            step(dve.tensor_tensor(lp, lam[:, 0:4:2, :], lam[:, 1:4:2, :], ALU.mult))
            dve.tensor_reduce(lam2, lp, AX_X, ALU.add).then_inc(Sm["lam_sum"], 1)
            wait_full(dve, "brow")
            dve.memset(brow[0:HB, T:REV], MASKED)
            step(dve.tensor_copy(brow[0:HB, 0:T], ps("brow")[0:HB, 0:T]))
            dve.sem_inc(free[where["brow", 0][0]], 1)
            dve.sem_inc(Sm["brow_ready"], 1)
            dve.wait_ge(Sm["lam_exp"], 1)
            step(dve.scalar_tensor_tensor(lamv, lam2[:, 1:2], LAMBDA_INIT, lam2[:, 0:1], ALU.subtract, ALU.subtract))

            def take_k(name, i, h):
                wait_full(dve, name, i)
                emptied(dve.tensor_copy(kT[:, h, :], ps(name, i)[:, 0:T]), name, i)

            for h in range(4):
                take_k("k", h, h)
            for i in range(4):
                wait_full(dve, "bias", i)
                emptied(dve.tensor_copy(bias[:, 2 * i:2 * i + 2, :], ps("bias", i).rearrange("p (a b) -> p a b", a=2)), "bias", i)
            wait_emptied(dve, "bias", 3)

            def add_bias(i):
                h, qt = i // 2, i % 2
                b, w = i % 2, (qt + 1) * P
                wait_full(dve, "sc", i)
                for half in range(2):
                    last = dve.tensor_tensor_reduce(sc[:, b, half * T:half * T + w], ps("sc", i)[:, half * T:half * T + w],
                                                    bias[:, h, T - w:T], -1.0, 3e38, ALU.add, ALU.min,
                                                    smx[:, b, half:half + 1])
                    if half:
                        emptied(last, "sc", i)
                wait_emptied(dve, "sc", i)
                dve.sem_inc(Sm["sc_ready"], 1)

            def difference(i):
                b, w = i % 2, (i % 2 + 1) * P
                dve.wait_ge(Sm["p_ready"], i + 1)
                step(dve.reciprocal(srec[:, b, :], ssum[:, b, :]))
                step(dve.tensor_tensor(srec[:, b, 1:2], srec[:, b, 1:2], lamv, ALU.mult))
                if i >= 2:
                    wait_full(dve, "atT", i - 2)
                step(dve.tensor_scalar(at[:, b, 0:w], pa[:, b, 0:w], srec[:, b, 0:1], None, ALU.mult))
                dve.scalar_tensor_tensor(at[:, b, 0:w], pa[:, b, T:T + w], srec[:, b, 1:2], at[:, b, 0:w], ALU.mult, ALU.add)\
                    .then_inc(Sm["at_ready"], 1)

            def heads_factor():
                dve.wait_ge(Sm["o_root"], 5)
                dve.reciprocal(msB[:, 0, :], msB[:, 0, :]).then_inc(Sm["o_scale"], 1)

            def take_heads(i):
                wait_full(dve, "oTb", i)
                dve.wait_ge(Sm["nwB_ready"], 1)
                emptied(dve.tensor_scalar(kT[:, 2 * i:2 * i + 2, :], ps("oTb", i).rearrange("p (a b) -> p a b", a=2), nwB, None,
                                          ALU.mult), "oTb", i)

            for k in range(ITEMS + 1):
                if k < ITEMS:
                    add_bias(k)
                if k >= 1:
                    difference(k - 1)
                if k < 8 and k % 2 == 1:
                    take_k("k2", k // 2, 4 + k // 2)
                elif k == 10:
                    heads_factor()
                elif k == 13:
                    take_heads(1)
            dve.wait_ge(Sm["o_root"], 6)
            step(dve.reciprocal(msB[:, 1, :], msB[:, 1, :]))
            for tt in range(TT):
                o3 = oN[:, tt, 512:1024].rearrange("p (h c) -> p h c", h=4)
                last = dve.tensor_tensor(o3, o3, bc(msB[:, 1, 4 * tt:4 * tt + 4], P), ALU.mult)
            last.then_inc(Sm["o_normed"], 1)
            take_heads(3)
            layer_norm(2, "yb", lnp)
            experts(1)
            layer_norm(3, "y1", lnp)

        @block.gpsimd
        def _(pool):
            def step(ins):
                in_step(pool, ins, pool_step)

            def four_of(v):
                return v.unsqueeze(1).to_broadcast([P, 4, P])

            def load_lnp(dst, l, k):
                pool.dma_start(dst[:, 0, :], ln_w[l, k:k + 1, :].to_broadcast([P, D])).then_inc(ld_lnp, 16)
                pool.dma_start(dst[:, 1, :], ln_b[l, k:k + 1, :].to_broadcast([P, D])).then_inc(ld_lnp, 16)

            def layer_norm(r, lnp):
                halves = [(tt, n) for tt in range(TT) for n in range(2) if r < 3 or n == 0]
                for i, (tt, n) in enumerate(halves):
                    pool.wait_ge(Sm["ln_scaled"], 4 * r + i + 1)
                    x2 = xN[:, tt, 512 * n:512 * n + 512]
                    pool.tensor_tensor(x2, x2, lnp[:, 1, 512 * n:512 * n + 512], ALU.add).then_inc(Sm["x_ready"], 1)

            pool.wait_ge(ld_cst, 16)
            for i in range(4):
                pool.wait_ge(Sm["dm_exp"], i + 1)
                d = Dm[:, 4 * i:4 * i + 4, :]
                pool.tensor_tensor(d, d, four_of(low), ALU.mult).then_inc(Sm["dm_ready"], 1)
            pool.wait_ge(Sm["dm_ready"], 4)
            pool.wait_ge(Sm["scales_ready"], 1)
            for b in range(4):
                m4 = Nm[:, 4 * b:4 * b + 4, :]
                nb4 = nb[:, b // 2, 4 * (b % 2):4 * (b % 2) + 4].unsqueeze(2).to_broadcast([P, 4, P])
                pool.tensor_tensor(m4, Dm[:, 4 * b:4 * b + 4, :], nb4, ALU.mult).then_inc(Sm["nb_ready"], 1)
            for b in range(4):
                wait_emptied(pool, "kk", b)
                t4 = Ti[:, 4 * b:4 * b + 4, :]
                step(pool.tensor_tensor(t4, Nm[:, 4 * b:4 * b + 4, :], four_of(mask(C_LEV)), ALU.mult))
                pool.tensor_tensor(t4, t4, four_of(ident), ALU.add).then_inc(Sm["T_init"], 1)
            for lev in range(1, 7):
                for b in range(4):
                    wait_full(pool, f"p{lev - 1}" if lev > 1 else "dtr", b)
                    pool.tensor_tensor(Dm[:, 4 * b:4 * b + 4, :], Nm[:, 4 * b:4 * b + 4, :], four_of(mask(C_LEV + lev)),
                                       ALU.mult).then_inc(Sm["L_ready"], 1)
            pool.wait_ge(Sm["L_ready"], 24)
            pool.wait_ge(ld_par, 16 * 3)
            for i in range(4):
                wait_emptied(pool, "zz", i)
            for tt in range(TT):
                z3 = z[:, tt, :].rearrange("p (a b) -> p a b", a=8)
                last = pool.tensor_tensor(z3, z3, nw.unsqueeze(1).to_broadcast([P, 8, P]), ALU.mult)
            last.then_inc(Sm["z_ready"], 1)
            pool.wait_ge(Sm["z_ready"], 1)
            for hg in range(2):
                pool.wait_ge(Sm["first_scale"], hg + 1)
                o3 = oN[:, 0, 512 * hg:512 * hg + 512].rearrange("p (a b) -> p a b", a=4)
                m4 = ms[:, 0, 4 * hg:4 * hg + 4].unsqueeze(2).to_broadcast([P, 4, P])
                step(pool.tensor_tensor(o3, o3, m4, ALU.mult))
                pool.tensor_tensor(o3, o3, z[:, 0, 512 * hg:512 * hg + 512].rearrange("p (a b) -> p a b", a=4), ALU.mult)\
                    .then_inc(Sm["first_normed"], 1)
            for i in range(2):
                wait_full(pool, "o1", i)
            load_lnp(lnp, 0, 0)
            layer_norm(0, lnp)
            pool.wait_ge(Sm["x_ready"], 4)
            load_lnp(lnp, 0, 1)
            layer_norm(1, lnp)

            pool.wait_ge(Sm["x_ready"], 8)
            pool.memset(view(4096, HB * 2 * T), 0.0).then_inc(Sm["qz_zero"], 1)
            pool.wait_ge(ld_att, 16 * 4)
            pool.tensor_scalar(nwB, nwB, 1.0 - LAMBDA_INIT, None, ALU.mult).then_inc(Sm["nwB_ready"], 1)
            pool.wait_ge(Sm["brow_ready"], 1)
            pool.dma_start(bias_rows, brow[0:HB, :]).then_inc(st_bias, 16)
            pool.wait_ge(st_bias, 16)
            pool.dma_start(braw[:, :, :], bass.AP(bias_rows.tensor, 0, [[1, P], [REV, HB], [1, T]])).then_inc(ld_bias, 16)

            pool.wait_ge(Sm["o_scale"], 1)
            o4 = oN[:, :, 0:512].rearrange("p t (h c) -> p t h c", h=4)
            pool.tensor_tensor(o4, o4, msB[:, 0, :].rearrange("p (t h) -> p t h", t=TT).unsqueeze(3)
                               .to_broadcast([P, TT, 4, P]), ALU.mult).then_inc(Sm["o_normed"], 1)
            wait_full(pool, "sc", 15)
            load_lnp(lnp, 1, 0)
            layer_norm(2, lnp)
            pool.wait_ge(Sm["x_ready"], 12)
            load_lnp(lnp, 1, 1)
            layer_norm(3, lnp)


_INS = ["x", "a_w_in", "a_conv", "a_A_log", "a_dt_bias", "a_norm_w", "a_w_out", "b_w_q", "b_w_kv", "b_lambda",
        "b_subln_w", "b_w_out", "rel_bias", "router_w", "router_b", "moe_w_gate", "moe_w_up", "moe_w_down", "ln_w", "ln_b"]


def kernel(**inputs):
    import concourse.bacc as bacc
    from concourse.bass_utils import run_bass_kernel_spmd

    nc = bacc.Bacc("TRN2", target_bir_lowering=False, num_devices=1)
    arrays, args = {}, []
    for name in _INS:
        arrays[f"in_{name}"] = np.ascontiguousarray(inputs[name])
    arrays["in_consts"] = constants()
    arrays["in_buckets"] = bucket_rows()
    for name, a in arrays.items():
        args.append(nc.dram_tensor(name, a.shape, mybir.dt.from_np(a.dtype), kind="ExternalInput").ap())
    args.append(nc.dram_tensor("bias_rows", [HB, REV], F32, kind="Internal").ap())
    args.append(nc.dram_tensor("out_0", (1, T, D), F32, kind="ExternalOutput").ap())
    build(nc, *args)
    r = run_bass_kernel_spmd(nc, [arrays], core_ids=[0])
    return r.results[0]["out_0"]
```
